# Optimizing a Trainium2 kernel written in Bass

```python
import jax, jax.numpy as jnp
from jax import lax
import numpy as np

D_MODEL = 1024
BATCH = 1
SEQ = 1024
DEPTH = 1

EPS = 1e-6
SSD_EXPAND = 2
SSD_D_INNER = SSD_EXPAND * D_MODEL
SSD_HEAD_DIM = 64
SSD_N_HEADS = SSD_D_INNER // SSD_HEAD_DIM
SSD_N_GROUPS = 4
SSD_D_STATE = 128
SSD_GN = SSD_N_GROUPS * SSD_D_STATE
SSD_CONV_DIM = SSD_D_INNER + 2 * SSD_GN
SSD_CONV_WIDTH = 5
SSD_CHUNK = 128
DT_MIN = 0.001
DT_MAX = 0.1
ATTN_N_HEADS = 16
ATTN_N_KV_HEADS = 4
ATTN_HEAD_DIM = 64
ATTN_Q_DIM = ATTN_N_HEADS * ATTN_HEAD_DIM
ATTN_KV_DIM = ATTN_N_KV_HEADS * ATTN_HEAD_DIM
ATTN_WINDOW = 128
ATTN_BLOCK = 128
D_FF = -(-8 * D_MODEL // (3 * 256)) * 256
IN_SIZES = (SSD_D_INNER, SSD_CONV_DIM, SSD_N_HEADS, SSD_N_HEADS,
            ATTN_Q_DIM, ATTN_KV_DIM, ATTN_KV_DIM, D_MODEL, D_MODEL)
IN_PROJ_DIM = sum(IN_SIZES)

kernel_name = 'hybrid_ssd_swa_gated_encoder'

def _split_cols(t, sizes):
    out, start = [], 0
    for s in sizes:
        out.append(t[..., start:start + s])
        start += s
    return out

def rmsnorm(x, w):
    xf = x.astype(jnp.float32)
    y = xf * lax.rsqrt(jnp.mean(xf * xf, axis=-1, keepdims=True) + EPS)
    return (y * w.astype(jnp.float32)).astype(x.dtype)

def depthwise_conv(x, w, b):
    K, C = w.shape
    y = lax.conv_general_dilated(x, w[:, None, :].astype(x.dtype), window_strides=(1,),
                                 padding=[(K // 2, K // 2)],
                                 dimension_numbers=('NWC', 'WIO', 'NWC'),
                                 feature_group_count=C)
    return y + b

def ssd_scan(xs, dt, A, Bm, Cm):
    Bsz, L, H, P = xs.shape
    G, N = Bm.shape[2], Bm.shape[3]
    R = H // G
    Q = SSD_CHUNK
    nc = L // Q
    xdt = (xs * dt[..., None]).reshape(Bsz, nc, Q, G, R, P)
    a = (dt.astype(jnp.float32) * A.astype(jnp.float32)).reshape(Bsz, nc, Q, G, R)
    Bc = Bm.reshape(Bsz, nc, Q, G, N)
    Cc = Cm.reshape(Bsz, nc, Q, G, N)
    a_cum = jnp.cumsum(a, axis=2)
    a_cum_t = jnp.moveaxis(a_cum, 2, -1)
    seg = a_cum_t[..., :, None] - a_cum_t[..., None, :]
    lower = jnp.tril(jnp.ones((Q, Q), dtype=bool))
    decay_in = jnp.exp(jnp.where(lower, seg, -jnp.inf))
    CB = jnp.einsum('bclgn,bcsgn->bcgls', Cc, Bc)
    y_diag = jnp.einsum('bcgls,bcgrls,bcsgrp->bclgrp', CB, decay_in, xdt)
    decay_to_end = jnp.exp(a_cum[:, :, -1:] - a_cum)
    states = jnp.einsum('bcsgn,bcsgr,bcsgrp->bcgrpn', Bc, decay_to_end, xdt)
    chunk_decay = jnp.exp(a_cum[:, :, -1])

    def step(h, inp):
        s_c, d_c = inp
        return h * d_c[..., None, None] + s_c, h

    h0 = jnp.zeros_like(states[:, 0])
    _, states_in = lax.scan(step, h0, (jnp.moveaxis(states, 1, 0), jnp.moveaxis(chunk_decay, 1, 0)))
    states_in = jnp.moveaxis(states_in, 0, 1)
    y_off = jnp.einsum('bclgn,bcgrpn,bclgr->bclgrp', Cc, states_in, jnp.exp(a_cum))
    return (y_diag + y_off).reshape(Bsz, L, H, P)

def bidirectional_ssd(xs, dt_f, dt_b, A_f, A_b, Bm, Cm):
    flip = lambda t: jnp.flip(t, axis=1)
    y_f = ssd_scan(xs, dt_f, A_f, Bm, Cm)
    y_b = flip(ssd_scan(flip(xs), flip(dt_b), A_b, flip(Bm), flip(Cm)))
    return y_f + y_b

def windowed_gqa(q, k, v, sink):
    Bsz, L, H, Dh = q.shape
    KV = k.shape[2]
    R = H // KV
    W = ATTN_BLOCK
    nb = L // W
    qb = q.reshape(Bsz, nb, W, KV, R, Dh)
    pad = ((0, 0), (W, W), (0, 0), (0, 0))
    kp = jnp.pad(k, pad).reshape(Bsz, nb + 2, W, KV, Dh)
    vp = jnp.pad(v, pad).reshape(Bsz, nb + 2, W, KV, Dh)
    kwin = jnp.concatenate([kp[:, :-2], kp[:, 1:-1], kp[:, 2:]], axis=2)
    vwin = jnp.concatenate([vp[:, :-2], vp[:, 1:-1], vp[:, 2:]], axis=2)
    scores = jnp.einsum('bnqkrd,bnskd->bnkrqs', qb, kwin).astype(jnp.float32) * (Dh ** -0.5)
    blk = jnp.arange(nb)[:, None] * W
    q_pos = blk + jnp.arange(W)[None, :]
    k_pos = blk - W + jnp.arange(3 * W)[None, :]
    dist = jnp.abs(q_pos[:, :, None] - k_pos[:, None, :])
    valid = (dist <= ATTN_WINDOW) & (k_pos[:, None, :] >= 0) & (k_pos[:, None, :] < L)
    slopes = jnp.exp2(-8.0 * jnp.arange(1, H + 1, dtype=jnp.float32) / H).reshape(KV, R)
    bias = -slopes[None, :, :, None, None] * dist[:, None, None].astype(jnp.float32)
    scores = jnp.where(valid[:, None, None][None], scores + bias[None], -jnp.inf)
    sink_l = sink.astype(jnp.float32).reshape(KV, R)[None, None, :, :, None]
    m = jnp.maximum(jnp.max(scores, axis=-1), sink_l)
    p = jnp.exp(scores - m[..., None])
    denom = jnp.sum(p, axis=-1) + jnp.exp(sink_l - m)
    out = jnp.einsum('bnkrqs,bnskd->bnqkrd', p, vwin.astype(jnp.float32))
    out = out / jnp.moveaxis(denom, -1, 2)[..., None]
    return out.reshape(Bsz, L, H * Dh).astype(q.dtype)

def setup_inputs(seed: int = 0) -> dict:
    key = jax.random.key(seed)
    ks = jax.random.split(key, 20)
    f32 = jnp.float32
    nrm = lambda k, shape, s: jax.random.normal(k, shape, f32) * s
    gain = lambda k, n: 1.0 + 0.05 * jax.random.normal(k, (DEPTH, n), f32)

    def dt_bias(k):
        u = jax.random.uniform(k, (DEPTH, SSD_N_HEADS), f32)
        dt = jnp.exp(u * (np.log(DT_MAX) - np.log(DT_MIN)) + np.log(DT_MIN))
        return dt + jnp.log(-jnp.expm1(-dt))

    def a_log(k):
        return jnp.log(jax.random.uniform(k, (DEPTH, SSD_N_HEADS), f32, 1.0, 16.0))

    return {
        'x': jax.random.normal(ks[0], (BATCH, SEQ, D_MODEL), f32),
        'pre_mix_norm': gain(ks[1], D_MODEL),
        'w_in': nrm(ks[2], (DEPTH, D_MODEL, IN_PROJ_DIM), D_MODEL ** -0.5),
        'conv_w': nrm(ks[3], (DEPTH, SSD_CONV_WIDTH, SSD_CONV_DIM), SSD_CONV_WIDTH ** -0.5),
        'conv_b': nrm(ks[4], (DEPTH, SSD_CONV_DIM), 0.02),
        'dt_bias_f': dt_bias(ks[5]),
        'dt_bias_b': dt_bias(ks[6]),
        'A_log_f': a_log(ks[7]),
        'A_log_b': a_log(ks[8]),
        'D_skip': 1.0 + 0.1 * jax.random.normal(ks[9], (DEPTH, SSD_N_HEADS), f32),
        'ssd_norm': gain(ks[10], SSD_D_INNER),
        'w_ssd_proj': nrm(ks[11], (DEPTH, SSD_D_INNER, D_MODEL), SSD_D_INNER ** -0.5),
        'attn_sink': nrm(ks[12], (DEPTH, ATTN_N_HEADS), 0.5),
        'w_attn_proj': nrm(ks[13], (DEPTH, ATTN_Q_DIM, D_MODEL), ATTN_Q_DIM ** -0.5),
        'w_out': nrm(ks[14], (DEPTH, D_MODEL, D_MODEL), D_MODEL ** -0.5),
        'post_mix_norm': gain(ks[15], D_MODEL),
        'pre_ffn_norm': gain(ks[16], D_MODEL),
        'w_ffn_in': nrm(ks[17], (DEPTH, D_MODEL, 2 * D_FF), D_MODEL ** -0.5),
        'w_ffn_out': nrm(ks[18], (DEPTH, D_FF, D_MODEL), D_FF ** -0.5),
        'post_ffn_norm': gain(ks[19], D_MODEL),
    }

def reference(x, pre_mix_norm, w_in, conv_w, conv_b, dt_bias_f, dt_bias_b, A_log_f, A_log_b,
              D_skip, ssd_norm, w_ssd_proj, attn_sink, w_attn_proj, w_out, post_mix_norm,
              pre_ffn_norm, w_ffn_in, w_ffn_out, post_ffn_norm):
    Bsz, L, _ = x.shape
    for i in range(DEPTH):
        h = rmsnorm(x, pre_mix_norm[i])
        proj = h @ w_in[i]
        z, xBC, dtf_raw, dtb_raw, q, k, v, gate_a, gate_b = _split_cols(proj, IN_SIZES)
        xBC = jax.nn.silu(depthwise_conv(xBC, conv_w[i], conv_b[i]))
        xs, Bm, Cm = _split_cols(xBC, (SSD_D_INNER, SSD_GN, SSD_GN))
        xs = xs.reshape(Bsz, L, SSD_N_HEADS, SSD_HEAD_DIM)
        Bm = Bm.reshape(Bsz, L, SSD_N_GROUPS, SSD_D_STATE)
        Cm = Cm.reshape(Bsz, L, SSD_N_GROUPS, SSD_D_STATE)
        dt_f = jax.nn.softplus(dtf_raw + dt_bias_f[i])
        dt_b = jax.nn.softplus(dtb_raw + dt_bias_b[i])
        A_f = -jnp.exp(A_log_f[i])
        A_b = -jnp.exp(A_log_b[i])
        y = bidirectional_ssd(xs, dt_f, dt_b, A_f, A_b, Bm, Cm) + D_skip[i][:, None] * xs
        y = y.reshape(Bsz, L, SSD_D_INNER).astype(x.dtype)
        y = rmsnorm(y * jax.nn.silu(z), ssd_norm[i])
        y_ssd = y @ w_ssd_proj[i]
        q = q.reshape(Bsz, L, ATTN_N_HEADS, ATTN_HEAD_DIM)
        k = k.reshape(Bsz, L, ATTN_N_KV_HEADS, ATTN_HEAD_DIM)
        v = v.reshape(Bsz, L, ATTN_N_KV_HEADS, ATTN_HEAD_DIM)
        y_attn = windowed_gqa(q, k, v, attn_sink[i]) @ w_attn_proj[i]
        mix = (jax.nn.sigmoid(gate_a) * y_ssd + jax.nn.sigmoid(gate_b) * y_attn) @ w_out[i]
        x = x + rmsnorm(mix, post_mix_norm[i])
        h2 = rmsnorm(x, pre_ffn_norm[i])
        g, u = _split_cols(h2 @ w_ffn_in[i], (D_FF, D_FF))
        f = (jax.nn.silu(g) * u) @ w_ffn_out[i]
        x = x + rmsnorm(f, post_ffn_norm[i])
    return x


_drawn_inputs = setup_inputs


def setup_inputs(seed=0):
    import zlib

    import numpy as np

    out = dict(_drawn_inputs(seed))
    spreads = {}
    factors = {'attn_sink': 5.284}
    for name, (base, spread) in spreads.items():
        noise = np.random.default_rng([zlib.crc32(name.encode()), seed]).standard_normal(out[name].shape)
        drawn = base * np.exp(spread * noise) if base else spread * noise
        out[name] = __import__('jax').numpy.asarray(drawn.astype(out[name].dtype))
    for name, factor in factors.items():
        out[name] = (out[name] * factor).astype(out[name].dtype)
    return out
```

```python
from contextlib import ExitStack

import concourse.bass as bass
from concourse import mybir

ALU = mybir.AluOpType
ACT = mybir.ActivationFunctionType
F32 = mybir.dt.float32
F32R = mybir.dt.float32r
AX_X = mybir.AxisListType.X
ds = bass.ds

P = 128
EPS = 1e-6
HEAD = 64
STATE = 128
CHUNK = 128
WINDOW = 128
MASKED = -1e30
LOG1P_TERMS = 8


def hybrid_encoder_layer(nc, x, pre_mix_norm, w_in, conv_w, conv_b, dt_bias_f, dt_bias_b, A_log_f, A_log_b,
                         D_skip, ssd_norm, w_ssd_proj, attn_sink, w_attn_proj, w_out, post_mix_norm,
                         pre_ffn_norm, w_ffn_in, w_ffn_out, post_ffn_norm, out):
    _, L, D = x.shape
    KT = D // P
    NT = L // CHUNK
    taps, conv_dim = conv_w.shape[1:]
    pad = taps // 2
    inner = w_ssd_proj.shape[1]
    H = D_skip.shape[1]
    G = (conv_dim - inner) // (2 * STATE)
    R = H // G
    XT = R * HEAD // P
    NI = inner // P
    QH = attn_sink.shape[1]
    q_dim = w_attn_proj.shape[1]
    KV = 4
    kv_dim = KV * HEAD
    QR = QH // KV
    F = w_ffn_out.shape[1]
    FT = F // P
    FH = FT // 2
    HALF = 512
    SCALE = HEAD ** -0.5
    c_z, c_xbc = 0, inner
    c_dt = c_xbc + conv_dim
    c_q = c_dt + 2 * H
    c_k = c_q + q_dim
    c_v = c_k + kv_dim
    c_gate = c_v + kv_dim

    stages = [("dt", 1, 1), ("xbc", conv_dim // P, 1), ("z", NI, 1), ("gate", 2 * KT, 1), ("kv", 2 * kv_dim // P, 1),
              ("q", q_dim // P, 1), ("attn", KT, 1), ("ssd", 2 * KT, 2), ("mix", KT, 1), ("ffn_in", 2 * FT, 1),
              ("ffn_out", 4 * KT, 2)]
    U0, O0, NU = {}, {}, {}
    u = o = 0
    for name, n, per in stages:
        U0[name], O0[name], NU[name] = u, o, n
        u, o = u + n, o + n // per
    ALL_UNITS = u
    ST, n = {}, 0
    for name, tiles in (("xbc", conv_dim // P), ("z", NI), ("gate", 2 * KT), ("attn", KT), ("proj", KT), ("x1", NT),
                        ("ffn", 2 * KT), ("out", NT)):
        ST[name], n = n, n + 8 * tiles
        ST[name + " end"] = n

    w1 = w_in[0].rearrange("(k p) n -> p k n", p=P)
    w_ssd = w_ssd_proj[0].rearrange("(j k p) n -> p j k n", p=P, k=KT)
    w_mix = w_out[0].rearrange("(k p) n -> p k n", p=P)
    w_f1 = w_ffn_in[0].rearrange("(k p) n -> p k n", p=P)
    w_f2 = w_ffn_out[0].rearrange("(j k p) n -> p j k n", p=P, k=FH)
    w_at = w_attn_proj[0].rearrange("(g r i p) n -> r g p i n", g=KV // 2, r=2, i=QR)
    x_rows = x[0].rearrange("(t p) d -> t p d", p=P)
    out_rows = out[0].rearrange("(t p) d -> t p d", p=P)

    def dram(name, shape):
        return nc.dram_tensor(name, shape, F32, kind="Internal").ap()

    xbc_d = dram("xbc_d", [conv_dim // P, P, L])
    z_d = dram("z_d", [NI, P, L])
    gate_d = dram("gate_d", [2 * KT, P, L])
    attn_d = dram("attn_d", [KT, P, L])
    mix_d = dram("mix_d", [KT, P, L])
    proj_d = dram("proj_d", [P, KT, L])
    ffn_d = dram("ffn_d", [P, KT, L])
    x1_d = dram("x1_d", [NT, P, D])
    cum_d = dram("cum_d", [G, NT, 2, R, CHUNK])

    top = [16512]

    def at(name, shape, off, dt=F32):
        return nc.alloc_sbuf_tensor_at(name, shape, dt, offset=off)

    def const(name, shape):
        n = 4
        for s in shape[1:]:
            n *= s
        off = top[0]
        top[0] += (n + 31) // 32 * 32
        return at(name, shape, off)

    ident = const("ident", [P, P])
    tri = const("tri", [P, 2, P])
    ones = const("ones", [P, P])
    dist_off = top[0]
    dist = const("dist", [P, 3, 3 * CHUNK])
    norm_a = const("norm_a", [P, D])
    norm_off = top[0]
    norm_b = const("norm_b", [P, D])
    cw = const("cw", [P, conv_dim // P, taps])
    cb = const("cb", [P, conv_dim // P])
    dcol = const("dcol", [P, NI])
    ncol = const("ncol", [P, NI])
    sink = const("sink", [P, QH])
    dtb = const("dtb", [P, 1])
    alog = const("alog", [P, 1])
    stat = const("stat", [P, 2, 8])
    soft = const("soft", [P, 2, 6, QR])
    gact = at("gact", [P, L], dist_off)
    slot = FH * P * 4
    wraw = [at(f"wraw{j}", [P, FH, P], top[0] + j * slot) for j in range(2)]
    whi = [at(f"whi{j}", [P, FH, P], top[0] + (2 + j) * slot, F32R) for j in range(2)]
    wlo = [at(f"wlo{j}", [P, FH, P], top[0] + (4 + j) * slot, F32R) for j in range(2)]
    top[0] += 6 * slot
    late = top[0]
    dtok = const("dtok", [P, 2, NT, H])
    acum = const("acum", [P, 2, NT, H])
    wend = const("wend", [P, 2, NT, H])
    dec = const("dec", [P, 2, NT, H])
    base = top[0]
    K = 1024

    act_hi = at("act_hi", [P, KT, L], base, F32R)
    act_lo = at("act_lo", [P, KT, L], base + 32 * K, F32R)
    qT = at("qT", [P, KT, L], base + 64 * K)
    kwin = L + 2 * CHUNK
    k_all = at("k_all", [P, KV // 2, kwin], base + 96 * K)
    k_hi = at("k_hi", [P, KV // 2, 3 * CHUNK], base + 106 * K, F32R)
    k_lo = at("k_lo", [P, KV // 2, 3 * CHUNK], base + 109 * K, F32R)
    v_all = at("v_all", [P, NT + 2, kv_dim], base + 116 * K)
    tmp = base + 126 * K
    x_t = [at(f"x_t{j}", [P, D], tmp + j * 4 * K) for j in range(2)]
    x_n = [at(f"x_n{j}", [P, D], tmp + (2 + j) * 4 * K) for j in range(2)]
    junk = at("junk", [P, D], tmp + 16 * K)
    praw = [at(f"praw{j}", [P, L + 2 * pad], tmp + j * 4128) for j in range(2)]
    cacc = [at(f"cacc{j}", [P, L], tmp + 8256 + j * 4 * K) for j in range(2)]
    stage = [at(f"stage{j}", [P, L], tmp + 8256 + (2 + j) * 4 * K) for j in range(2)]
    dt_v = at("dt_v", [P, L], base + 64 * K)
    dt_e = at("dt_e", [P, L], base + 68 * K)
    dt_t = at("dt_t", [P, L], base + 72 * K)
    dt_t2 = at("dt_t2", [P, L], base + 76 * K)
    dt_q = at("dt_q", [P, L], base + 80 * K)
    dt_r = at("dt_r", [P, L], base + 84 * K)
    atok = at("atok", [P, NT, 2, H], base + 88 * K)
    rows = at("rows", [P, NT, CHUNK], base + 90 * K)
    ddif = at("ddif", [P, 2, NT, H], base + 94 * K)
    qs_hi = at("qs_hi", [P, KT, CHUNK], base, F32R)
    qs_lo = at("qs_lo", [P, KT, CHUNK], base + 4 * K, F32R)
    prob = [at(f"prob{j}", [P, QR, 3 * CHUNK], base + (8 + 6 * j) * K) for j in range(2)]
    probT = at("probT", [P, 3, QR * CHUNK], base + 20 * K)
    v_win = at("v_win", [P, 3, kv_dim], base + 26 * K)
    gate_t = [at(f"gate_t{j}", [P, L], base + (96 + 4 * j) * K) for j in range(2)]
    aout = [at(f"aout{j}", [P, L], base + (104 + 4 * j) * K) for j in range(2)]
    y_all = at("y_all", [P, NI, L], base)
    s0 = base + 64 * K
    h_back = at("h_back", [P, NT + 1, R * HEAD], s0)
    s1 = s0 + 18 * K
    xin = [at(f"xin{j}", [P, XT, CHUNK], s1 + j * 2 * K) for j in range(2)]
    bin_ = [at(f"bin{j}", [P, CHUNK], s1 + 4 * K + j * 512) for j in range(2)]
    cin = [at(f"cin{j}", [P, CHUNK], s1 + 5 * K + j * 512) for j in range(2)]
    zin = [at(f"zin{j}", [P, XT, CHUNK], s1 + 6 * K + j * 2 * K) for j in range(2)]
    s2 = s1 + 10 * K
    seg = [at(f"seg{j}", [P, 2, R, CHUNK], s2 + j * 8 * K) for j in range(2)]
    cdec = [at(f"cdec{j}", [P, 2, R, CHUNK], s2 + (16 + j * 8) * K) for j in range(2)]
    s3 = s2 + 32 * K
    xtok = [at(f"xtok{j}", [P, R, HEAD], s3 + j * 2 * K) for j in range(2)]
    xdt = [at(f"xdt{j}", [P, 2, R, HEAD], s3 + (4 + j * 4) * K) for j in range(2)]
    xend = [at(f"xend{j}", [P, R, HEAD], s3 + (12 + j * 2) * K) for j in range(2)]
    btok = [at(f"btok{j}", [P, STATE], s3 + 16 * K + j * 512) for j in range(2)]
    gm = [at(f"gm{j}", [P, 2, CHUNK], s3 + 17 * K + j * K) for j in range(2)]
    h_fwd = [at(f"h_fwd{j}", [P, R, HEAD], s3 + (19 + 2 * j) * K) for j in range(2)]
    h_tmp = at("h_tmp", [P, R, HEAD], norm_off + 2 * K)
    ddiag = at("ddiag", [P, XT, P], norm_off)
    hb_now = [at(f"hb_now{j}", [P, R, HEAD], s3 + (23 + j * 2) * K) for j in range(2)]
    y_lo = at("y_lo", [P, NI, L], base, F32R)
    y_hi = at("y_hi", [P, NI, L], base + 64 * K, F32R)
    sqj = at("sqj", [P, L], base + 128 * K)
    sqs = at("sqs", [P, L], base + 132 * K)
    yscale = at("yscale", [P, L], base + 136 * K)
    mga = at("mga", [P, L], base + 140 * K)
    mat = at("mat", [P, L], base + 144 * K)
    mout = at("mout", [P, L], dist_off)
    mraw = [at(f"mraw{j}", [P, L], base + (64 + 4 * j) * K) for j in range(2)]
    pout = [at(f"pout{j}", [P, L], base + (72 + 4 * j) * K) for j in range(2)]
    nf = [at(f"nf{j}", [P, KT, CHUNK], base + (96 + 4 * j) * K) for j in range(2)]
    nx = [at(f"nx{j}", [P, D], base + (104 + 4 * j) * K) for j in range(2)]
    n1 = [at(f"n1{j}", [P, D], base + (112 + 4 * j) * K) for j in range(2)]
    n2 = [at(f"n2{j}", [P, D], base + (120 + 4 * j) * K) for j in range(2)]
    nj = at("nj", [P, D], base + 128 * K)
    h2_hi = at("h2_hi", [P, KT, L], late, F32R)
    h2_lo = at("h2_lo", [P, KT, L], late + 32 * K, F32R)
    f_act = at("f_act", [P, FT, L], late + 64 * K)
    f_lo = at("f_lo", [P, FT, L], late + 64 * K, F32R)
    f_hi = at("f_hi", [P, FT, HALF], late, F32R)
    fout = [at(f"fout{j}", [P, HALF], late + (44 + 2 * j) * K) for j in range(2)]

    ps = nc.alloc_psum_tensor("ps", [P, 8, 512], F32)

    sems = {}

    def S(name):
        if name not in sems:
            sems[name] = nc.alloc_semaphore(name)
        return sems[name]

    def wait(eng, name, value):
        if not (isinstance(value, int) and value <= 0):
            eng.wait_ge(S(name), value)

    def pairs(eng, n, step, first=0, peel=False):
        if peel:
            step(0, 0)
            step(1, 1)
            first = 2
        turns = (n - first) // 2
        if turns > 0:
            with eng.Fori(0, turns) as i:
                for j in range(2):
                    step(i * 2 + (first + j), (first + j) % 2)
        for t in range(first + 2 * max(turns, 0), n):
            step(t, t % 2)

    def skewed(eng, n, parts):
        depth = max(lag for _, lag in parts)
        lead = depth + depth % 2
        for s in range(lead):
            for part, lag in parts:
                if 0 <= s - lag < n:
                    part(s - lag, (s - lag) % 2)
        with eng.Fori(0, (n - lead) // 2) as i:
            for j in range(2):
                for part, lag in parts:
                    part(i * 2 + (lead + j - lag), (lead + j - lag) % 2)
        for s in range(n, n + depth):
            for part, lag in parts:
                if s - lag < n:
                    part(s - lag, (s - lag) % 2)

    def pair_of(o):
        return ps[:, 2 * (o % 2):2 * (o % 2) + 2, :]

    block = nc.Block()
    with block:

        @block.sync
        def _(sp):
            def slot_free(v, p):
                wait(sp, "w_lo_done", v - 1)

            def landed(p):
                return S(f"w_landed{p}")

            def w_plain(src, first):
                def load(v, p, t):
                    slot_free(v, p)
                    sp.dma_start(wraw[p][:, 0:KT, :], src[:, :, ds(t * P + first, P)]).then_inc(landed(p), 64)
                return load

            def w_query(v, p, t, half):
                slot_free(v, p)
                for r in range(2):
                    sp.dma_start(wraw[p][:, 0:KT, r * HEAD:(r + 1) * HEAD],
                                 w1[:, :, ds(t * HEAD + (c_q + (2 * half + r) * QR * HEAD), HEAD)]
                                 ).then_inc(landed(p), 32)

            def w_attn(v, p, t):
                slot_free(v, p)
                for r in range(2):
                    for g in range(2):
                        sp.dma_start(wraw[p][r * HEAD:(r + 1) * HEAD, g * QR:(g + 1) * QR, :],
                                     w_at[r, g][:, :, ds(t * P, P)]).then_inc(landed(p), 16)

            def w_ssd_half(v, p, t, j):
                slot_free(v, p)
                sp.dma_start(wraw[p][:, 0:KT, :], w_ssd[:, j, :, ds(t * P, P)]).then_inc(landed(p), 64)

            def w_ffn_half(v, p, t, j):
                slot_free(v, p)
                sp.dma_start(wraw[p][:, 0:FH, :], w_f2[:, j, :, ds(t * P, P)]).then_inc(landed(p), 64)

            loads = {
                "dt": lambda v, p, t, j: w_plain(w1, c_dt)(v, p, t),
                "xbc": lambda v, p, t, j: w_plain(w1, c_xbc)(v, p, t),
                "z": lambda v, p, t, j: w_plain(w1, c_z)(v, p, t),
                "gate": lambda v, p, t, j: w_plain(w1, c_gate)(v, p, t),
                "kv": lambda v, p, t, j: w_plain(w1, c_k)(v, p, t),
                "q": None,
                "attn": lambda v, p, t, j: w_attn(v, p, t),
                "mix": lambda v, p, t, j: w_plain(w_mix, 0)(v, p, t),
            }

            def weights(stage_name, lo, hi, extra=None):
                load = loads[stage_name]
                u0 = U0[stage_name]

                def step(t, p):
                    load(t + u0, (p + u0) % 2, t, 0)
                    if extra:
                        extra(t, p)
                pairs(sp, hi, step, first=lo)

            def small(dst, src):
                sp.dma_start(dst, src).then_inc(S("small_landed"), 16)

            weights("dt", 0, 1)
            small(norm_a[:], pre_mix_norm[0:1, :].to_broadcast((P, D)))

            def x_load(t, p):
                wait(sp, "xn_done", t - 1)
                sp.dma_start(x_t[p][:], x_rows[ds(t, 1), :, :].rearrange("t p d -> p (t d)")).then_inc(S(f"tile_landed{p}"), 16)
            for t in range(2):
                x_load(t, t)
            with nc.allow_non_contiguous_dma(reason="a few KB of columns"):
                small(dtb[0:H, :], dt_bias_f.rearrange("a h -> h a"))
                small(dtb[H:2 * H, :], dt_bias_b.rearrange("a h -> h a"))
                small(alog[0:H, :], A_log_f.rearrange("a h -> h a"))
                small(alog[H:2 * H, :], A_log_b.rearrange("a h -> h a"))
                for j in range(taps):
                    small(cw[:, :, j], conv_w[0, j].rearrange("(t p) -> p t", p=P))
                small(cb[:], conv_b[0].rearrange("(t p) -> p t", p=P))
                small(ncol[:], ssd_norm[0].rearrange("(t p) -> p t", p=P))
                for r in range(2):
                    small(dcol[r * HEAD:(r + 1) * HEAD, :],
                          D_skip[0].rearrange("(t r) -> r t", r=2)[r:r + 1, :].to_broadcast((HEAD, NI)))
            small(sink[:], attn_sink[0:1, :].to_broadcast((P, QH)))
            pairs(sp, NT, x_load, first=2)

            weights("xbc", 0, NU["xbc"])
            weights("z", 0, NU["z"])
            weights("gate", 0, NU["gate"])
            weights("kv", 0, NU["kv"])
            for half in range(2):
                def query_step(t, p, half=half):
                    v = t + (U0["q"] + half * QR)
                    w_query(v, (p + U0["q"]) % 2, t, half)
                pairs(sp, QR, query_step)

            def gate_b_load(t, p):
                wait(sp, "attn_gated", t - 1)
                if isinstance(t, int) and t == 0:
                    wait(sp, "stored0", ST["gate end"])
                    wait(sp, "stored1", ST["gate end"])
                    wait(sp, "o_moved", 2 * NT)
                    wait(sp, "pv_done", 4 * NT)
                sp.dma_start(gate_t[p][:], gate_d[ds(t + KT, 1), :, :].rearrange("t p l -> p (t l)")
                             ).then_inc(S(f"tile_landed{p}"), 16)
            weights("attn", 0, 2)
            for t in range(2):
                gate_b_load(t, t)
            weights("attn", 2, KT, extra=gate_b_load)
            for t in range(2):
                w_ssd_half(U0["ssd"] + t, (U0["ssd"] + t) % 2, 0, t)

            for j in range(2):
                wait(sp, f"stored{j}", ST["attn end"])
            wait(sp, "cum_stored", 16 * 2 * G)
            wait(sp, "attn_gated", KT)
            with sp.Fori(0, G) as g:
                def back_load(i, p):
                    m = g * NT + i
                    tok = ds(i * -CHUNK + (NT - 1) * CHUNK, CHUNK)
                    sp.wait_ge(S("fwd_read"), g * NT + 2)
                    sp.wait_ge(S("back_turned"), m + 1)
                    sp.dma_start(xin[p][:], xbc_d[ds(g * XT, XT), :, tok].rearrange("t p l -> p t l")
                                 ).then_inc(S(f"back_landed{p}"), 16)
                    sp.dma_start(bin_[p][:], xbc_d[ds(g + NI, 1), :, tok].rearrange("t p l -> p (t l)")
                                 ).then_inc(S(f"back_landed{p}"), 16)
                pairs(sp, NT, back_load)

                def fwd_load(c, p):
                    n = g * NT + c
                    tok = ds(c * CHUNK, CHUNK)
                    sp.wait_ge(S("back_turned"), g * NT + NT + 2)
                    sp.wait_ge(S("y_done"), n + 1)
                    sp.dma_start(seg[p][:].rearrange("p d r l -> p (d r l)"),
                                 cum_d[ds(g, 1), ds(c, 1)].rearrange("g c d r l -> (g c) (d r l)").to_broadcast((P, 2 * R * CHUNK))
                                 ).then_inc(S(f"seg_landed{p}"), 16)
                    sp.wait_ge(S("fwd_read"), n + 1)
                    sp.wait_ge(S("c_read_dve"), n + 1)
                    sp.wait_ge(S("c_read_pool"), n + 1)
                    sp.dma_start(xin[p][:], xbc_d[ds(g * XT, XT), :, tok].rearrange("t p l -> p t l")
                                 ).then_inc(S(f"fwd_landed{p}"), 16)
                    sp.dma_start(bin_[p][:], xbc_d[ds(g + NI, 1), :, tok].rearrange("t p l -> p (t l)")
                                 ).then_inc(S(f"fwd_landed{p}"), 16)
                    sp.dma_start(cin[p][:], xbc_d[ds(g + (NI + G), 1), :, tok].rearrange("t p l -> p (t l)")
                                 ).then_inc(S(f"fwd_landed{p}"), 16)
                    sp.wait_ge(S("y_gated"), n + 1)
                    sp.dma_start(zin[p][:], z_d[ds(g * XT, XT), :, tok].rearrange("t p l -> p t l")
                                 ).then_inc(S(f"z_landed{p}"), 16)
                pairs(sp, NT, fwd_load)

            wait(sp, "sq_summed", NI)
            def merge_load(t):
                wait(sp, "merge_out", t)
                sp.dma_start(mga[:], gate_d[ds(t, 1), :, :].rearrange("t p l -> p (t l)")).then_inc(S("merge_landed"), 16)
                sp.dma_start(mat[:], attn_d[ds(t, 1), :, :].rearrange("t p l -> p (t l)")).then_inc(S("merge_landed"), 16)
            merge_load(0)
            with sp.Fori(1, KT) as t:
                for j in range(2):
                    w_ssd_half(t * 2 + (U0["ssd"] + j), (U0["ssd"] + j) % 2, t, j)
                merge_load(t)
            weights("mix", 0, 2)

            def mix_load(t, p):
                wait(sp, "mix_lo_done", t - 1)
                sp.dma_start(mraw[p][:], mix_d[ds(t, 1), :, :].rearrange("t p l -> p (t l)")).then_inc(S(f"tile_landed{p}"), 16)
            wait(sp, "mm_done", U0["mix"])
            wait(sp, "mix_stored", 16 * KT)
            pairs(sp, KT, mix_load, peel=True)
            weights("mix", 2, KT)

            def ffn_in_weights(v, p, t, j):
                w_plain(w_f1, j * F)(v, p, t)
            for j in range(2):
                ffn_in_weights(U0["ffn_in"] + j, (U0["ffn_in"] + j) % 2, 0, j)

            def norm_load(src, add, n0):
                def load(t, p):
                    wait(sp, "n_turned", t + (n0 - 1))
                    sp.dma_start(nf[p][:], src[:, :, ds(t * CHUNK, CHUNK)]).then_inc(S(f"n_f_landed{p}"), 16)
                    wait(sp, "n_added", t + (n0 - 1))
                    if n0:
                        wait(sp, "stored0", ST["x1 end"])
                        wait(sp, "stored1", ST["x1 end"])
                    sp.dma_start(nx[p][:], add[ds(t, 1), :, :].rearrange("t p d -> p (t d)")).then_inc(S(f"n_x_landed{p}"), 16)
                return load
            sp.dma_start(norm_a[:], post_mix_norm[0:1, :].to_broadcast((P, D))).then_inc(S("norm2_landed"), 16)
            sp.dma_start(norm_b[:], pre_ffn_norm[0:1, :].to_broadcast((P, D))).then_inc(S("norm2_landed"), 16)
            wait(sp, "stored0", ST["proj end"])
            wait(sp, "stored1", ST["proj end"])
            pairs(sp, NT, norm_load(proj_d, x_rows, 0), peel=True)

            def ffn_pair(t, last):
                for j in range(2):
                    ffn_in_weights(t * 2 + (U0["ffn_in"] + j), (U0["ffn_in"] + j) % 2, t, j)
            with sp.Fori(1, FT) as t:
                ffn_pair(t, False)
            for j in range(2):
                w_ffn_half(U0["ffn_out"] + j, (U0["ffn_out"] + j) % 2, 0, j)
            with sp.Fori(1, KT) as t:
                for j in range(2):
                    w_ffn_half(t * 2 + (U0["ffn_out"] + j), (U0["ffn_out"] + j) % 2, t, j)
            with sp.Fori(0, KT) as t:
                for j in range(2):
                    w_ffn_half(t * 2 + (U0["ffn_out"] + 2 * KT + j), (U0["ffn_out"] + j) % 2, t, j)

            sp.dma_start(norm_a[:], post_ffn_norm[0:1, :].to_broadcast((P, D))).then_inc(S("norm3_landed"), 16)
            wait(sp, "mm_done", ALL_UNITS)
            wait(sp, "stored0", ST["ffn end"])
            wait(sp, "stored1", ST["ffn end"])
            pairs(sp, NT, norm_load(ffn_d, x1_d, NT))

        @block.gpsimd
        def _(pool):
            gp = nc.gpsimd
            pool.sem_inc(S("c_read_pool"), 2)
            pool.sem_inc(S("xdt_done"), 3)
            one = pool.to_reg(1.0)
            zero = pool.to_reg(0.0)
            masked = pool.to_reg(MASKED)

            def step(ins):
                step.n += 1
                ins.then_inc(S("const_step"), 1)
                pool.wait_ge(S("const_step"), step.n)
            step.n = 0
            gp.memset(ones[:], 1.0).then_inc(S("const_step"), 1)
            gp.memset(ident[:], 0.0).then_inc(S("const_step"), 1)
            step.n = 2
            pool.wait_ge(S("const_step"), 2)
            step(gp.affine_select(out=ident[:], in_=ident[:], pattern=[[-1, P]], compare_op=ALU.not_equal, fill=one,
                                  base=0, channel_multiplier=1))
            step(gp.affine_select(out=tri[:, 0, :], in_=ones[:], pattern=[[1, P]], compare_op=ALU.is_ge, fill=zero,
                                  base=0, channel_multiplier=-1))
            step(gp.affine_select(out=tri[:, 1, :], in_=ones[:], pattern=[[-1, P]], compare_op=ALU.is_ge, fill=zero,
                                  base=0, channel_multiplier=1))
            W3 = 3 * CHUNK
            for v in range(3):
                step(gp.iota(dist[:, v, :], pattern=[[-1, W3]], base=CHUNK, channel_multiplier=1,
                             allow_small_or_imprecise_dtypes=True))
            gp.memset(k_all[:, :, 0:CHUNK], 0.0).then_inc(S("pads_done"), 1)
            gp.memset(k_all[:, :, L + CHUNK:kwin], 0.0).then_inc(S("pads_done"), 1)
            gp.memset(v_all[:, 0, :], 0.0).then_inc(S("pads_done"), 1)
            gp.memset(v_all[:, NT + 1, :], 0.0).then_inc(S("pads_done"), 1)
            pool.wait_ge(S("dist_negated"), 1)
            for v in range(3):
                step(gp.affine_select(out=dist[:, v, :], in_=dist[:, v, :], pattern=[[1, W3]], compare_op=ALU.is_ge,
                                      fill=masked, base=WINDOW - CHUNK, channel_multiplier=-1))
                step(gp.affine_select(out=dist[:, v, :], in_=dist[:, v, :], pattern=[[-1, W3]], compare_op=ALU.is_ge,
                                      fill=masked, base=WINDOW + CHUNK, channel_multiplier=1))
            step(gp.affine_select(out=dist[:, 0, :], in_=dist[:, 0, :], pattern=[[1, W3]], compare_op=ALU.is_ge,
                                  fill=masked, base=-CHUNK, channel_multiplier=0))
            gp.affine_select(out=dist[:, 2, :], in_=dist[:, 2, :], pattern=[[-1, W3]], compare_op=ALU.is_ge,
                             fill=masked, base=2 * CHUNK - 1, channel_multiplier=0).then_inc(S("dist_done"), 1)

            pool.wait_ge(S("rows_done"), 2)
            for d in range(2):
                for g in range(G):
                    pool.dma_start(cum_d[g, :, d, :, :].rearrange("c r l -> r c l"),
                                   rows[d * H + g * R:d * H + (g + 1) * R, :, :]).then_inc(S("cum_stored"), 16)

            def store(dst, buf, done, n0=0):
                def s(t, p):
                    pool.wait_ge(S(done), t + (n0 + 1))
                    pool.dma_start(dst(t), buf[p][:]).then_inc(S(f"stored{p}"), 16)
                return s

            def tile_of(d):
                return lambda t: d[ds(t, 1), :, :].rearrange("t p l -> p (t l)")
            pairs(pool, conv_dim // P, store(tile_of(xbc_d), stage, "xbc_out"))
            pairs(pool, NI, store(tile_of(z_d), stage, "moved", O0["z"]))
            pairs(pool, 2 * KT, store(tile_of(gate_d), stage, "moved", O0["gate"]))

            def normalise(b, j):
                q = j % 2
                pool.wait_ge(S("rden_done"), b * KV + (j + 1))
                gp.tensor_tensor(prob[q][:], prob[q][:], soft[:, q, 4, :].unsqueeze(2).to_broadcast((P, QR, 3 * CHUNK)),
                                 ALU.mult).then_inc(S("prob_ready"), 1)

            def attn_block(b):
                normalise(b, 0)
                wait(pool, "pv_done", b * KV)
                gp.tensor_copy(v_win[:], v_all[:, ds(b, 3), :]).then_inc(S("v_win_done"), 1)
                for j in range(1, KV):
                    normalise(b, j)
            pool.wait_ge(S("pads_done"), 4)
            pool.wait_ge(S("v_turned"), NT)
            attn_block(0)
            with pool.Fori(1, NT) as b:
                attn_block(b)
            pairs(pool, KT, store(tile_of(attn_d), aout, "attn_gated"))

            def heads(tab, d, c, g):
                return tab[:, d, ds(c, 1), ds(g * R, R)].rearrange("p c r -> p (c r)")

            def wide(ap, n):
                return ap.unsqueeze(2).to_broadcast((P, R, n))
            pool.wait_ge(S("attn_gated"), KT)
            pool.wait_ge(S("stored0"), ST["attn end"])
            pool.wait_ge(S("stored1"), ST["attn end"])
            gp.memset(h_back[:, NT, :], 0.0).then_inc(S("h_zero"), 1)
            pool.wait_ge(S("h_zero"), 1)
            with pool.Fori(0, G) as g:
                def back(i, p):
                    m = g * NT + i
                    c = i * -1 + (NT - 1)
                    pool.wait_ge(S("h_fwd_done"), g * NT)
                    pool.wait_ge(S("h_back_done"), m)
                    gp.tensor_tensor(h_tmp[:], h_back[:, ds(c + 1, 1), :].rearrange("p c (r e) -> p (c r) e", e=HEAD),
                                     wide(heads(dec, 1, c, g), HEAD), ALU.mult).then_inc(S("h_decayed"), 1)
                pairs(pool, NT, back)

                def fwd_a(c, p):
                    n = g * NT + c
                    pool.wait_ge(S("seg_exp"), n + 1)
                    gp.tensor_tensor(seg[p][:, 1, :, :], seg[p][:, 1, :, :], wide(heads(acum, 1, c, g), CHUNK), ALU.subtract
                                     ).then_inc(S("seg_b_done"), 1)
                    pool.wait_ge(S(f"fwd_landed{p}"), g * (48 * NT // 2) + (c * 24 + (48 - 24 * p)))
                    gp.tensor_tensor(cdec[p][:, 1, :, :], cdec[p][:, 1, :, :], cin[p][:].unsqueeze(1).to_broadcast((P, R, CHUNK)),
                                     ALU.mult).then_inc(S("c_read_pool"), 1)
                    pool.wait_ge(S("xtok_done"), n + 1)
                    pool.wait_ge(S("y_done"), n + 1)
                    for d in range(2):
                        gp.tensor_tensor(xdt[p][:, d, :, :], xtok[p][:], wide(heads(dtok, d, c, g), HEAD), ALU.mult
                                         ).then_inc(S("xdt_done"), 1)
                    gp.tensor_tensor(xend[p][:], xtok[p][:], wide(heads(wend, 0, c, g), HEAD), ALU.mult
                                     ).then_inc(S("xdt_done"), 1)
                pairs(pool, NT, fwd_a)

            with pool.Fori(0, KT) as t:
                pool.wait_ge(S("merge_out"), t + 1)
                pool.dma_start(mix_d[ds(t, 1), :, :].rearrange("t p l -> p (t l)"), mout[:]).then_inc(S("mix_stored"), 16)
            pairs(pool, KT, store(lambda t: proj_d[:, ds(t, 1), :].rearrange("p t l -> p (t l)"), pout, "proj_out"))
            pairs(pool, NT, store(lambda t: x1_d[ds(t, 1), :, :].rearrange("t p d -> p (t d)"), n1, "n_added"))
            for half in range(2):
                def ffn_store(t, p, half=half):
                    pool.wait_ge(S("ffn_out_done"), t + (half * KT + 1))
                    pool.dma_start(ffn_d[:, ds(t, 1), half * HALF:(half + 1) * HALF].rearrange("p t l -> p (t l)"),
                                   fout[p][:]).then_inc(S(f"stored{p}"), 16)
                pairs(pool, KT, ffn_store)

            def result(t, p):
                pool.wait_ge(S("n_added"), t + (NT + 1))
                pool.dma_start(out_rows[ds(t, 1), :, :].rearrange("t p d -> p (t d)"), n1[p][:]).then_inc(S(f"stored{p}"), 16)
            pairs(pool, NT, result)
            pool.wait_ge(S("stored0"), ST["out end"])
            pool.wait_ge(S("stored1"), ST["out end"])

        @block.scalar
        def _(act):
            sc = nc.scalar

            def w_hi(v, p, kt=KT):
                act.wait_ge(S(f"w_landed{p}"), (v - p) * 32 + 64)
                wait(act, "mm_done", v - 1)
                sc.copy(whi[p][:, 0:kt, :], wraw[p][:, 0:kt, :]).then_inc(S("w_hi_done"), 1)

            def ahead(name, work, n=None, first=0):
                u0 = U0[name]

                def step(t, p):
                    w_hi(t + (u0 + 1), (p + u0 + 1) % 2)
                    work(t, p)
                pairs(act, NU[name] if n is None else n, step, first=first)

            def unit_done(name, t, per=1):
                act.wait_ge(S("mm_done"), t * per + (U0[name] + per))

            def out_ps(name, p):
                return pair_of(O0[name] + p)

            w_hi(0, 0)

            def sq_x(t, p):
                act.wait_ge(S(f"tile_landed{p}"), (t - p) * 8 + 16)
                sc.activation(junk[:], x_t[p][:], ACT.Square, accum_out=stat[:, p, 0:1]).then_inc(S("n_squared"), 1)
                act.wait_ge(S("n_mean"), t + 1)
                sc.activation(stat[:, p, 2:3], stat[:, p, 1:2], ACT.Sqrt).then_inc(S("n_root"), 1)

            def hi_h(t, p):
                act.wait_ge(S("x_turned"), t + 1)
                sc.copy(act_hi[:, :, ds(t * CHUNK, CHUNK)],
                        ps[:, 2 * p:2 * p + 2, :].rearrange("p a (b l) -> p (a b) l", l=CHUNK)).then_inc(S("h_hi_done"), 1)
            skewed(act, NT, [(sq_x, 0), (hi_h, 1)])

            HH = 2 * H
            w_hi(1, 1)
            act.wait_ge(S("small_landed"), 16 * (1 + 4 + taps + 2 + 2 + 1))
            act.wait_ge(S("mm_done"), 1)
            sc.activation(dt_v[0:HH, :], ps[0:HH, 0:2, :].rearrange("p a l -> p (a l)"), ACT.Identity, bias=dtb[0:HH, :]
                          ).then_inc(S("moved"), 1)
            sc.activation(alog[0:HH, :], alog[0:HH, :], ACT.Exp).then_inc(S("dt_act"), 1)
            act.wait_ge(S("dt_dve"), 1)
            sc.activation(dt_e[0:HH, :], dt_e[0:HH, :], ACT.Exp).then_inc(S("dt_act"), 1)
            act.wait_ge(S("dt_turned"), 1)
            sc.copy(dtok[:], ps[:, 4, :].rearrange("p (c d h) -> p d c h", c=NT, d=2)).then_inc(S("dt_tok"), 1)
            sc.copy(atok[:].rearrange("p c d h -> p (c d h)"), ps[:, 5, :]).then_inc(S("dt_tok"), 1)
            act.wait_ge(S("dt_summed"), 1)
            sc.copy(acum[:].rearrange("p d c h -> p (d c h)"), ps[:, 6, :]).then_inc(S("acum_done"), 1)
            act.wait_ge(S("dt_dve_tok"), 1)
            sc.activation(dec[:].rearrange("p d c h -> p (d c h)"), ps[:, 7, :], ACT.Exp).then_inc(S("tables_done"), 1)
            sc.activation(wend[:].rearrange("p d c h -> p (d c h)"), ddif[:].rearrange("p d c h -> p (d c h)"), ACT.Exp
                          ).then_inc(S("tables_done"), 1)
            act.wait_ge(S("rows_summed"), 1)
            psr = ps[:, 4:8, :].rearrange("p a (c d l) -> p (a c) d l", d=2, l=CHUNK)
            for d in range(2):
                sc.copy(rows[d * H:(d + 1) * H, :, :], psr[d * H:(d + 1) * H, :, d, :]).then_inc(S("rows_done"), 1)

            NX = conv_dim // P

            def xbc_raw(t, p):
                w_hi(t + (U0["xbc"] + 1), (p + U0["xbc"] + 1) % 2)
                unit_done("xbc", t)
                wait(act, "conv_done", t - 1)
                sc.copy(praw[p][:, pad:pad + L], out_ps("xbc", p).rearrange("p a l -> p (a l)")).then_inc(S("moved"), 1)

            def xbc_silu(t, p):
                act.wait_ge(S("conv_done"), t + 1)
                wait(act, f"stored{p}", (t - p) * 8)
                sc.activation(stage[p][:], cacc[p][:], ACT.Silu).then_inc(S("xbc_out"), 1)
            act.wait_ge(S("praw_zeroed"), 4)
            skewed(act, NX, [(xbc_raw, 0), (xbc_silu, 1)])

            def z_work(t, p):
                unit_done("z", t)
                wait(act, f"stored{p}", (t - p) * 8 + ST["z"])
                sc.activation(stage[p][:], out_ps("z", p).rearrange("p a l -> p (a l)"), ACT.Silu).then_inc(S("moved"), 1)
            ahead("z", z_work)

            def g_work(t, p):
                unit_done("gate", t)
                wait(act, f"stored{p}", (t - p) * 8 + ST["gate"])
                sc.activation(stage[p][:], out_ps("gate", p).rearrange("p a l -> p (a l)"), ACT.Sigmoid
                              ).then_inc(S("moved"), 1)
            ahead("gate", g_work)

            for t in range(KV):
                w_hi(t + U0["kv"] + 1, (t + U0["kv"] + 1) % 2)
                unit_done("kv", t)
                if t < KV // 2:
                    sc.copy(k_all[:, t, CHUNK:CHUNK + L], out_ps("kv", t % 2).rearrange("p a l -> p (a l)")
                            ).then_inc(S("moved"), 1)
                else:
                    if t == KV // 2:
                        act.wait_ge(S("stored0"), ST["gate end"])
                        act.wait_ge(S("stored1"), ST["gate end"])
                    sc.copy(stage[t % 2][:], out_ps("kv", t % 2).rearrange("p a l -> p (a l)")).then_inc(S("moved"), 1)

            def q_work(t, p):
                unit_done("q", t)
                sc.copy(qT[:, ds(t, 1), :].rearrange("p t l -> p (t l)"),
                        out_ps("q", p).rearrange("p a l -> p (a l)")).then_inc(S("moved"), 1)
            ahead("q", q_work)

            def stage_q(b):
                wait(act, "scored", b * QH)
                sc.copy(qs_hi[:], qT[:, :, ds(b * CHUNK, CHUNK)]).then_inc(S("qs_hi_done"), 1)
                sc.copy(k_hi[:], k_all[:, :, ds(b * CHUNK, 3 * CHUNK)]).then_inc(S("qs_hi_done"), 1)

            def exps(b, j):
                q = j % 2
                act.wait_ge(S("max_done"), b * KV + (j + 1))
                for r in range(QR):
                    sc.activation(prob[q][:, r, :], prob[q][:, r, :], ACT.Exp, bias=soft[:, q, 2, r:r + 1], scale=SCALE,
                                  accum_out=soft[:, q, 3, r:r + 1]).then_inc(S("exp_done"), 1)
                sc.activation(soft[:, q, 5, :], soft[:, q, 5, :], ACT.Exp).then_inc(S("exp_done"), 1)

            def move_pT(b, j):
                act.wait_ge(S("p_turned"), b * KV + (j + 1))
                act.wait_ge(S("pv_done"), b * KV + j)
                sc.copy(probT[:], ps[:, 4:7, :]).then_inc(S("pT_done"), 1)

            act.wait_ge(S("moved"), O0["attn"])
            act.wait_ge(S("mm_done"), U0["attn"])
            stage_q(0)
            exps(0, 0)

            def act_block(b, last=False):
                for j in range(KV):
                    if j < KV - 1:
                        exps(b, j + 1)
                    elif not last:
                        exps(b + 1, 0)
                    move_pT(b, j)
                    if j == 1 and not last:
                        stage_q(b + 1)
            with act.Fori(0, NT - 1) as b:
                act_block(b)
            act_block(NT - 1, True)

            act.wait_ge(S("o_moved"), 2 * NT)
            act.wait_ge(S("pv_done"), KV * NT)

            def o_hi(t, p):
                sc.copy(act_hi[:, ds(t, 1), :], qT[:, ds(t, 1), :]).then_inc(S("o_hi_done"), 1)
            pairs(act, KT, o_hi)
            ahead("attn", lambda t, p: None)

            act.wait_ge(S("attn_gated"), KT)
            with act.Fori(0, G) as g:
                act.wait_ge(S("y_done"), g * NT + 2)

                def back(i, p):
                    m = g * NT + i
                    act.wait_ge(S("back_turned"), m + 3)
                    act.wait_ge(S("back_state"), m + 1)
                    sc.copy(btok[p][:], ps[:, 2 + p, 0:STATE]).then_inc(S("back_btok"), 1)
                pairs(act, NT, back)

                def fwd_exp(c, p):
                    n = g * NT + c
                    act.wait_ge(S(f"seg_landed{p}"), n * 8 + (16 - 8 * p))
                    act.wait_ge(S("y_done"), n + 1)
                    sc.activation(cdec[p][:].rearrange("p d r l -> p (d r l)"), seg[p][:].rearrange("p d r l -> p (d r l)"),
                                  ACT.Exp).then_inc(S("seg_exp"), 1)
                    act.wait_ge(S("fwd_turned"), n + 1)
                    act.wait_ge(S("h_back_done"), g * NT + NT)
                    act.wait_ge(S("xdt_done"), g * (3 * NT) + c * 3)
                    sc.copy(xtok[p][:].rearrange("p r e -> p (r e)"), ps[:, p, :]).then_inc(S("xtok_done"), 1)
                    act.wait_ge(S("fwd_state"), n + 1)
                    sc.copy(btok[p][:], ps[:, 2 + p, 0:STATE]).then_inc(S("fwd_btok"), 1)
                    sc.copy(hb_now[p][:].rearrange("p r e -> p (r e)"),
                            h_back[:, ds(c + 1, 1), :].rearrange("p c e -> p (c e)")).then_inc(S("hb_done"), 1)

                def fwd_mask(c, p):
                    n = g * NT + c
                    act.wait_ge(S("arg_done"), n + 1)
                    sc.activation(seg[p][:, 0, :, :], seg[p][:, 0, :, :], ACT.Exp).then_inc(S("decay_done"), 1)
                skewed(act, NT, [(fwd_exp, 0), (fwd_mask, 1)])

            act.wait_ge(S("y_gated"), G * NT + 2)
            act.wait_ge(S("y_done"), G * NT + 2)

            def y_hi_step(t, p):
                sc.activation(y_hi[:, ds(t, 1), :].rearrange("p t l -> p (t l)"),
                              y_all[:, ds(t, 1), :].rearrange("p t l -> p (t l)"), ACT.Copy, scale=ncol[:, ds(t, 1)]
                              )
                wait(act, "sq_summed", t)
                act.sem_inc(S("y_hi_done"), 1)
                sc.activation(sqj[:], y_all[:, ds(t, 1), :].rearrange("p t l -> p (t l)"), ACT.Square
                              ).then_inc(S("y_squared"), 1)
            with act.Fori(0, NI) as t:
                y_hi_step(t, 0)
            w_hi(U0["ssd"] + 1, (U0["ssd"] + 1) % 2)
            act.wait_ge(S("sq_mean"), 1)
            sc.activation(yscale[:], yscale[:], ACT.Sqrt).then_inc(S("y_root"), 1)
            with act.Fori(0, KT) as t:
                w_hi(t * 2 + (U0["ssd"] + 2), U0["ssd"] % 2)
                w_hi(t * 2 + (U0["ssd"] + 3), (U0["ssd"] + 1) % 2)

            def m_hi(t, p):
                act.wait_ge(S(f"tile_landed{p}"), (t - p) * 8 + (8 * (NT + KT) + 16))
                sc.copy(act_hi[:, ds(t, 1), :].rearrange("p t l -> p (t l)"), mraw[p][:]).then_inc(S("mix_hi_done"), 1)
            pairs(act, KT, m_hi)

            def p_work(t, p):
                unit_done("mix", t)
                wait(act, f"stored{p}", (t - p) * 8 + ST["proj"])
                sc.copy(pout[p][:], out_ps("mix", p).rearrange("p a l -> p (a l)")).then_inc(S("proj_out"), 1)

            def p_step(t, p):
                w_hi(t + (U0["mix"] + 2), (p + U0["mix"]) % 2)
                p_work(t, p)
            pairs(act, KT - 1 - (KT - 1) % 2, p_step)
            w_hi(KT - 2 + U0["mix"] + 2, (KT - 2 + U0["mix"]) % 2)
            p_work(KT - 2, 0)
            p_work(KT - 1, 1)

            def n_a(n0):
                def part(t, p):
                    act.wait_ge(S("n_turned"), t + (n0 + 1))
                    sc.activation(nj[:], ps[:, 2 * p:2 * p + 2, :].rearrange("p a l -> p (a l)"), ACT.Square,
                                  accum_out=stat[:, p, 0:1]).then_inc(S("n_squared"), 1)
                    act.wait_ge(S("n_mean"), t + (n0 + NT + 1))
                    sc.activation(stat[:, p, 2:3], stat[:, p, 1:2], ACT.Sqrt).then_inc(S("n_root"), 1)
                return part

            def n_b(t, p):
                act.wait_ge(S("n_added"), t + 1)
                sc.activation(nj[:], n1[p][:], ACT.Square, accum_out=stat[:, p, 4:5]).then_inc(S("n2_squared_b"), 1)
                act.wait_ge(S("n2_mean_b"), t + 1)
                sc.activation(stat[:, p, 6:7], stat[:, p, 5:6], ACT.Sqrt).then_inc(S("n2_root_b"), 1)

            def n_c(t, p):
                act.wait_ge(S("h2_turned"), t + 1)
                sc.copy(h2_hi[:, :, ds(t * CHUNK, CHUNK)],
                        ps[:, 4 + 2 * p:6 + 2 * p, :].rearrange("p a (b l) -> p (a b) l", l=CHUNK)
                        ).then_inc(S("h2_hi_done"), 1)
            skewed(act, NT, [(n_a(0), 0), (n_b, 1), (n_c, 2)])

            def f_step(t, last=False):
                wait(act, "gact_read", t)
                act.wait_ge(S("mm_done"), t * 2 + (U0["ffn_in"] + 1))
                sc.activation(gact[:], pair_of(O0["ffn_in"]).rearrange("p a l -> p (a l)"), ACT.Silu).then_inc(S("g_done"), 1)

            w_hi(U0["ffn_in"] + 1, (U0["ffn_in"] + 1) % 2)
            with act.Fori(0, FT - 1) as t:
                f_step(t)
                w_hi(t * 2 + (U0["ffn_in"] + 2), U0["ffn_in"] % 2)
                w_hi(t * 2 + (U0["ffn_in"] + 3), (U0["ffn_in"] + 1) % 2)
            f_step(FT - 1)
            w_hi(U0["ffn_out"], U0["ffn_out"] % 2, FH)
            w_hi(U0["ffn_out"] + 1, (U0["ffn_out"] + 1) % 2, FH)
            act.wait_ge(S("mm_done"), U0["ffn_out"])
            act.wait_ge(S("gact_read"), FT)
            for half in range(2):
                if half:
                    act.wait_ge(S("mm_done"), U0["ffn_out"] + 2 * KT)
                with act.Fori(0, FT) as k:
                    sc.copy(f_hi[:, ds(k, 1), :].rearrange("p t l -> p (t l)"),
                            f_act[:, ds(k, 1), half * HALF:(half + 1) * HALF].rearrange("p t l -> p (t l)")
                            ).then_inc(S("f_hi_done"), 1)

                def ffn_work(t, p, half=half):
                    u = t * 2 + (U0["ffn_out"] + 2 * KT * half)
                    act.wait_ge(S("mm_done"), u + 2)
                    wait(act, f"stored{p}", (t - p) * 8 + (ST["ffn"] + 8 * KT * half))
                    sc.copy(fout[p][:], ps[:, 2 * ((O0["ffn_out"] + p) % 2), :]).then_inc(S("ffn_out_done"), 1)

                def ffn_step(t, p, half=half):
                    u = t * 2 + (U0["ffn_out"] + 2 * KT * half)
                    w_hi(u + 2, U0["ffn_out"] % 2, FH)
                    ffn_work(t, p)
                    w_hi(u + 3, (U0["ffn_out"] + 1) % 2, FH)
                if half == 0:
                    pairs(act, KT, ffn_step)
                else:
                    pairs(act, KT - 2, ffn_step)
                    ffn_step(KT - 2, 0)
                    ffn_work(KT - 1, 1)
            skewed(act, NT, [(n_a(NT), 0)])

        @block.vector
        def _(dve):
            ve = nc.vector
            dve.sem_inc(S("c_read_dve"), 2)
            dve.sem_inc(S("y_gated"), 2)

            def w_low(v, p, kt=KT):
                dve.wait_ge(S("w_hi_done"), v + 1)
                ve.tensor_tensor(wlo[p][:, 0:kt, :], wraw[p][:, 0:kt, :], whi[p][:, 0:kt, :].bitcast(F32), ALU.subtract
                                 ).then_inc(S("w_lo_done"), 1)

            def ahead(name, work, n=None, first=0):
                u0 = U0[name]

                def step(t, p):
                    w_low(t + (u0 + 1), (p + u0 + 1) % 2)
                    work(t, p)
                pairs(dve, NU[name] if n is None else n, step, first=first)

            def out_ps(name, p):
                return pair_of(O0[name] + p)

            w_low(0, 0)

            dve.wait_ge(S("small_landed"), 16 * (1 + 4 + taps + 2 + 2 + 1))

            def mean(dst, src, done):
                ve.tensor_scalar(dst, src, 1.0 / D, EPS, ALU.mult, ALU.add).then_inc(S(done), 1)

            def x_norm(t, p):
                dve.wait_ge(S("n_squared"), t + 1)
                mean(stat[:, p, 1:2], stat[:, p, 0:1], "n_mean")
                dve.wait_ge(S("n_root"), t + 1)
                ve.reciprocal(stat[:, p, 3:4], stat[:, p, 2:3]).then_inc(S("n_rstd"), 1)
                dve.wait_ge(S("n_rstd"), t + 1)
                wait(dve, "x_turned", t - 1)
                ve.scalar_tensor_tensor(x_n[p][:], x_t[p][:], stat[:, p, 3:4], norm_a[:], ALU.mult, ALU.mult
                                        ).then_inc(S("xn_done"), 1)

            def h_low(t, p):
                dve.wait_ge(S("h_hi_done"), t + 1)
                cols = ds(t * CHUNK, CHUNK)
                ve.tensor_tensor(act_lo[:, :, cols], ps[:, 2 * p:2 * p + 2, :].rearrange("p a (b l) -> p (a b) l", l=CHUNK),
                                 act_hi[:, :, cols].bitcast(F32), ALU.subtract).then_inc(S("h_done"), 1)
            skewed(dve, NT, [(x_norm, 0), (h_low, 1)])

            HH = 2 * H
            w_low(1, 1)
            count = [0]

            def link(ins):
                count[0] += 1
                ins.then_inc(S("dt_dve"), 1)
                dve.wait_ge(S("dt_dve"), count[0])
            for j in range(2):
                ve.memset(praw[j][:, 0:pad], 0.0).then_inc(S("praw_zeroed"), 1)
                ve.memset(praw[j][:, pad + L:], 0.0).then_inc(S("praw_zeroed"), 1)
            dve.wait_ge(S("moved"), 1)
            v_, e_, t_, t2_, q_, r_ = (a[0:HH, :] for a in (dt_v, dt_e, dt_t, dt_t2, dt_q, dt_r))
            link(ve.scalar_tensor_tensor(e_, v_, -1.0, v_, ALU.mult, ALU.min))
            dve.wait_ge(S("dt_act"), 2)
            link(ve.tensor_scalar(r_, e_, 2.0, None, ALU.add))
            link(ve.reciprocal(q_, r_))
            link(ve.tensor_tensor(t_, e_, q_, ALU.mult))
            link(ve.tensor_tensor(t2_, t_, t_, ALU.mult))
            link(ve.tensor_scalar(q_, t2_, 1.0 / (2 * LOG1P_TERMS + 1), None, ALU.mult))
            for k in range(LOG1P_TERMS - 1, 0, -1):
                link(ve.scalar_tensor_tensor(q_, q_, 1.0 / (2 * k + 1), t2_, ALU.add, ALU.mult))
            link(ve.scalar_tensor_tensor(q_, q_, 1.0, t_, ALU.add, ALU.mult))
            link(ve.tensor_scalar(r_, v_, 0.0, None, ALU.max))
            link(ve.scalar_tensor_tensor(v_, q_, 2.0, r_, ALU.mult, ALU.add))
            ve.tensor_scalar(e_, v_, alog[0:HH, :], -1.0, ALU.mult, ALU.mult).then_inc(S("dt_ready"), 1)
            dve.wait_ge(S("const_step"), 8)
            ve.scalar_tensor_tensor(dist[:].rearrange("p v k -> p (v k)"), dist[:].rearrange("p v k -> p (v k)"), -1.0,
                                    dist[:].rearrange("p v k -> p (v k)"), ALU.mult, ALU.min).then_inc(S("dist_negated"), 1)
            dve.wait_ge(S("acum_done"), 1)
            flat = "p d c h -> p (d c h)"
            ve.tensor_tensor(ddif[:].rearrange(flat), ps[:, 7, :], acum[:].rearrange(flat), ALU.subtract
                             ).then_inc(S("dt_dve_tok"), 1)
            dve.wait_ge(S("tables_done"), 2)
            ve.tensor_tensor(wend[:].rearrange(flat), wend[:].rearrange(flat), dtok[:].rearrange(flat), ALU.mult
                             ).then_inc(S("wend_done"), 1)

            NX = conv_dim // P

            def conv_w_ahead(t, p):
                w_low(t + (U0["xbc"] + 1), (p + U0["xbc"] + 1) % 2)

            def conv(t, p):
                dve.wait_ge(S("moved"), t + 2)
                wait(dve, "xbc_out", t - 1)
                ve.tensor_scalar(cacc[p][:], praw[p][:, 0:L], cw[:, ds(t, 1), 0:1].rearrange("p t a -> p (t a)"),
                                 cb[:, ds(t, 1)], ALU.mult, ALU.add).then_inc(S("conv_step"), 1)
                for j in range(1, taps):
                    dve.wait_ge(S("conv_step"), t * (taps - 1) + j)
                    ins = ve.scalar_tensor_tensor(cacc[p][:], praw[p][:, j:j + L],
                                                  cw[:, ds(t, 1), j:j + 1].rearrange("p t a -> p (t a)"), cacc[p][:],
                                                  ALU.mult, ALU.add)
                    if j < taps - 1:
                        ins.then_inc(S("conv_step"), 1)
                    else:
                        ins.then_inc(S("conv_done"), 1)
            skewed(dve, NX, [(conv_w_ahead, 0), (conv, 1)])

            ahead("z", lambda t, p: None)
            ahead("gate", lambda t, p: None)
            for t in range(KV):
                w_low(t + U0["kv"] + 1, (t + U0["kv"] + 1) % 2)

            def v_move(t, p):
                dve.wait_ge(S("v_turn"), t + 1)
                ve.tensor_copy(v_all[:, ds(t + 1, 1), :].rearrange("p t e -> p (t e)"), ps[:, 4 + p, 0:kv_dim]
                               ).then_inc(S("v_turned"), 1)
            for t in range(NT):
                v_move(t, t % 2)
            ahead("q", lambda t, p: None)

            def low_q(b):
                dve.wait_ge(S("qs_hi_done"), b * 2 + 1)
                ve.tensor_tensor(qs_lo[:], qT[:, :, ds(b * CHUNK, CHUNK)], qs_hi[:].bitcast(F32), ALU.subtract
                                 ).then_inc(S("qs_done"), 1)
                dve.wait_ge(S("qs_hi_done"), b * 2 + 2)
                ve.tensor_tensor(k_lo[:], k_all[:, :, ds(b * CHUNK, 3 * CHUNK)], k_hi[:].bitcast(F32), ALU.subtract
                                 ).then_inc(S("qs_done"), 1)

            def maxima(b, j, variant):
                q = j % 2
                if not (isinstance(b, int) and b == 0 and j < 2):
                    dve.wait_ge(S("p_turned"), b * KV + (j - 1))
                for r in range(QR):
                    slope = 2.0 ** (-8.0 * (j * QR + r + 1) / QH)
                    dve.wait_ge(S("scored"), b * QH + (j * QR + r + 1))
                    ve.scalar_tensor_tensor(prob[q][:, r, :], dist[:, variant, :], slope / SCALE, ps[:, r, 0:3 * CHUNK],
                                            ALU.mult, ALU.add).then_inc(S("biased"), 1)
                dve.wait_ge(S("biased"), b * QH + (j * QR + QR))
                ve.tensor_reduce(soft[:, q, 0, :], prob[q][:], AX_X, ALU.max).then_inc(S("max_step"), 1)
                n = b * (3 * KV) + 3 * j
                dve.wait_ge(S("max_step"), n + 1)
                ve.scalar_tensor_tensor(soft[:, q, 1, :], soft[:, q, 0, :], SCALE, sink[:, j * QR:(j + 1) * QR],
                                        ALU.mult, ALU.max).then_inc(S("max_step"), 1)
                dve.wait_ge(S("max_step"), n + 2)
                ve.tensor_scalar(soft[:, q, 2, :], soft[:, q, 1, :], -1.0, None, ALU.mult).then_inc(S("max_step"), 1)
                ve.tensor_tensor(soft[:, q, 5, :], sink[:, j * QR:(j + 1) * QR], soft[:, q, 1, :], ALU.subtract
                                 ).then_inc(S("max_done"), 1)

            def denominators(b, j):
                q = j % 2
                dve.wait_ge(S("exp_done"), b * (KV * (QR + 1)) + (j + 1) * (QR + 1))
                ve.tensor_tensor(soft[:, q, 3, :], soft[:, q, 3, :], soft[:, q, 5, :], ALU.add).then_inc(S("den_done"), 1)
                dve.wait_ge(S("den_done"), b * KV + (j + 1))
                ve.reciprocal(soft[:, q, 4, :], soft[:, q, 3, :]).then_inc(S("rden_done"), 1)

            def move_o(b, g):
                dve.wait_ge(S("pv_done"), b * KV + 2 * (g + 1))
                ve.tensor_copy(qT[:, g * QR:(g + 1) * QR, ds(b * CHUNK, CHUNK)],
                               ps[:, 7, :].rearrange("p (r l) -> p r l", r=QR)).then_inc(S("o_moved"), 1)

            dve.wait_ge(S("dist_done"), 1)
            low_q(0)
            maxima(0, 0, 0)

            def dve_block(b, variant, after):
                for j in range(KV):
                    if j < KV - 1:
                        maxima(b, j + 1, variant)
                    elif after is not None:
                        maxima(b + 1, 0, after)
                    denominators(b, j)
                    if j == 0 and not (isinstance(b, int) and b == 0):
                        move_o(b - 1, 1)
                    if j == 2:
                        move_o(b, 0)
                    if j == 1 and after is not None:
                        low_q(b + 1)
            dve_block(0, 0, 1)
            with dve.Fori(1, NT - 2) as b:
                dve_block(b, 1, 1)
            dve_block(NT - 2, 1, 2)
            dve_block(NT - 1, 2, None)
            move_o(NT - 1, 1)

            def o_low(t, p):
                dve.wait_ge(S("o_hi_done"), t + 1)
                ve.tensor_tensor(act_lo[:, ds(t, 1), :], qT[:, ds(t, 1), :], act_hi[:, ds(t, 1), :].bitcast(F32), ALU.subtract
                                 ).then_inc(S("o_done"), 1)
            pairs(dve, KT, o_low)

            def attn_gate(t, p):
                dve.wait_ge(S("mm_done"), t + (U0["attn"] + 1))
                dve.wait_ge(S(f"tile_landed{p}"), (t - p) * 8 + (8 * NT + 16))
                wait(dve, f"stored{p}", (t - p) * 8 + ST["attn"])
                ve.tensor_tensor(aout[p][:], out_ps("attn", p).rearrange("p a l -> p (a l)"), gate_t[p][:], ALU.mult
                                 ).then_inc(S("attn_gated"), 1)
            ahead("attn", attn_gate)

            dve.wait_ge(S("stored0"), ST["attn end"])
            dve.wait_ge(S("stored1"), ST["attn end"])

            def heads(tab, d, c, g):
                return tab[:, d, ds(c, 1), ds(g * R, R)].rearrange("p c r -> p (c r)")

            def wide(ap, n):
                return ap.unsqueeze(2).to_broadcast((P, R, n))
            dve.wait_ge(S("wend_done"), 1)
            with dve.Fori(0, G) as g:
                dve.wait_ge(S("y_done"), g * NT + 2)
                dve.wait_ge(S("h_fwd_done"), g * NT)
                ve.memset(h_fwd[0][:], 0.0).then_inc(S("h_cleared"), 1)
                for i in range(XT):
                    ve.tensor_scalar(ddiag[:, i, :], ident[:], dcol[:, ds(g * XT + i, 1)], None, ALU.mult
                                     ).then_inc(S("ddiag_done"), 1)

                def back_x(i, p):
                    m = g * NT + i
                    c = i * -1 + (NT - 1)
                    dve.wait_ge(S("back_turned"), m + 3)
                    dve.wait_ge(S("back_state"), m + 1)
                    ve.tensor_tensor(xend[p][:], ps[:, p, :].rearrange("p (r e) -> p r e", e=HEAD),
                                     wide(heads(wend, 1, c, g), HEAD), ALU.mult).then_inc(S("back_x"), 1)

                def back_h(i, p):
                    m = g * NT + i
                    c = i * -1 + (NT - 1)
                    dve.wait_ge(S("back_state"), m + 3)
                    dve.wait_ge(S("h_decayed"), m + 1)
                    dve.wait_ge(S("hb_done"), g * NT)
                    ve.tensor_tensor(h_back[:, ds(c, 1), :].rearrange("p c e -> p (c e)"), ps[:, 4 + p, :],
                                     h_tmp[:].rearrange("p r e -> p (r e)"), ALU.add).then_inc(S("h_back_done"), 1)
                skewed(dve, NT, [(back_x, 0), (back_h, 1)])

                def fwd_a(c, p):
                    n = g * NT + c
                    dve.wait_ge(S("fwd_turned"), n + 1)
                    ve.tensor_tensor(gm[p][:], ps[:, 4, 0:CHUNK].unsqueeze(1).to_broadcast((P, 2, CHUNK)), tri[:], ALU.mult
                                     ).then_inc(S("gm_done"), 1)
                    dve.wait_ge(S("seg_exp"), n + 1)
                    ve.tensor_tensor(seg[p][:, 0, :, :], seg[p][:, 0, :, :], wide(heads(acum, 0, c, g), CHUNK), ALU.subtract
                                     ).then_inc(S("seg_step"), 1)
                    ve.tensor_tensor(cdec[p][:, 0, :, :], cdec[p][:, 0, :, :], cin[p][:].unsqueeze(1).to_broadcast((P, R, CHUNK)),
                                     ALU.mult).then_inc(S("c_read_dve"), 1)
                    dve.wait_ge(S("seg_step"), n * 2 + 1)
                    ve.tensor_scalar(seg[p][:, 0, :, :], seg[p][:, 0, :, :], 0.0, None, ALU.min).then_inc(S("seg_step"), 1)
                    dve.wait_ge(S("seg_step"), n * 2 + 2)
                    dve.wait_ge(S("seg_b_done"), n + 1)
                    ve.scalar_tensor_tensor(seg[p][:, 0, :, :], seg[p][:, 1, :, :], 0.0, seg[p][:, 0, :, :], ALU.min, ALU.add
                                            ).then_inc(S("arg_done"), 1)

                def fwd_b(c, p):
                    n = g * NT + c
                    dve.wait_ge(S("decay_done"), n + 1)
                    dve.wait_ge(S("gm_done"), n + 1)
                    ve.tensor_tensor(seg[p][:, 1, :, :], seg[p][:, 0, :, :],
                                     gm[p][:, 1, :].unsqueeze(1).to_broadcast((P, R, CHUNK)), ALU.mult).then_inc(S("mask_step"), 1)
                    dve.wait_ge(S("mask_step"), n + 1)
                    ve.tensor_tensor(seg[p][:, 0, :, :], seg[p][:, 0, :, :],
                                     gm[p][:, 0, :].unsqueeze(1).to_broadcast((P, R, CHUNK)), ALU.mult).then_inc(S("mask_done"), 1)
                    dve.wait_ge(S("h_cleared"), g + 1)
                    dve.wait_ge(S("h_fwd_done"), n)
                    ve.tensor_tensor(h_tmp[:], h_fwd[p][:], wide(heads(dec, 0, c, g), HEAD), ALU.mult).then_inc(S("h_step"), 1)
                    dve.wait_ge(S("h_step"), n + 1)
                    dve.wait_ge(S("fwd_state"), n + 3)
                    dve.wait_ge(S("y_done"), n + 2)
                    ve.tensor_tensor(h_fwd[1 - p][:].rearrange("p r e -> p (r e)"), ps[:, 5, :],
                                     h_tmp[:].rearrange("p r e -> p (r e)"), ALU.add).then_inc(S("h_fwd_done"), 1)

                def fwd_c(c, p):
                    n = g * NT + c
                    dve.wait_ge(S("y_done"), n + 3)
                    dve.wait_ge(S(f"z_landed{p}"), n * 8 + (16 - 8 * p))
                    ve.tensor_tensor(y_all[:, ds(g * XT, XT), ds(c * CHUNK, CHUNK)],
                                     ps[:, 6 + p, :].rearrange("p (t l) -> p t l", t=XT), zin[p][:], ALU.mult
                                     ).then_inc(S("y_gated"), 1)
                skewed(dve, NT, [(fwd_a, 0), (fwd_b, 1), (fwd_c, 2)])

            ve.memset(sqs[:], 0.0).then_inc(S("sq_zero"), 1)
            dve.wait_ge(S("sq_zero"), 1)
            with dve.Fori(0, NI) as t:
                row = y_all[:, ds(t, 1), :].rearrange("p t l -> p (t l)")
                dve.wait_ge(S("y_squared"), t + 1)
                ve.tensor_tensor(sqs[:], sqs[:], sqj[:], ALU.add).then_inc(S("sq_summed"), 1)
                ve.scalar_tensor_tensor(y_lo[:, ds(t, 1), :].rearrange("p t l -> p (t l)"), row, ncol[:, ds(t, 1)],
                                        y_hi[:, ds(t, 1), :].rearrange("p t l -> p (t l)").bitcast(F32),
                                        ALU.mult, ALU.subtract).then_inc(S("y_lo_done"), 1)
                dve.wait_ge(S("sq_summed"), t + 1)
            w_low(U0["ssd"] + 1, (U0["ssd"] + 1) % 2)
            dve.wait_ge(S("sq_spread"), 1)
            ve.tensor_scalar(yscale[:], ps[:, 4:6, :].rearrange("p a l -> p (a l)"), 1.0 / inner, EPS, ALU.mult, ALU.add
                             ).then_inc(S("sq_mean"), 1)
            dve.wait_ge(S("y_root"), 1)
            ve.reciprocal(yscale[:], yscale[:]).then_inc(S("yscale_done"), 1)
            dve.wait_ge(S("yscale_done"), 1)

            def merge_out(t, p):
                dve.wait_ge(S("mm_done"), t * 2 + (U0["ssd"] + 2))
                dve.wait_ge(S("merge_landed"), t * 32 + 32)
                wait(dve, "mix_stored", t * 16)
                ve.tensor_tensor(mout[:], out_ps("ssd", p).rearrange("p a l -> p (a l)"), yscale[:], ALU.mult
                                 ).then_inc(S("merge_step"), 1)
                dve.wait_ge(S("merge_step"), t * 2 + 1)
                ve.tensor_tensor(mout[:], mout[:], mga[:], ALU.mult).then_inc(S("merge_step"), 1)
                dve.wait_ge(S("merge_step"), t * 2 + 2)
                ve.tensor_tensor(mout[:], mout[:], mat[:], ALU.add).then_inc(S("merge_out"), 1)

            def merge_step(t, p):
                w_low(t * 2 + (U0["ssd"] + 2), U0["ssd"] % 2)
                merge_out(t, p)
                w_low(t * 2 + (U0["ssd"] + 3), (U0["ssd"] + 1) % 2)
            pairs(dve, KT, merge_step)

            def m_low(t, p):
                dve.wait_ge(S("mix_hi_done"), t + 1)
                ve.tensor_tensor(act_lo[:, ds(t, 1), :].rearrange("p t l -> p (t l)"), mraw[p][:],
                                 act_hi[:, ds(t, 1), :].rearrange("p t l -> p (t l)").bitcast(F32), ALU.subtract
                                 ).then_inc(S("mix_lo_done"), 1)
            pairs(dve, KT, m_low)
            with dve.Fori(0, (KT - 2) // 2) as i:
                for j in range(2):
                    w_low(i * 2 + (U0["mix"] + 2 + j), (U0["mix"] + j) % 2)
            w_low(U0["ffn_in"], U0["ffn_in"] % 2)

            def n_a(n0):
                def part(t, p):
                    dve.wait_ge(S("n_squared"), t + (n0 + NT + 1))
                    mean(stat[:, p, 1:2], stat[:, p, 0:1], "n_mean")
                    dve.wait_ge(S("n_root"), t + (n0 + NT + 1))
                    ve.reciprocal(stat[:, p, 3:4], stat[:, p, 2:3]).then_inc(S("n_rstd"), 1)
                    dve.wait_ge(S("n_rstd"), t + (n0 + NT + 1))
                    if n0 == 0:
                        wait(dve, "h2_turned", t - 1)
                    ve.scalar_tensor_tensor(n2[p][:], ps[:, 2 * p:2 * p + 2, :].rearrange("p a l -> p (a l)"), stat[:, p, 3:4],
                                            norm_a[:], ALU.mult, ALU.mult).then_inc(S("n_scaled"), 1)
                    dve.wait_ge(S("n_scaled"), t + (n0 + 1))
                    dve.wait_ge(S(f"n_x_landed{p}"), (t - p) * 8 + (8 * n0 + 16))
                    name = "out" if n0 else "x1"
                    wait(dve, f"stored{p}", (t - p) * 8 + ST[name])
                    ve.tensor_tensor(n1[p][:], n2[p][:], nx[p][:], ALU.add).then_inc(S("n_added"), 1)
                return part

            def n_b(t, p):
                dve.wait_ge(S("n2_squared_b"), t + 1)
                mean(stat[:, p, 5:6], stat[:, p, 4:5], "n2_mean_b")
                dve.wait_ge(S("n2_root_b"), t + 1)
                ve.reciprocal(stat[:, p, 7:8], stat[:, p, 6:7]).then_inc(S("n2_rstd_b"), 1)
                dve.wait_ge(S("n2_rstd_b"), t + 1)
                ve.scalar_tensor_tensor(n2[p][:], n1[p][:], stat[:, p, 7:8], norm_b[:], ALU.mult, ALU.mult
                                        ).then_inc(S("h2_done"), 1)

            def n_c(t, p):
                dve.wait_ge(S("h2_hi_done"), t + 1)
                cols = ds(t * CHUNK, CHUNK)
                ve.tensor_tensor(h2_lo[:, :, cols], ps[:, 4 + 2 * p:6 + 2 * p, :].rearrange("p a (b l) -> p (a b) l", l=CHUNK),
                                 h2_hi[:, :, cols].bitcast(F32), ALU.subtract).then_inc(S("h2_lo_done"), 1)
            dve.wait_ge(S("norm2_landed"), 32)
            skewed(dve, NT, [(n_a(0), 0), (n_b, 1), (n_c, 2)])

            dve.wait_ge(S("stored0"), ST["x1 end"])
            dve.wait_ge(S("stored1"), ST["x1 end"])

            def f_step(t):
                dve.wait_ge(S("g_done"), t + 1)
                dve.wait_ge(S("mm_done"), t * 2 + (U0["ffn_in"] + 2))
                ve.tensor_tensor(f_act[:, ds(t, 1), :].rearrange("p t l -> p (t l)"),
                                 pair_of(O0["ffn_in"] + 1).rearrange("p a l -> p (a l)"), gact[:], ALU.mult
                                 ).then_inc(S("gact_read"), 1)
            w_low(U0["ffn_in"] + 1, (U0["ffn_in"] + 1) % 2)
            with dve.Fori(0, FT - 1) as t:
                w_low(t * 2 + (U0["ffn_in"] + 2), U0["ffn_in"] % 2)
                f_step(t)
                w_low(t * 2 + (U0["ffn_in"] + 3), (U0["ffn_in"] + 1) % 2)
            w_low(U0["ffn_out"], U0["ffn_out"] % 2, FH)
            f_step(FT - 1)
            w_low(U0["ffn_out"] + 1, (U0["ffn_out"] + 1) % 2, FH)
            for half in range(2):
                cols = slice(half * HALF, (half + 1) * HALF)
                with dve.Fori(0, FT) as k:
                    dve.wait_ge(S("f_hi_done"), k + (half * FT + 1))
                    ve.tensor_tensor(f_lo[:, ds(k, 1), cols].rearrange("p t l -> p (t l)"),
                                     f_act[:, ds(k, 1), cols].rearrange("p t l -> p (t l)"),
                                     f_hi[:, ds(k, 1), :].rearrange("p t l -> p (t l)").bitcast(F32), ALU.subtract
                                     ).then_inc(S("f_lo_done"), 1)
                n = 2 * KT if half == 0 else 2 * KT - 2
                with dve.Fori(0, n // 2) as i:
                    for j in range(2):
                        w_low(i * 2 + (U0["ffn_out"] + 2 * KT * half + 2 + j), (U0["ffn_out"] + j) % 2, FH)
            dve.wait_ge(S("norm3_landed"), 16)
            skewed(dve, NT, [(n_a(NT), 0)])

        @block.tensor
        def _(pe):
            te = nc.tensor
            for name in ("back_turned", "back_state", "fwd_read", "fwd_state", "y_done"):
                pe.sem_inc(S(name), 2)

            def product(dst, p, kt, moving, first=True, last=True, ready=None):
                for k in range(kt):
                    if ready:
                        ready(k)
                    begin, end = first and k == 0, last and k == kt - 1
                    ins = None
                    for h, d in enumerate(dst):
                        mh, ml = moving(h, k)
                        te.matmul(d, whi[p][:, k, :], mh, start=begin, stop=False)
                        te.matmul(d, whi[p][:, k, :], ml, start=False, stop=False)
                    for h, d in enumerate(dst):
                        ins = te.matmul(d, wlo[p][:, k, :], moving(h, k)[0], start=False, stop=end)
                return ins

            def from_act(h, k):
                cols = slice(h * HALF, (h + 1) * HALF)
                return act_hi[:, k, cols], act_lo[:, k, cols]

            def from_h2(h, k):
                cols = slice(h * HALF, (h + 1) * HALF)
                return h2_hi[:, k, cols], h2_lo[:, k, cols]

            def unit(name, t, p, ready=None, moving=from_act):
                u0, o0 = U0[name], O0[name]
                b = 2 * ((o0 + p) % 2)
                pe.wait_ge(S("w_lo_done"), t + (u0 + 1))
                product([ps[:, b, :], ps[:, b + 1, :]], (u0 + p) % 2, KT, moving, ready=ready).then_inc(S("mm_done"), 1)

            pe.wait_ge(S("const_step"), 8)

            def turn_x(t, p):
                pe.wait_ge(S("xn_done"), t + 1)
                wait(pe, "h_done", t - 1)
                for k in range(KT):
                    ins = te.transpose(ps[:, 2 * p + k // 4, (k % 4) * P:(k % 4 + 1) * P], x_n[p][:, k * P:(k + 1) * P], ident[:])
                ins.then_inc(S("x_turned"), 1)
            pairs(pe, NT, turn_x, peel=True)
            pe.wait_ge(S("h_done"), NT)
            unit("dt", 0, 0)

            def xbc_unit(t, p):
                wait(pe, "moved", t)
                unit("xbc", t, p)
            xbc_unit(0, 0)
            pe.wait_ge(S("dt_ready"), 1)
            HH = 2 * H
            for src, bank in ((dt_v, 4), (dt_e, 5)):
                for c in range(NT):
                    ins = te.transpose(ps[:, bank, c * HH:(c + 1) * HH], src[0:HH, c * CHUNK:(c + 1) * CHUNK], ident[0:HH, 0:HH])
            ins.then_inc(S("dt_turned"), 1)
            pe.wait_ge(S("dt_tok"), 2)
            for d in range(2):
                for bank, mat_ in ((6, tri[:, d, :]), (7, ones[:])):
                    ins = te.matmul(ps[:, bank, d * NT * H:(d + 1) * NT * H].rearrange("p (c h) -> p c h", h=H), mat_,
                                    atok[:, :, d, :], start=True, stop=True, skip_group_check=True)
            ins.then_inc(S("dt_summed"), 1)
            pe.wait_ge(S("tables_done"), 2)
            for c in range(NT):
                ins = te.matmul(ps[0:HH, 4 + c // 2, (c % 2) * 256:(c % 2 + 1) * 256], atok[:, c, :, :].rearrange("p d h -> p (d h)"),
                                tri[:].rearrange("p d l -> p (d l)"), start=True, stop=True, skip_group_check=True)
            ins.then_inc(S("rows_summed"), 1)
            xbc_unit(1, 1)
            pairs(pe, conv_dim // P, xbc_unit, first=2)

            def z_unit(t, p):
                wait(pe, "moved", t + (O0["z"] - 1))
                unit("z", t, p)
            pairs(pe, NI, z_unit)

            def gate_unit(t, p):
                wait(pe, "moved", t + (O0["gate"] - 1))
                unit("gate", t, p)
            pairs(pe, 2 * KT, gate_unit)
            for t in range(KV):
                pe.wait_ge(S("moved"), O0["kv"] + t - 1)
                unit("kv", t, t % 2)

            def q_unit(t, p):
                wait(pe, "moved", t + (O0["q"] - 1))
                unit("q", t, p)
            pe.wait_ge(S("moved"), O0["q"])
            for t in range(NT):
                wait(pe, "v_turned", t - 1)
                for j in range(2):
                    ins = te.transpose(ps[:, 4 + t % 2, j * P:(j + 1) * P], stage[j][:, t * CHUNK:(t + 1) * CHUNK], ident[:])
                ins.then_inc(S("v_turn"), 1)
            pairs(pe, q_dim // P, q_unit)

            def score(b, j):
                half = slice((j % 2) * HEAD, (j % 2 + 1) * HEAD)
                g = j // 2
                pe.wait_ge(S("qs_done"), b * 2 + 2)
                if not (isinstance(b, int) and b == 0 and j == 0):
                    pe.wait_ge(S("biased"), b * QH + j * QR)
                for r in range(QR):
                    i = g * QR + r
                    te.matmul(ps[:, r, 0:3 * CHUNK], qs_hi[half, i, :], k_hi[half, g, :], start=True, stop=False)
                    te.matmul(ps[:, r, 0:3 * CHUNK], qs_hi[half, i, :], k_lo[half, g, :], start=False, stop=False)
                    te.matmul(ps[:, r, 0:3 * CHUNK], qs_lo[half, i, :], k_hi[half, g, :], start=False, stop=True
                              ).then_inc(S("scored"), 1)

            def turn_p(b, j):
                pe.wait_ge(S("prob_ready"), b * KV + (j + 1))
                pe.wait_ge(S("pT_done"), b * KV + j)
                for kb in range(3):
                    for r in range(QR):
                        ins = te.transpose(ps[:, 4 + kb, r * CHUNK:(r + 1) * CHUNK],
                                           prob[j % 2][:, r, kb * CHUNK:(kb + 1) * CHUNK], ident[:])
                ins.then_inc(S("p_turned"), 1)

            def weigh_v(b, j):
                pe.wait_ge(S("v_win_done"), b + 1)
                pe.wait_ge(S("pT_done"), b * KV + (j + 1))
                if j % 2 == 0:
                    pe.wait_ge(S("o_moved"), b * 2 + j // 2)
                for kb in range(3):
                    ins = te.matmul(ps[(j % 2) * HEAD:(j % 2 + 1) * HEAD, 7, :], v_win[:, kb, j * HEAD:(j + 1) * HEAD],
                                    probT[:, kb, :], start=kb == 0, stop=kb == 2)
                ins.then_inc(S("pv_done"), 1)

            pe.wait_ge(S("pads_done"), 4)
            pe.wait_ge(S("moved"), O0["attn"])
            score(0, 0)
            score(0, 1)

            def pe_block(b, last=False):
                for j in range(KV):
                    turn_p(b, j)
                    if j < 2:
                        score(b, j + 2)
                    elif not last:
                        score(b + 1, j - 2)
                    weigh_v(b, j)
            with pe.Fori(0, NT - 1) as b:
                pe_block(b)
            pe_block(NT - 1, True)

            def o_ready(k):
                pe.wait_ge(S("o_done"), k + 1)

            def attn_unit(t, p):
                wait(pe, "attn_gated", t - 1)
                unit("attn", t, p, ready=o_ready if isinstance(t, int) and t == 0 else None)
            attn_unit(0, 0)
            attn_unit(1, 1)
            pairs(pe, KT, attn_unit, first=2)

            pe.wait_ge(S("attn_gated"), KT)
            with pe.Fori(0, G) as g:
                def turn_back(i, p):
                    m = g * NT + i
                    pe.wait_ge(S(f"back_landed{p}"), g * (32 * NT // 2) + (i * 16 + (32 - 16 * p)))
                    pe.wait_ge(S("back_x"), m)
                    pe.wait_ge(S("back_btok"), m)
                    for k in range(XT):
                        te.transpose(ps[:, p, k * P:(k + 1) * P], xin[p][:, k, :], ident[:])
                    te.transpose(ps[:, 2 + p, 0:STATE], bin_[p][:], ident[:]).then_inc(S("back_turned"), 1)

                def state_back(i, p):
                    m = g * NT + i
                    pe.wait_ge(S("back_x"), m + 1)
                    pe.wait_ge(S("back_btok"), m + 1)
                    pe.wait_ge(S("h_back_done"), m)
                    te.matmul(ps[:, 4 + p, :], btok[p][:], xend[p][:].rearrange("p r e -> p (r e)"), start=True, stop=True
                              ).then_inc(S("back_state"), 1)
                skewed(pe, NT, [(turn_back, 0), (state_back, 1)])

                def turn_fwd(c, p):
                    n = g * NT + c
                    pe.wait_ge(S(f"fwd_landed{p}"), g * (48 * NT // 2) + (c * 24 + (48 - 24 * p)))
                    pe.wait_ge(S("xtok_done"), n)
                    pe.wait_ge(S("fwd_btok"), n)
                    pe.wait_ge(S("gm_done"), n)
                    pe.wait_ge(S("h_back_done"), g * NT + NT)
                    for k in range(XT):
                        te.transpose(ps[:, p, k * P:(k + 1) * P], xin[p][:, k, :], ident[:])
                    te.transpose(ps[:, 2 + p, 0:STATE], bin_[p][:], ident[:])
                    te.matmul(ps[:, 4, 0:CHUNK], bin_[p][:], cin[p][:], start=True, stop=True).then_inc(S("fwd_turned"), 1)

                def skip_x(c, p):
                    n = g * NT + c
                    pe.wait_ge(S("y_gated"), n + 1)
                    pe.wait_ge(S("ddiag_done"), g * XT + XT)
                    for k in range(XT):
                        ins = te.matmul(ps[:, 6 + p, k * CHUNK:(k + 1) * CHUNK], ddiag[:, k, :], xin[p][:, k, :],
                                        start=k == 0, stop=False, skip_group_check=True)
                    ins.then_inc(S("fwd_read"), 1)

                def sums(c, p):
                    n = g * NT + c
                    pe.wait_ge(S("xdt_done"), g * (3 * NT) + (c * 3 + 6))
                    pe.wait_ge(S("fwd_btok"), n + 1)
                    pe.wait_ge(S("h_fwd_done"), n)
                    pe.wait_ge(S("h_cleared"), g + 1)
                    te.matmul(ps[:, 5, :], btok[p][:], xend[p][:].rearrange("p r e -> p (r e)"), start=True, stop=True
                              ).then_inc(S("fwd_state"), 1)
                    pe.wait_ge(S("c_read_dve"), n + 3)
                    pe.wait_ge(S("c_read_pool"), n + 3)
                    pe.wait_ge(S("hb_done"), n + 1)
                    pe.wait_ge(S("mask_done"), n + 1)
                    for r in range(R):
                        dst = ps[(r % 2) * HEAD:(r % 2 + 1) * HEAD, 6 + p, (r // 2) * CHUNK:(r // 2 + 1) * CHUNK]
                        for a, (lhs, rhs) in enumerate(((h_fwd[p][:, r, :], cdec[p][:, 0, r, :]),
                                                        (hb_now[p][:, r, :], cdec[p][:, 1, r, :]),
                                                        (xdt[p][:, 1, r, :], seg[p][:, 1, r, :]),
                                                        (xdt[p][:, 0, r, :], seg[p][:, 0, r, :]))):
                            ins = te.matmul(dst, lhs, rhs, start=False, stop=a == 3, skip_group_check=True)
                    ins.then_inc(S("y_done"), 1)
                skewed(pe, NT, [(turn_fwd, 0), (sums, 1), (skip_x, 0)])

            def from_y(j):
                def moving(h, k):
                    cols = slice(h * HALF, (h + 1) * HALF)
                    return y_hi[:, j * KT + k, cols], y_lo[:, j * KT + k, cols]
                return moving

            def ssd_out(t, p, ready=None):
                u0 = U0["ssd"]
                b = 2 * ((O0["ssd"] + p) % 2)
                for j in range(2):
                    pe.wait_ge(S("w_lo_done"), t * 2 + (u0 + j + 1))
                    if j == 0:
                        wait(pe, "merge_out", t - 1)
                    product([ps[:, b, :], ps[:, b + 1, :]], (u0 + j) % 2, KT, from_y(j), first=j == 0, last=j == 1,
                            ready=(lambda k, j=j: ready(j * KT + k)) if ready else None).then_inc(S("mm_done"), 1)
            pe.wait_ge(S("y_gated"), G * NT + 2)
            ssd_out(0, 0, ready=lambda k: pe.wait_ge(S("y_lo_done"), k + 1))
            pe.wait_ge(S("sq_summed"), NI)
            for h in range(2):
                ins = te.matmul(ps[:, 4 + h, :], ones[:], sqs[:, h * HALF:(h + 1) * HALF], start=True, stop=True)
            ins.then_inc(S("sq_spread"), 1)
            ssd_out(1, 1)
            pairs(pe, KT, ssd_out, first=2)

            def mix_unit(t, p):
                wait(pe, "proj_out", t - 1)
                unit("mix", t, p, ready=(lambda k: pe.wait_ge(S("mix_lo_done"), k + 1)) if isinstance(t, int) and t == 0 else None)
            pe.wait_ge(S("merge_out"), KT)
            mix_unit(0, 0)
            mix_unit(1, 1)
            pairs(pe, KT, mix_unit, first=2)

            def turn_f(n0):
                def part(t, p):
                    pe.wait_ge(S(f"n_f_landed{p}"), (t - p) * 8 + (8 * n0 + 16))
                    wait(pe, "n_scaled", t + (n0 - 1))
                    for k in range(KT):
                        ins = te.transpose(ps[:, 2 * p + k // 4, (k % 4) * P:(k % 4 + 1) * P], nf[p][:, k, :], ident[:])
                    ins.then_inc(S("n_turned"), 1)
                return part

            def turn_h2(t, p):
                pe.wait_ge(S("h2_done"), t + 1)
                wait(pe, "h2_lo_done", t - 1)
                for k in range(KT):
                    ins = te.transpose(ps[:, 4 + 2 * p + k // 4, (k % 4) * P:(k % 4 + 1) * P], n2[p][:, k * P:(k + 1) * P], ident[:])
                ins.then_inc(S("h2_turned"), 1)
            pe.wait_ge(S("proj_out"), KT)
            skewed(pe, NT, [(turn_f(0), 0), (turn_h2, 1)])

            pe.wait_ge(S("h2_lo_done"), NT)
            pe.wait_ge(S("n_scaled"), NT)

            def ffn_pair(t):
                wait(pe, "g_done", t)
                unit("ffn_in", t * 2, 0, moving=from_h2)
                wait(pe, "gact_read", t)
                unit("ffn_in", t * 2 + 1, 1, moving=from_h2)
            with pe.Fori(0, FT) as t:
                ffn_pair(t)

            def ffn_out(t, p, half, ready=None):
                u0 = U0["ffn_out"] + half * 2 * KT
                b = 2 * ((O0["ffn_out"] + p) % 2)
                for j in range(2):
                    pe.wait_ge(S("w_lo_done"), t * 2 + (u0 + j + 1))
                    if j == 0:
                        wait(pe, "ffn_out_done", t + (half * KT - 1))

                    def moving(h, k, j=j):
                        return f_hi[:, j * FH + k, :], f_lo[:, j * FH + k, half * HALF:(half + 1) * HALF]
                    product([ps[:, b, :]], (u0 + j) % 2, FH, moving, first=j == 0, last=j == 1,
                            ready=(lambda k, j=j: ready(j * FH + k)) if ready else None).then_inc(S("mm_done"), 1)
            pe.wait_ge(S("gact_read"), FT)
            for half in range(2):
                ffn_out(0, 0, half, ready=lambda k: pe.wait_ge(S("f_lo_done"), k + half * FT + 1))
                ffn_out(1, 1, half)
                pairs(pe, KT, lambda t, p: ffn_out(t, p, half), first=2)
            pe.wait_ge(S("ffn_out_done"), 2 * KT)
            skewed(pe, NT, [(turn_f(NT), 0)])


_INS = ['x', 'pre_mix_norm', 'w_in', 'conv_w', 'conv_b', 'dt_bias_f', 'dt_bias_b', 'A_log_f', 'A_log_b', 'D_skip',
        'ssd_norm', 'w_ssd_proj', 'attn_sink', 'w_attn_proj', 'w_out', 'post_mix_norm', 'pre_ffn_norm', 'w_ffn_in',
        'w_ffn_out', 'post_ffn_norm']


def kernel(**inputs):
    import numpy as _np
    import concourse.bacc as _bacc
    from concourse import mybir as _mybir
    from concourse.bass_utils import run_bass_kernel_spmd as _run

    nc = _bacc.Bacc("TRN2", target_bir_lowering=False, num_devices=1)
    arrays, args = {}, []
    for name in _INS:
        a = _np.ascontiguousarray(inputs[name])
        arrays[f"in_{name}_dram"] = a
        args.append(nc.dram_tensor(f"in_{name}_dram", a.shape, _mybir.dt.from_np(a.dtype), kind="ExternalInput").ap())
    args.append(nc.dram_tensor("out_dram", inputs['x'].shape, _mybir.dt.float32, kind="ExternalOutput").ap())
    hybrid_encoder_layer(nc, *args)
    r = _run(nc, [arrays], core_ids=[0])
    return r.results[0]["out_dram"]
```

```python
from contextlib import ExitStack

import concourse.bass as bass
from concourse import mybir

ALU = mybir.AluOpType
ACT = mybir.ActivationFunctionType
F32 = mybir.dt.float32
F32R = mybir.dt.float32r
AX_X = mybir.AxisListType.X
ds = bass.ds

P = 128
EPS = 1e-6
HEAD = 64
STATE = 128
CHUNK = 128
WINDOW = 128
MASKED = -1e30
LOG1P_TERMS = 8


def hybrid_encoder_layer(nc, x, pre_mix_norm, w_in, conv_w, conv_b, dt_bias_f, dt_bias_b, A_log_f, A_log_b,
                         D_skip, ssd_norm, w_ssd_proj, attn_sink, w_attn_proj, w_out, post_mix_norm,
                         pre_ffn_norm, w_ffn_in, w_ffn_out, post_ffn_norm, out):
    _, L, D = x.shape
    KT = D // P
    NT = L // CHUNK
    taps, conv_dim = conv_w.shape[1:]
    pad = taps // 2
    inner = w_ssd_proj.shape[1]
    H = D_skip.shape[1]
    G = (conv_dim - inner) // (2 * STATE)
    R = H // G
    XT = R * HEAD // P
    NI = inner // P
    QH = attn_sink.shape[1]
    q_dim = w_attn_proj.shape[1]
    KV = 4
    kv_dim = KV * HEAD
    QR = QH // KV
    F = w_ffn_out.shape[1]
    FT = F // P
    FK = [KT] + 2 * [(FT - KT) // 2]
    FK0 = [0, KT, KT + (FT - KT) // 2]
    HALF = 512
    SCALE = HEAD ** -0.5
    c_z, c_xbc = 0, inner
    c_dt = c_xbc + conv_dim
    c_q = c_dt + 2 * H
    c_k = c_q + q_dim
    c_v = c_k + kv_dim
    c_gate = c_v + kv_dim

    stages = [("dt", 1, 1), ("xbc", conv_dim // P, 1), ("kv", 2 * kv_dim // P, 1), ("q", q_dim // P, 1),
              ("zg", NI + 2 * KT, 1), ("attn", KT, 1), ("ssd", 2 * KT, 2), ("mix", KT, 1), ("ffn_in", 2 * FT, 1),
              ("ffn_out", 6 * KT, 3)]
    U0, O0, NU = {}, {}, {}
    u = o = 0
    for name, n, per in stages:
        U0[name], O0[name], NU[name] = u, o, n
        u, o = u + n, o + n // per
    ALL_UNITS = u
    ST, n = {}, 0
    for name, tiles in (("xbc", conv_dim // P), ("attn", KT), ("proj", KT), ("x1", NT),
                        ("ffn", 2 * KT), ("out", NT)):
        ST[name], n = n, n + 8 * tiles
        ST[name + " end"] = n

    w1 = w_in[0].rearrange("(k p) n -> p k n", p=P)
    w_ssd = w_ssd_proj[0].rearrange("(j k p) n -> p j k n", p=P, k=KT)
    w_mix = w_out[0].rearrange("(k p) n -> p k n", p=P)
    w_f1 = w_ffn_in[0].rearrange("(k p) n -> p k n", p=P)
    w_f2 = w_ffn_out[0].rearrange("(k p) n -> p k n", p=P)
    w_at = w_attn_proj[0].rearrange("(g r i p) n -> r g p i n", g=KV // 2, r=2, i=QR)
    x_rows = x[0].rearrange("(t p) d -> t p d", p=P)
    out_rows = out[0].rearrange("(t p) d -> t p d", p=P)

    def dram(name, shape):
        return nc.dram_tensor(name, shape, F32, kind="Internal").ap()

    xbc_d = dram("xbc_d", [conv_dim // P, P, L])
    z_d = dram("z_d", [NI, P, L])
    gate_d = dram("gate_d", [2 * KT, P, L])
    y_d = dram("y_d", [NI, P, L])
    attn_d = dram("attn_d", [KT, P, L])
    mix_d = dram("mix_d", [KT, P, L])
    proj_d = dram("proj_d", [P, KT, L])
    ffn_d = dram("ffn_d", [P, KT, L])
    x1_d = dram("x1_d", [NT, P, D])
    cum_d = dram("cum_d", [G, NT, 2, R, CHUNK])

    top = [16512]

    def at(name, shape, off, dt=F32):
        return nc.alloc_sbuf_tensor_at(name, shape, dt, offset=off)

    def const(name, shape):
        n = 4
        for s in shape[1:]:
            n *= s
        off = top[0]
        top[0] += (n + 31) // 32 * 32
        return at(name, shape, off)

    ident = const("ident", [P, P])
    tri = const("tri", [P, 2, P])
    ones = const("ones", [P, P])
    dist_off = top[0]
    dist = const("dist", [P, 3, 3 * CHUNK])
    norm_a_off = top[0]
    norm_a = const("norm_a", [P, D])
    norm_off = top[0]
    norm_b = const("norm_b", [P, D])
    cw = const("cw", [P, conv_dim // P, taps])
    cb = const("cb", [P, conv_dim // P])
    dcol = const("dcol", [P, NI])
    ncol = const("ncol", [P, NI])
    sink = const("sink", [P, QH])
    dtb = const("dtb", [P, 1])
    alog = const("alog", [P, 1])
    stat = const("stat", [P, 2, 8])
    soft = const("soft", [P, 2, 6, QR])
    gact = at("gact", [P, L], dist_off)
    slot = KT * P * 4
    wraw = [at(f"wraw{j}", [P, KT, P], top[0] + j * slot) for j in range(2)]
    whi = [at(f"whi{j}", [P, KT, P], top[0] + (2 + j) * slot, F32R) for j in range(2)]
    wlo = [at(f"wlo{j}", [P, KT, P], top[0] + (4 + j) * slot, F32R) for j in range(2)]
    top[0] += 6 * slot
    late = top[0]
    dtok = const("dtok", [P, 2, NT, H])
    acum = const("acum", [P, 2, NT, H])
    wend = const("wend", [P, 2, NT, H])
    dec = const("dec", [P, 2, NT, H])
    base = top[0]
    K = 1024

    act_hi = at("act_hi", [P, KT, L], base, F32R)
    act_lo = at("act_lo", [P, KT, L], base + 32 * K, F32R)
    qT = at("qT", [P, KT, L], base + 64 * K)
    kwin = L + 2 * CHUNK
    k_all = at("k_all", [P, KV // 2, kwin], base + 96 * K)
    k_hi = at("k_hi", [P, KV // 2, 3 * CHUNK], base + 106 * K, F32R)
    k_lo = at("k_lo", [P, KV // 2, 3 * CHUNK], base + 109 * K, F32R)
    v_all = at("v_all", [P, NT + 2, kv_dim], base + 112 * K)
    tmp = base + 122 * K
    x_t = [at(f"x_t{j}", [P, D], tmp + j * 4 * K) for j in range(2)]
    x_n = [at(f"x_n{j}", [P, D], tmp + (2 + j) * 4 * K) for j in range(2)]
    junk = at("junk", [P, D], tmp + 16 * K)
    praw = [at(f"praw{j}", [P, L + 2 * pad], tmp + j * 4128) for j in range(2)]
    cacc = [at(f"cacc{j}", [P, L], tmp + 8256 + j * 4 * K) for j in range(2)]
    stage = [at(f"stage{j}", [P, L], base + (151 + j * 4) * K) for j in range(2)]
    dt_v = at("dt_v", [P, L], base + 64 * K)
    dt_e = at("dt_e", [P, L], base + 68 * K)
    dt_t = at("dt_t", [P, L], base + 72 * K)
    dt_t2 = at("dt_t2", [P, L], base + 76 * K)
    dt_q = at("dt_q", [P, L], base + 80 * K)
    dt_r = at("dt_r", [P, L], base + 84 * K)
    atok = at("atok", [P, NT, 2, H], base + 88 * K)
    rows = at("rows", [P, NT, CHUNK], base + 90 * K)
    ddif = at("ddif", [P, 2, NT, H], base + 94 * K)
    qs_hi = at("qs_hi", [P, KT, CHUNK], base + 122 * K, F32R)
    qs_lo = at("qs_lo", [P, KT, CHUNK], base + 126 * K, F32R)
    prob = [at(f"prob{j}", [P, QR, 3 * CHUNK], base + (130 + 6 * j) * K) for j in range(2)]
    probT = at("probT", [P, 3, QR * CHUNK], base + 142 * K)
    v_win = at("v_win", [P, 3, kv_dim], base + 148 * K)
    rdiag = at("rdiag", [P, QR, CHUNK], norm_off)
    gated = [at(f"gated{j}", [P, L], off) for j, off in enumerate((norm_a_off, dist_off))]
    s0 = base + 64 * K
    h_back = at("h_back", [P, NT + 1, R * HEAD], s0)
    s1 = s0 + 18 * K
    xin = [at(f"xin{j}", [P, XT, CHUNK], s1 + j * 2 * K) for j in range(2)]
    bin_ = [at(f"bin{j}", [P, CHUNK], s1 + 4 * K + j * 512) for j in range(2)]
    cin = [at(f"cin{j}", [P, CHUNK], s1 + 5 * K + j * 512) for j in range(2)]
    zin = [at(f"zin{j}", [P, XT, CHUNK], s1 + 6 * K + j * 2 * K) for j in range(2)]
    cum_all = at("cum_all", [P, 2, R, CHUNK], base + 151 * K)
    s2 = s1 + 10 * K
    seg = [at(f"seg{j}", [P, 2, R, CHUNK], s2 + j * 8 * K) for j in range(2)]
    cdec = [at(f"cdec{j}", [P, 2, R, CHUNK], s2 + (16 + j * 8) * K) for j in range(2)]
    s3 = s2 + 32 * K
    xtok = [at(f"xtok{j}", [P, R, HEAD], s3 + j * 2 * K) for j in range(2)]
    xdt = [at(f"xdt{j}", [P, 2, R, HEAD], s3 + (4 + j * 4) * K) for j in range(2)]
    xend = [at(f"xend{j}", [P, R, HEAD], s3 + (12 + j * 2) * K) for j in range(2)]
    btok = [at(f"btok{j}", [P, STATE], s3 + 16 * K + j * 512) for j in range(2)]
    gm = [at(f"gm{j}", [P, 2, CHUNK], s3 + 17 * K + j * K) for j in range(2)]
    h_fwd = [at(f"h_fwd{j}", [P, R, HEAD], s3 + (19 + 2 * j) * K) for j in range(2)]
    h_tmp = at("h_tmp", [P, R, HEAD], norm_off + 2 * K)
    ddiag = at("ddiag", [P, XT, P], norm_off)
    hb_now = [at(f"hb_now{j}", [P, R, HEAD], s3 + (23 + j * 2) * K) for j in range(2)]
    y_raw = [at(f"y_raw{j}", [P, L], base + (128 + 4 * j) * K) for j in range(4)]
    y_sq = [at(f"y_sq{j}", [P, L], base + (144 + 4 * j) * K) for j in range(2)]
    y_lo = at("y_lo", [P, NI, L], base, F32R)
    y_hi = at("y_hi", [P, NI, L], base + 64 * K, F32R)
    yscale = at("yscale", [P, L], base + 152 * K)
    mga = at("mga", [P, L], base + 128 * K)
    mat = at("mat", [P, L], base + 132 * K)
    mout = at("mout", [P, L], dist_off)
    mraw = [at(f"mraw{j}", [P, L], base + (64 + 4 * j) * K) for j in range(2)]
    pout = [at(f"pout{j}", [P, L], base + (72 + 4 * j) * K) for j in range(2)]
    nf = [at(f"nf{j}", [P, KT, CHUNK], base + (96 + 4 * j) * K) for j in range(2)]
    nx = [at(f"nx{j}", [P, D], base + (104 + 4 * j) * K) for j in range(2)]
    n1 = [at(f"n1{j}", [P, D], base + (112 + 4 * j) * K) for j in range(2)]
    n2 = [at(f"n2{j}", [P, D], base + (120 + 4 * j) * K) for j in range(2)]
    nj = at("nj", [P, D], base + 128 * K)
    h2_hi = at("h2_hi", [P, KT, L], late, F32R)
    h2_lo = at("h2_lo", [P, KT, L], late + 32 * K, F32R)
    f_act = at("f_act", [P, FT, L], late + 64 * K)
    f_lo = at("f_lo", [P, FT, L], late + 64 * K, F32R)
    f_hi = at("f_hi", [P, FT, HALF], late, F32R)
    fout = [at(f"fout{j}", [P, HALF], late + (44 + 2 * j) * K) for j in range(2)]

    ps = nc.alloc_psum_tensor("ps", [P, 8, 512], F32)

    sems = {}

    def S(name):
        if name not in sems:
            sems[name] = nc.alloc_semaphore(name)
        return sems[name]

    def wait(eng, name, value):
        if not (isinstance(value, int) and value <= 0):
            eng.wait_ge(S(name), value)

    def pairs(eng, n, step, first=0, peel=False):
        if peel:
            step(0, 0)
            step(1, 1)
            first = 2
        turns = (n - first) // 2
        if turns > 0:
            with eng.Fori(0, turns) as i:
                for j in range(2):
                    step(i * 2 + (first + j), (first + j) % 2)
        for t in range(first + 2 * max(turns, 0), n):
            step(t, t % 2)

    def fours(eng, n, step):
        for t in range(4):
            step(t, t)
        with eng.Fori(1, n // 4) as i:
            for j in range(4):
                step(i * 4 + j, j)

    def skewed(eng, n, parts):
        depth = max(lag for _, lag in parts)
        lead = depth + depth % 2
        for s in range(lead):
            for part, lag in parts:
                if 0 <= s - lag < n:
                    part(s - lag, (s - lag) % 2)
        with eng.Fori(0, (n - lead) // 2) as i:
            for j in range(2):
                for part, lag in parts:
                    part(i * 2 + (lead + j - lag), (lead + j - lag) % 2)
        for s in range(n, n + depth):
            for part, lag in parts:
                if s - lag < n:
                    part(s - lag, (s - lag) % 2)

    def pair_of(o):
        return ps[:, 2 * (o % 2):2 * (o % 2) + 2, :]

    block = nc.Block()
    with block:

        @block.sync
        def _(sp):
            def slot_free(v, p):
                wait(sp, "w_lo_done", v - 1)

            def landed(p):
                return S(f"w_landed{p}")

            def w_plain(src, first):
                def load(v, p, t):
                    slot_free(v, p)
                    sp.dma_start(wraw[p][:, 0:KT, :], src[:, :, ds(t * P + first, P)]).then_inc(landed(p), 64)
                return load

            def w_query(v, p, t, half):
                slot_free(v, p)
                for r in range(2):
                    sp.dma_start(wraw[p][:, 0:KT, r * HEAD:(r + 1) * HEAD],
                                 w1[:, :, ds(t * HEAD + (c_q + (2 * half + r) * QR * HEAD), HEAD)]
                                 ).then_inc(landed(p), 32)

            def w_attn(v, p, t):
                slot_free(v, p)
                for r in range(2):
                    for g in range(2):
                        sp.dma_start(wraw[p][r * HEAD:(r + 1) * HEAD, g * QR:(g + 1) * QR, :],
                                     w_at[r, g][:, :, ds(t * P, P)]).then_inc(landed(p), 16)

            def w_ssd_half(v, p, t, j):
                slot_free(v, p)
                sp.dma_start(wraw[p][:, 0:KT, :], w_ssd[:, j, :, ds(t * P, P)]).then_inc(landed(p), 64)

            def w_ffn_part(v, p, t, j):
                slot_free(v, p)
                sp.dma_start(wraw[p][:, 0:FK[j], :], w_f2[:, FK0[j]:FK0[j] + FK[j], ds(t * P, P)]).then_inc(landed(p), 64)

            loads = {
                "dt": lambda v, p, t, j: w_plain(w1, c_dt)(v, p, t),
                "xbc": lambda v, p, t, j: w_plain(w1, c_xbc)(v, p, t),
                "kv": lambda v, p, t, j: w_plain(w1, c_k)(v, p, t),
                "q": None,
                "attn": lambda v, p, t, j: w_attn(v, p, t),
                "mix": lambda v, p, t, j: w_plain(w_mix, 0)(v, p, t),
            }

            def weights(stage_name, lo, hi, extra=None):
                load = loads[stage_name]
                u0 = U0[stage_name]

                def step(t, p):
                    load(t + u0, (p + u0) % 2, t, 0)
                    if extra:
                        extra(t, p)
                pairs(sp, hi, step, first=lo)

            def small(dst, src):
                sp.dma_start(dst, src).then_inc(S("small_landed"), 16)

            weights("dt", 0, 1)
            small(norm_a[:], pre_mix_norm[0:1, :].to_broadcast((P, D)))

            def x_load(t, p):
                wait(sp, "xn_done", t - 1)
                sp.dma_start(x_t[p][:], x_rows[ds(t, 1), :, :].rearrange("t p d -> p (t d)")).then_inc(S(f"tile_landed{p}"), 16)
            for t in range(2):
                x_load(t, t)
            with nc.allow_non_contiguous_dma(reason="a few KB of columns"):
                small(dtb[0:H, :], dt_bias_f.rearrange("a h -> h a"))
                small(dtb[H:2 * H, :], dt_bias_b.rearrange("a h -> h a"))
                small(alog[0:H, :], A_log_f.rearrange("a h -> h a"))
                small(alog[H:2 * H, :], A_log_b.rearrange("a h -> h a"))
                for j in range(taps):
                    small(cw[:, :, j], conv_w[0, j].rearrange("(t p) -> p t", p=P))
                small(cb[:], conv_b[0].rearrange("(t p) -> p t", p=P))
                small(ncol[:], ssd_norm[0].rearrange("(t p) -> p t", p=P))
                for r in range(2):
                    small(dcol[r * HEAD:(r + 1) * HEAD, :],
                          D_skip[0].rearrange("(t r) -> r t", r=2)[r:r + 1, :].to_broadcast((HEAD, NI)))
            small(sink[:], attn_sink[0:1, :].to_broadcast((P, QH)))
            pairs(sp, NT, x_load, first=2)

            weights("xbc", 0, NU["xbc"])
            weights("kv", 0, NU["kv"])
            for half in range(2):
                def query_step(t, p, half=half):
                    v = t + (U0["q"] + half * QR)
                    w_query(v, (p + U0["q"]) % 2, t, half)
                pairs(sp, QR, query_step)

            with sp.Fori(0, NT) as b:
                for j in range(KV):
                    src = w_plain(w1, (c_z if j < 2 else c_gate) + (j % 2) * P)
                    src(b * KV + (U0["zg"] + j), (U0["zg"] + j) % 2, b * 2)

            wait(sp, "cum_stored", 16 * 2 * G)
            wait(sp, "zg_stored0", 16 + 8 * (NI + 2 * KT))
            wait(sp, "zg_stored1", 16 + 8 * (NI + 2 * KT))
            wait(sp, "o_done", KT)
            with sp.Fori(0, G) as g:
                def back_load(i, p):
                    tok = ds(i * -CHUNK + (NT - 1) * CHUNK, CHUNK)
                    sp.wait_ge(S("x_read"), g * (2 * NT) + (i + 1))
                    sp.dma_start(xin[p][:], xbc_d[ds(g * XT, XT), :, tok].rearrange("t p l -> p t l")
                                 ).then_inc(S(f"back_landed{p}"), 16)
                    sp.dma_start(bin_[p][:], xbc_d[ds(g + NI, 1), :, tok].rearrange("t p l -> p (t l)")
                                 ).then_inc(S(f"back_landed{p}"), 16)
                pairs(sp, NT, back_load)
                for j in range(2):
                    w_attn(g * 2 + (U0["attn"] + j), (U0["attn"] + j) % 2, g * 2 + j)
                    sp.wait_ge(S(f"stored{j}"), g * 16 + ST["attn"])
                    sp.dma_start(gated[j][:], gate_d[ds(g * 2 + (KT + j), 1), :, :].rearrange("t p l -> p (t l)")
                                 ).then_inc(S(f"tile_landed{j}"), 16)

                def fwd_load(c, p):
                    n = g * NT + c
                    tok = ds(c * CHUNK, CHUNK)
                    sp.wait_ge(S("c_read_dve"), n + 1)
                    sp.wait_ge(S("c_read_pool"), n + 1)
                    sp.dma_start(cin[p][:], xbc_d[ds(g + (NI + G), 1), :, tok].rearrange("t p l -> p (t l)")
                                 ).then_inc(S(f"fwd_landed{p}"), 16)
                    sp.wait_ge(S("x_read"), g * (2 * NT) + (c + (NT + 1)))
                    sp.dma_start(xin[p][:], xbc_d[ds(g * XT, XT), :, tok].rearrange("t p l -> p t l")
                                 ).then_inc(S(f"fwd_landed{p}"), 16)
                    sp.dma_start(bin_[p][:], xbc_d[ds(g + NI, 1), :, tok].rearrange("t p l -> p (t l)")
                                 ).then_inc(S(f"fwd_landed{p}"), 16)
                    sp.wait_ge(S("seg_exp"), n + 1)
                    sp.wait_ge(S("seg_f_done"), n + 1)
                    sp.wait_ge(S("seg_b_done"), n + 1)
                    sp.dma_start(cum_all[:].rearrange("p d r l -> p (d r l)"),
                                 cum_d[ds(g, 1), ds(c, 1)].rearrange("g c d r l -> (g c) (d r l)").to_broadcast((P, 2 * R * CHUNK))
                                 ).then_inc(S("seg_landed"), 16)

                def z_load(c, p):
                    n = g * NT + c
                    tok = ds(c * CHUNK, CHUNK)
                    sp.wait_ge(S(f"y_stored{p}"), n * 8 + (16 - 8 * p))
                    sp.dma_start(zin[p][:], z_d[ds(g * XT, XT), :, tok].rearrange("t p l -> p t l")
                                 ).then_inc(S(f"z_landed{p}"), 16)
                skewed(sp, NT, [(fwd_load, 0), (z_load, 1)])

            for t in range(2):
                w_ssd_half(U0["ssd"] + t, (U0["ssd"] + t) % 2, 0, t)
            for j in range(2):
                wait(sp, f"y_stored{j}", 16 + 8 * G * NT)
                wait(sp, f"stored{j}", ST["attn end"])
            wait(sp, "h_fwd_done", G * NT)

            def y_load(t, q):
                wait(sp, "y_lo_done", t - 3)
                wait(sp, "y_squared", t - 3)
                sp.dma_start(y_raw[q][:], y_d[ds(t, 1), :, :].rearrange("t p l -> p (t l)")).then_inc(S(f"y_landed{q}"), 16)
            fours(sp, NI, y_load)
            wait(sp, "y_lo_done", NI)
            wait(sp, "y_squared", NI)

            def merge_load(t):
                wait(sp, "merge_out", t)
                sp.dma_start(mga[:], gate_d[ds(t, 1), :, :].rearrange("t p l -> p (t l)")).then_inc(S("merge_landed"), 16)
                sp.dma_start(mat[:], attn_d[ds(t, 1), :, :].rearrange("t p l -> p (t l)")).then_inc(S("merge_landed"), 16)
            merge_load(0)
            with sp.Fori(1, KT) as t:
                for j in range(2):
                    w_ssd_half(t * 2 + (U0["ssd"] + j), (U0["ssd"] + j) % 2, t, j)
                merge_load(t)
            weights("mix", 0, 2)

            def mix_load(t, p):
                wait(sp, "mix_lo_done", t - 1)
                sp.dma_start(mraw[p][:], mix_d[ds(t, 1), :, :].rearrange("t p l -> p (t l)")).then_inc(S(f"tile_landed{p}"), 16)
            wait(sp, "mm_done", U0["mix"])
            wait(sp, "mix_stored", 16 * KT)
            pairs(sp, KT, mix_load, peel=True)
            weights("mix", 2, KT)

            def ffn_in_weights(v, p, t, j):
                w_plain(w_f1, j * F)(v, p, t)
            for j in range(2):
                ffn_in_weights(U0["ffn_in"] + j, (U0["ffn_in"] + j) % 2, 0, j)

            def norm_load(src, add, n0):
                def load(t, p):
                    wait(sp, "n_turned", t + (n0 - 1))
                    sp.dma_start(nf[p][:], src[:, :, ds(t * CHUNK, CHUNK)]).then_inc(S(f"n_f_landed{p}"), 16)
                    wait(sp, "n_added", t + (n0 - 1))
                    if n0:
                        wait(sp, "stored0", ST["x1 end"])
                        wait(sp, "stored1", ST["x1 end"])
                    sp.dma_start(nx[p][:], add[ds(t, 1), :, :].rearrange("t p d -> p (t d)")).then_inc(S(f"n_x_landed{p}"), 16)
                return load
            sp.dma_start(norm_a[:], post_mix_norm[0:1, :].to_broadcast((P, D))).then_inc(S("norm2_landed"), 16)
            sp.dma_start(norm_b[:], pre_ffn_norm[0:1, :].to_broadcast((P, D))).then_inc(S("norm2_landed"), 16)
            wait(sp, "stored0", ST["proj end"])
            wait(sp, "stored1", ST["proj end"])
            pairs(sp, NT, norm_load(proj_d, x_rows, 0), peel=True)

            def ffn_pair(t, last):
                for j in range(2):
                    ffn_in_weights(t * 2 + (U0["ffn_in"] + j), (U0["ffn_in"] + j) % 2, t, j)
            with sp.Fori(1, FT) as t:
                ffn_pair(t, False)
            for half in range(2):
                def ffn_out_weights(t, p, half=half):
                    for j in range(3):
                        w_ffn_part(t * 3 + (U0["ffn_out"] + 3 * KT * half + j), (U0["ffn_out"] + p + j) % 2, t, j)
                pairs(sp, KT, ffn_out_weights)

            sp.dma_start(norm_a[:], post_ffn_norm[0:1, :].to_broadcast((P, D))).then_inc(S("norm3_landed"), 16)
            wait(sp, "mm_done", ALL_UNITS)
            wait(sp, "stored0", ST["ffn end"])
            wait(sp, "stored1", ST["ffn end"])
            pairs(sp, NT, norm_load(ffn_d, x1_d, NT))

        @block.gpsimd
        def _(pool):
            gp = nc.gpsimd
            pool.sem_inc(S("c_read_pool"), 2)
            pool.sem_inc(S("seg_b_done"), 1)
            pool.sem_inc(S("xdt_done"), 3)
            one = pool.to_reg(1.0)
            zero = pool.to_reg(0.0)
            masked = pool.to_reg(MASKED)

            def step(ins):
                step.n += 1
                ins.then_inc(S("const_step"), 1)
                pool.wait_ge(S("const_step"), step.n)
            step.n = 0
            gp.memset(ones[:], 1.0).then_inc(S("const_step"), 1)
            gp.memset(ident[:], 0.0).then_inc(S("const_step"), 1)
            step.n = 2
            pool.wait_ge(S("const_step"), 2)
            step(gp.affine_select(out=ident[:], in_=ident[:], pattern=[[-1, P]], compare_op=ALU.not_equal, fill=one,
                                  base=0, channel_multiplier=1))
            step(gp.affine_select(out=tri[:, 0, :], in_=ones[:], pattern=[[1, P]], compare_op=ALU.is_ge, fill=zero,
                                  base=0, channel_multiplier=-1))
            step(gp.affine_select(out=tri[:, 1, :], in_=ones[:], pattern=[[-1, P]], compare_op=ALU.is_ge, fill=zero,
                                  base=0, channel_multiplier=1))
            W3 = 3 * CHUNK
            for v in range(3):
                step(gp.iota(dist[:, v, :], pattern=[[-1, W3]], base=CHUNK, channel_multiplier=1,
                             allow_small_or_imprecise_dtypes=True))
            gp.memset(k_all[:, :, 0:CHUNK], 0.0).then_inc(S("pads_done"), 1)
            gp.memset(k_all[:, :, L + CHUNK:kwin], 0.0).then_inc(S("pads_done"), 1)
            gp.memset(v_all[:, 0, :], 0.0).then_inc(S("pads_done"), 1)
            gp.memset(v_all[:, NT + 1, :], 0.0).then_inc(S("pads_done"), 1)
            pool.wait_ge(S("dist_negated"), 1)
            for v in range(3):
                step(gp.affine_select(out=dist[:, v, :], in_=dist[:, v, :], pattern=[[1, W3]], compare_op=ALU.is_ge,
                                      fill=masked, base=WINDOW - CHUNK, channel_multiplier=-1))
                step(gp.affine_select(out=dist[:, v, :], in_=dist[:, v, :], pattern=[[-1, W3]], compare_op=ALU.is_ge,
                                      fill=masked, base=WINDOW + CHUNK, channel_multiplier=1))
            step(gp.affine_select(out=dist[:, 0, :], in_=dist[:, 0, :], pattern=[[1, W3]], compare_op=ALU.is_ge,
                                  fill=masked, base=-CHUNK, channel_multiplier=0))
            gp.affine_select(out=dist[:, 2, :], in_=dist[:, 2, :], pattern=[[-1, W3]], compare_op=ALU.is_ge,
                             fill=masked, base=2 * CHUNK - 1, channel_multiplier=0).then_inc(S("dist_done"), 1)

            pool.wait_ge(S("rows_done"), 2)
            for d in range(2):
                for g in range(G):
                    pool.dma_start(cum_d[g, :, d, :, :].rearrange("c r l -> r c l"),
                                   rows[d * H + g * R:d * H + (g + 1) * R, :, :]).then_inc(S("cum_stored"), 16)

            def store(dst, buf, done, n0=0):
                def s(t, p):
                    pool.wait_ge(S(done), t + (n0 + 1))
                    pool.dma_start(dst(t), buf[p][:]).then_inc(S(f"stored{p}"), 16)
                return s

            def tile_of(d):
                return lambda t: d[ds(t, 1), :, :].rearrange("t p l -> p (t l)")
            pairs(pool, conv_dim // P, store(tile_of(xbc_d), stage, "xbc_out"))

            def diagonals(b, j):
                pool.wait_ge(S("rden_done"), b * KV + (j + 1))
                pool.wait_ge(S("p_turned"), b * KV + (j + 1))
                gp.tensor_tensor(rdiag[:], ident[:].unsqueeze(1).to_broadcast((P, QR, CHUNK)),
                                 soft[:, j % 2, 4, :].unsqueeze(2).to_broadcast((P, QR, CHUNK)), ALU.mult
                                 ).then_inc(S("rdiag_done"), 1)

            def attn_block(b):
                diagonals(b, 0)
                wait(pool, "pv_done", b * KV)
                gp.tensor_copy(v_win[:], v_all[:, ds(b, 3), :]).then_inc(S("v_win_done"), 1)
                for j in range(1, KV):
                    diagonals(b, j)
            pool.wait_ge(S("pads_done"), 4)
            pool.wait_ge(S("v_turned"), NT)
            attn_block(0)
            with pool.Fori(1, NT) as b:
                attn_block(b)

            def heads(tab, d, c, g):
                return tab[:, d, ds(c, 1), ds(g * R, R)].rearrange("p c r -> p (c r)")

            def wide(ap, n):
                return ap.unsqueeze(2).to_broadcast((P, R, n))
            pool.wait_ge(S("o_done"), KT)
            gp.memset(h_back[:, NT, :], 0.0).then_inc(S("h_zero"), 1)
            pool.wait_ge(S("h_zero"), 1)
            with pool.Fori(0, G) as g:
                def back(i, p):
                    m = g * NT + i
                    c = i * -1 + (NT - 1)
                    pool.wait_ge(S("h_fwd_done"), g * NT)
                    pool.wait_ge(S("h_back_done"), m)
                    gp.tensor_tensor(h_tmp[:], h_back[:, ds(c + 1, 1), :].rearrange("p c (r e) -> p (c r) e", e=HEAD),
                                     wide(heads(dec, 1, c, g), HEAD), ALU.mult).then_inc(S("h_decayed"), 1)
                pairs(pool, NT, back)

                def fwd_a(c, p):
                    n = g * NT + c
                    pool.wait_ge(S("y_done"), n + 1)
                    pool.wait_ge(S("seg_landed"), n * 16 + 16)
                    gp.tensor_tensor(seg[p][:, 1, :, :], cum_all[:, 1, :, :], wide(heads(acum, 1, c, g), CHUNK), ALU.subtract
                                     ).then_inc(S("seg_b_done"), 1)
                    pool.wait_ge(S(f"fwd_landed{p}"), g * (48 * NT // 2) + (c * 24 + (48 - 24 * p)))
                    pool.wait_ge(S("seg_exp"), n + 2)
                    gp.tensor_tensor(cdec[p][:, 1, :, :], cdec[p][:, 1, :, :], cin[p][:].unsqueeze(1).to_broadcast((P, R, CHUNK)),
                                     ALU.mult).then_inc(S("c_read_pool"), 1)
                    pool.wait_ge(S("xtok_done"), n + 1)
                    for d in range(2):
                        gp.tensor_tensor(xdt[p][:, d, :, :], xtok[p][:], wide(heads(dtok, d, c, g), HEAD), ALU.mult
                                         ).then_inc(S("xdt_done"), 1)
                    gp.tensor_tensor(xend[p][:], xtok[p][:], wide(heads(wend, 0, c, g), HEAD), ALU.mult
                                     ).then_inc(S("xdt_done"), 1)
                pairs(pool, NT, fwd_a)
                for j in range(2):
                    pool.wait_ge(S("attn_gated"), g * 2 + (j + 2))
                    pool.dma_start(attn_d[ds(g * 2 + j, 1), :, :].rearrange("t p l -> p (t l)"), gated[j][:]
                                   ).then_inc(S(f"stored{j}"), 16)

            with pool.Fori(0, KT) as t:
                pool.wait_ge(S("merge_out"), t + 1)
                pool.dma_start(mix_d[ds(t, 1), :, :].rearrange("t p l -> p (t l)"), mout[:]).then_inc(S("mix_stored"), 16)
            pairs(pool, KT, store(lambda t: proj_d[:, ds(t, 1), :].rearrange("p t l -> p (t l)"), pout, "proj_out"))
            pairs(pool, NT, store(lambda t: x1_d[ds(t, 1), :, :].rearrange("t p d -> p (t d)"), n1, "n_added"))
            for half in range(2):
                def ffn_store(t, p, half=half):
                    pool.wait_ge(S("ffn_out_done"), t + (half * KT + 1))
                    pool.dma_start(ffn_d[:, ds(t, 1), half * HALF:(half + 1) * HALF].rearrange("p t l -> p (t l)"),
                                   fout[p][:]).then_inc(S(f"stored{p}"), 16)
                pairs(pool, KT, ffn_store)

            def result(t, p):
                pool.wait_ge(S("n_added"), t + (NT + 1))
                pool.dma_start(out_rows[ds(t, 1), :, :].rearrange("t p d -> p (t d)"), n1[p][:]).then_inc(S(f"stored{p}"), 16)
            pairs(pool, NT, result)
            pool.wait_ge(S("stored0"), ST["out end"])
            pool.wait_ge(S("stored1"), ST["out end"])

        @block.scalar
        def _(act):
            sc = nc.scalar

            def w_hi(v, p, kt=KT):
                act.wait_ge(S(f"w_landed{p}"), (v - p) * 32 + 64)
                wait(act, "mm_done", v - 1)
                sc.copy(whi[p][:, 0:kt, :], wraw[p][:, 0:kt, :]).then_inc(S("w_hi_done"), 1)

            def ahead(name, work, n=None, first=0):
                u0 = U0[name]

                def step(t, p):
                    w_hi(t + (u0 + 1), (p + u0 + 1) % 2)
                    work(t, p)
                pairs(act, NU[name] if n is None else n, step, first=first)

            def unit_done(name, t, per=1):
                act.wait_ge(S("mm_done"), t * per + (U0[name] + per))

            def out_ps(name, p):
                return pair_of(O0[name] + p)

            act.sem_inc(S("pT_done"), 1)
            act.sem_inc(S("seg_exp"), 1)
            w_hi(0, 0)

            def sq_x(t, p):
                act.wait_ge(S(f"tile_landed{p}"), (t - p) * 8 + 16)
                sc.activation(junk[:], x_t[p][:], ACT.Square, accum_out=stat[:, p, 0:1]).then_inc(S("n_squared"), 1)
                act.wait_ge(S("n_mean"), t + 1)
                sc.activation(stat[:, p, 2:3], stat[:, p, 1:2], ACT.Sqrt).then_inc(S("n_root"), 1)

            def hi_h(t, p):
                act.wait_ge(S("x_turned"), t + 1)
                sc.copy(act_hi[:, :, ds(t * CHUNK, CHUNK)],
                        ps[:, 2 * p:2 * p + 2, :].rearrange("p a (b l) -> p (a b) l", l=CHUNK)).then_inc(S("h_hi_done"), 1)
            skewed(act, NT, [(sq_x, 0), (hi_h, 1)])

            HH = 2 * H
            w_hi(1, 1)
            act.wait_ge(S("small_landed"), 16 * (1 + 4 + taps + 2 + 2 + 1))
            act.wait_ge(S("mm_done"), 1)
            sc.activation(dt_v[0:HH, :], ps[0:HH, 0:2, :].rearrange("p a l -> p (a l)"), ACT.Identity, bias=dtb[0:HH, :]
                          ).then_inc(S("moved"), 1)
            sc.activation(alog[0:HH, :], alog[0:HH, :], ACT.Exp).then_inc(S("dt_act"), 1)
            act.wait_ge(S("dt_dve"), 1)
            sc.activation(dt_e[0:HH, :], dt_e[0:HH, :], ACT.Exp).then_inc(S("dt_act"), 1)
            act.wait_ge(S("dt_turned"), 1)
            sc.copy(dtok[:], ps[:, 4, :].rearrange("p (c d h) -> p d c h", c=NT, d=2)).then_inc(S("dt_tok"), 1)
            sc.copy(atok[:].rearrange("p c d h -> p (c d h)"), ps[:, 5, :]).then_inc(S("dt_tok"), 1)
            act.wait_ge(S("dt_summed"), 1)
            sc.copy(acum[:].rearrange("p d c h -> p (d c h)"), ps[:, 6, :]).then_inc(S("acum_done"), 1)
            act.wait_ge(S("dt_dve_tok"), 1)
            sc.activation(dec[:].rearrange("p d c h -> p (d c h)"), ps[:, 7, :], ACT.Exp).then_inc(S("tables_done"), 1)
            sc.activation(wend[:].rearrange("p d c h -> p (d c h)"), ddif[:].rearrange("p d c h -> p (d c h)"), ACT.Exp
                          ).then_inc(S("tables_done"), 1)
            act.wait_ge(S("rows_summed"), 1)
            psr = ps[:, 4:8, :].rearrange("p a (c d l) -> p (a c) d l", d=2, l=CHUNK)
            for d in range(2):
                sc.copy(rows[d * H:(d + 1) * H, :, :], psr[d * H:(d + 1) * H, :, d, :]).then_inc(S("rows_done"), 1)

            NX = conv_dim // P

            def xbc_raw(t, p):
                w_hi(t + (U0["xbc"] + 1), (p + U0["xbc"] + 1) % 2)
                unit_done("xbc", t)
                wait(act, "conv_done", t - 1)
                sc.copy(praw[p][:, pad:pad + L], out_ps("xbc", p).rearrange("p a l -> p (a l)")).then_inc(S("moved"), 1)

            def xbc_silu(t, p):
                act.wait_ge(S("conv_done"), t + 1)
                wait(act, f"stored{p}", (t - p) * 8)
                sc.activation(stage[p][:], cacc[p][:], ACT.Silu).then_inc(S("xbc_out"), 1)
            act.wait_ge(S("praw_zeroed"), 4)
            skewed(act, NX, [(xbc_raw, 0), (xbc_silu, 1)])

            for t in range(KV):
                w_hi(t + U0["kv"] + 1, (t + U0["kv"] + 1) % 2)
                unit_done("kv", t)
                if t < KV // 2:
                    sc.copy(k_all[:, t, CHUNK:CHUNK + L], out_ps("kv", t % 2).rearrange("p a l -> p (a l)")
                            ).then_inc(S("moved"), 1)
                else:
                    if t == KV // 2:
                        act.wait_ge(S("stored0"), ST["xbc end"])
                        act.wait_ge(S("stored1"), ST["xbc end"])
                    sc.copy(stage[t % 2][:], out_ps("kv", t % 2).rearrange("p a l -> p (a l)")).then_inc(S("moved"), 1)

            def q_work(t, p):
                unit_done("q", t)
                sc.copy(qT[:, ds(t, 1), :].rearrange("p t l -> p (t l)"),
                        out_ps("q", p).rearrange("p a l -> p (a l)")).then_inc(S("moved"), 1)
            act.wait_ge(S("cum_stored"), 16 * 2 * G)
            ahead("q", q_work)

            def zg_unit(b, j):
                t = b * KV + j
                p = j % 2
                act.wait_ge(S("mm_done"), t + (U0["zg"] + 1))
                act.wait_ge(S(f"zg_stored{p}"), (t - p) * 8 + 16)
                sc.activation(stage[p][:], ps[:, 0:2, :].rearrange("p a l -> p (a l)"), ACT.Silu if j < 2 else ACT.Sigmoid
                              ).then_inc(S("moved"), 1)
                act.wait_ge(S("moved"), t + (O0["zg"] + 1))
                act.dma_start((z_d if j < 2 else gate_d)[ds(b * 2 + p, 1), :, :].rearrange("t p l -> p (t l)"), stage[p][:]
                              ).then_inc(S(f"zg_stored{p}"), 16)

            def stage_q(b):
                wait(act, "scored", b * QH)
                sc.copy(qs_hi[:], qT[:, :, ds(b * CHUNK, CHUNK)]).then_inc(S("qs_hi_done"), 1)
                sc.copy(k_hi[:], k_all[:, :, ds(b * CHUNK, 3 * CHUNK)]).then_inc(S("qs_hi_done"), 1)

            def exps(b, j):
                q = j % 2
                act.wait_ge(S("max_done"), b * KV + (j + 1))
                for r in range(QR):
                    sc.activation(prob[q][:, r, :], prob[q][:, r, :], ACT.Exp, bias=soft[:, q, 2, r:r + 1], scale=SCALE,
                                  accum_out=soft[:, q, 3, r:r + 1]).then_inc(S("exp_done"), 1)
                sc.activation(soft[:, q, 5, :], soft[:, q, 5, :], ACT.Exp).then_inc(S("exp_done"), 1)

            def move_pT(b, j):
                act.wait_ge(S("p_turned"), b * KV + (j + 2))
                act.wait_ge(S("pv_done"), b * KV + j)
                sc.copy(probT[:], ps[:, 4:7, :]).then_inc(S("pT_done"), 1)

            act.wait_ge(S("moved"), O0["zg"])
            act.wait_ge(S("v_turned"), NT)
            for j in range(2):
                act.sem_inc(S(f"zg_stored{j}"), 16)
            stage_q(0)
            exps(0, 0)

            def act_block(b, last=False):
                for j in range(KV):
                    if not (last and j == KV - 1):
                        w_hi(b * KV + (U0["zg"] + j + 1), (U0["zg"] + j + 1) % 2)
                    if j == 2 and not last:
                        stage_q(b + 1)
                    if j < KV - 1:
                        exps(b, j + 1)
                    elif not last:
                        exps(b + 1, 0)
                    move_pT(b, j)
                    zg_unit(b, j)
            with act.Fori(0, NT - 1) as b:
                act_block(b)
            act_block(NT - 1, True)

            act.wait_ge(S("o_moved"), 2 * NT + 1)
            act.wait_ge(S("pv_done"), KV * NT)

            def o_hi(t, p):
                sc.copy(act_hi[:, ds(t, 1), :], qT[:, ds(t, 1), :]).then_inc(S("o_hi_done"), 1)
            pairs(act, KT, o_hi)

            act.wait_ge(S("o_done"), KT)
            for j in range(2):
                act.sem_inc(S(f"y_stored{j}"), 16)
            with act.Fori(0, G) as g:
                act.wait_ge(S("y_done"), g * NT + 2)

                def back(i, p):
                    m = g * NT + i
                    act.wait_ge(S("x_read"), g * (2 * NT) + (i + 3))
                    act.wait_ge(S("back_state"), m + 1)
                    sc.copy(btok[p][:], ps[:, 1, 0:STATE]).then_inc(S("back_btok"), 1)
                pairs(act, NT, back)
                for j in range(2):
                    w_hi(g * 2 + (U0["attn"] + j), (U0["attn"] + j) % 2)

                def fwd_exp(c, p):
                    n = g * NT + c
                    act.wait_ge(S("seg_landed"), n * 16 + 16)
                    act.wait_ge(S("y_done"), n + 1)
                    sc.activation(cdec[p][:].rearrange("p d r l -> p (d r l)"), cum_all[:].rearrange("p d r l -> p (d r l)"),
                                  ACT.Exp).then_inc(S("seg_exp"), 1)
                    act.wait_ge(S("fwd_turned"), n + 1)
                    act.wait_ge(S("h_back_done"), g * NT + NT)
                    act.wait_ge(S("xdt_done"), g * (3 * NT) + c * 3)
                    sc.copy(xtok[p][:].rearrange("p r e -> p (r e)"), ps[:, 0, :]).then_inc(S("xtok_done"), 1)
                    act.wait_ge(S("fwd_state"), n + 1)
                    sc.copy(btok[p][:], ps[:, 1, 0:STATE]).then_inc(S("fwd_btok"), 1)
                    sc.copy(hb_now[p][:].rearrange("p r e -> p (r e)"),
                            h_back[:, ds(c + 1, 1), :].rearrange("p c e -> p (c e)")).then_inc(S("hb_done"), 1)

                def fwd_mask(c, p):
                    n = g * NT + c
                    act.wait_ge(S("arg_done"), n + 1)
                    sc.activation(seg[p][:, 0, :, :], seg[p][:, 0, :, :], ACT.Exp).then_inc(S("decay_done"), 1)

                def y_store(c, p):
                    n = g * NT + c
                    act.wait_ge(S("y_gated"), n + 3)
                    act.dma_start(y_d[ds(g * XT, XT), :, ds(c * CHUNK, CHUNK)].rearrange("t p l -> p t l"), zin[p][:]
                                  ).then_inc(S(f"y_stored{p}"), 16)
                skewed(act, NT, [(y_store, 3), (fwd_mask, 1), (fwd_exp, 0)])
            w_hi(U0["ssd"], U0["ssd"] % 2)
            w_hi(U0["ssd"] + 1, (U0["ssd"] + 1) % 2)

            act.wait_ge(S("y_gated"), G * NT + 2)
            act.wait_ge(S("y_done"), G * NT + 2)
            act.wait_ge(S("h_fwd_done"), G * NT)
            act.wait_ge(S("attn_gated"), KT + 1)

            def y_hi_step(t, q):
                act.wait_ge(S(f"y_landed{q}"), (t - q) * 4 + 16)
                sc.activation(y_hi[:, ds(t, 1), :].rearrange("p t l -> p (t l)"), y_raw[q][:], ACT.Copy,
                              scale=ncol[:, ds(t, 1)]).then_inc(S("y_hi_done"), 1)
                wait(act, "sq_summed", t - 1)
                sc.activation(y_sq[q % 2][:], y_raw[q][:], ACT.Square).then_inc(S("y_squared"), 1)
            fours(act, NI, y_hi_step)
            act.wait_ge(S("sq_mean"), 1)
            sc.activation(yscale[:], yscale[:], ACT.Sqrt).then_inc(S("y_root"), 1)
            with act.Fori(0, KT) as t:
                w_hi(t * 2 + (U0["ssd"] + 2), U0["ssd"] % 2)
                w_hi(t * 2 + (U0["ssd"] + 3), (U0["ssd"] + 1) % 2)

            def m_hi(t, p):
                act.wait_ge(S(f"tile_landed{p}"), (t - p) * 8 + (8 * (NT + KT) + 16))
                sc.copy(act_hi[:, ds(t, 1), :].rearrange("p t l -> p (t l)"), mraw[p][:]).then_inc(S("mix_hi_done"), 1)
            pairs(act, KT, m_hi)

            def p_work(t, p):
                unit_done("mix", t)
                wait(act, f"stored{p}", (t - p) * 8 + ST["proj"])
                sc.copy(pout[p][:], out_ps("mix", p).rearrange("p a l -> p (a l)")).then_inc(S("proj_out"), 1)

            def p_step(t, p):
                w_hi(t + (U0["mix"] + 2), (p + U0["mix"]) % 2)
                p_work(t, p)
            pairs(act, KT - 1 - (KT - 1) % 2, p_step)
            w_hi(KT - 2 + U0["mix"] + 2, (KT - 2 + U0["mix"]) % 2)
            p_work(KT - 2, 0)
            p_work(KT - 1, 1)

            def n_a(n0):
                def part(t, p):
                    act.wait_ge(S("n_turned"), t + (n0 + 1))
                    sc.activation(nj[:], ps[:, 2 * p:2 * p + 2, :].rearrange("p a l -> p (a l)"), ACT.Square,
                                  accum_out=stat[:, p, 0:1]).then_inc(S("n_squared"), 1)
                    act.wait_ge(S("n_mean"), t + (n0 + NT + 1))
                    sc.activation(stat[:, p, 2:3], stat[:, p, 1:2], ACT.Sqrt).then_inc(S("n_root"), 1)
                return part

            def n_b(t, p):
                act.wait_ge(S("n_added"), t + 1)
                sc.activation(nj[:], n1[p][:], ACT.Square, accum_out=stat[:, p, 4:5]).then_inc(S("n2_squared_b"), 1)
                act.wait_ge(S("n2_mean_b"), t + 1)
                sc.activation(stat[:, p, 6:7], stat[:, p, 5:6], ACT.Sqrt).then_inc(S("n2_root_b"), 1)

            def n_c(t, p):
                act.wait_ge(S("h2_turned"), t + 1)
                sc.copy(h2_hi[:, :, ds(t * CHUNK, CHUNK)],
                        ps[:, 4 + 2 * p:6 + 2 * p, :].rearrange("p a (b l) -> p (a b) l", l=CHUNK)
                        ).then_inc(S("h2_hi_done"), 1)
            skewed(act, NT, [(n_a(0), 0), (n_b, 1), (n_c, 2)])

            def f_step(t, last=False):
                wait(act, "gact_read", t)
                act.wait_ge(S("mm_done"), t * 2 + (U0["ffn_in"] + 1))
                sc.activation(gact[:], pair_of(O0["ffn_in"]).rearrange("p a l -> p (a l)"), ACT.Silu).then_inc(S("g_done"), 1)

            w_hi(U0["ffn_in"] + 1, (U0["ffn_in"] + 1) % 2)
            with act.Fori(0, FT - 1) as t:
                f_step(t)
                w_hi(t * 2 + (U0["ffn_in"] + 2), U0["ffn_in"] % 2)
                w_hi(t * 2 + (U0["ffn_in"] + 3), (U0["ffn_in"] + 1) % 2)
            f_step(FT - 1)
            w_hi(U0["ffn_out"], U0["ffn_out"] % 2, FK[0])
            w_hi(U0["ffn_out"] + 1, (U0["ffn_out"] + 1) % 2, FK[1])
            act.wait_ge(S("mm_done"), U0["ffn_out"])
            act.wait_ge(S("gact_read"), FT)
            for half in range(2):
                if half:
                    act.wait_ge(S("mm_done"), U0["ffn_out"] + 3 * KT)
                with act.Fori(0, FT) as k:
                    sc.copy(f_hi[:, ds(k, 1), :].rearrange("p t l -> p (t l)"),
                            f_act[:, ds(k, 1), half * HALF:(half + 1) * HALF].rearrange("p t l -> p (t l)")
                            ).then_inc(S("f_hi_done"), 1)

                def ffn_work(t, p, half=half):
                    act.wait_ge(S("mm_done"), t * 3 + (U0["ffn_out"] + 3 * KT * half + 3))
                    wait(act, f"stored{p}", (t - p) * 8 + (ST["ffn"] + 8 * KT * half))
                    sc.copy(fout[p][:], ps[:, 2 * ((O0["ffn_out"] + p) % 2), :]).then_inc(S("ffn_out_done"), 1)

                def ffn_hi(t, p, j, half=half):
                    w_hi(t * 3 + (U0["ffn_out"] + 3 * KT * half + j), (U0["ffn_out"] + p + j) % 2, FK[j % 3])

                def ffn_step(t, p, last=False):
                    ffn_hi(t, p, 2)
                    if not last:
                        ffn_hi(t, p, 3)
                    ffn_work(t, p)
                    if not last:
                        ffn_hi(t, p, 4)
                if half == 0:
                    pairs(act, KT, ffn_step)
                else:
                    pairs(act, KT - 2, ffn_step)
                    ffn_step(KT - 2, 0)
                    ffn_step(KT - 1, 1, last=True)
            skewed(act, NT, [(n_a(NT), 0)])

        @block.vector
        def _(dve):
            ve = nc.vector
            dve.sem_inc(S("c_read_dve"), 2)
            dve.sem_inc(S("y_gated"), 2)
            dve.sem_inc(S("seg_f_done"), 1)
            dve.sem_inc(S("o_moved"), 1)
            dve.sem_inc(S("attn_gated"), 1)

            def w_low(v, p, kt=KT):
                dve.wait_ge(S("w_hi_done"), v + 1)
                ve.tensor_tensor(wlo[p][:, 0:kt, :], wraw[p][:, 0:kt, :], whi[p][:, 0:kt, :].bitcast(F32), ALU.subtract
                                 ).then_inc(S("w_lo_done"), 1)

            def ahead(name, work, n=None, first=0):
                u0 = U0[name]

                def step(t, p):
                    w_low(t + (u0 + 1), (p + u0 + 1) % 2)
                    work(t, p)
                pairs(dve, NU[name] if n is None else n, step, first=first)

            def out_ps(name, p):
                return pair_of(O0[name] + p)

            w_low(0, 0)

            dve.wait_ge(S("small_landed"), 16 * (1 + 4 + taps + 2 + 2 + 1))

            def mean(dst, src, done):
                ve.tensor_scalar(dst, src, 1.0 / D, EPS, ALU.mult, ALU.add).then_inc(S(done), 1)

            def x_norm(t, p):
                dve.wait_ge(S("n_squared"), t + 1)
                mean(stat[:, p, 1:2], stat[:, p, 0:1], "n_mean")
                dve.wait_ge(S("n_root"), t + 1)
                ve.reciprocal(stat[:, p, 3:4], stat[:, p, 2:3]).then_inc(S("n_rstd"), 1)
                dve.wait_ge(S("n_rstd"), t + 1)
                wait(dve, "x_turned", t - 1)
                ve.scalar_tensor_tensor(x_n[p][:], x_t[p][:], stat[:, p, 3:4], norm_a[:], ALU.mult, ALU.mult
                                        ).then_inc(S("xn_done"), 1)

            def h_low(t, p):
                dve.wait_ge(S("h_hi_done"), t + 1)
                cols = ds(t * CHUNK, CHUNK)
                ve.tensor_tensor(act_lo[:, :, cols], ps[:, 2 * p:2 * p + 2, :].rearrange("p a (b l) -> p (a b) l", l=CHUNK),
                                 act_hi[:, :, cols].bitcast(F32), ALU.subtract).then_inc(S("h_done"), 1)
            skewed(dve, NT, [(x_norm, 0), (h_low, 1)])

            HH = 2 * H
            w_low(1, 1)
            count = [0]

            def link(ins):
                count[0] += 1
                ins.then_inc(S("dt_dve"), 1)
                dve.wait_ge(S("dt_dve"), count[0])
            for j in range(2):
                ve.memset(praw[j][:, 0:pad], 0.0).then_inc(S("praw_zeroed"), 1)
                ve.memset(praw[j][:, pad + L:], 0.0).then_inc(S("praw_zeroed"), 1)
            dve.wait_ge(S("moved"), 1)
            v_, e_, t_, t2_, q_, r_ = (a[0:HH, :] for a in (dt_v, dt_e, dt_t, dt_t2, dt_q, dt_r))
            link(ve.scalar_tensor_tensor(e_, v_, -1.0, v_, ALU.mult, ALU.min))
            dve.wait_ge(S("dt_act"), 2)
            link(ve.tensor_scalar(r_, e_, 2.0, None, ALU.add))
            link(ve.reciprocal(q_, r_))
            link(ve.tensor_tensor(t_, e_, q_, ALU.mult))
            link(ve.tensor_tensor(t2_, t_, t_, ALU.mult))
            link(ve.tensor_scalar(q_, t2_, 1.0 / (2 * LOG1P_TERMS + 1), None, ALU.mult))
            for k in range(LOG1P_TERMS - 1, 0, -1):
                link(ve.scalar_tensor_tensor(q_, q_, 1.0 / (2 * k + 1), t2_, ALU.add, ALU.mult))
            link(ve.scalar_tensor_tensor(q_, q_, 1.0, t_, ALU.add, ALU.mult))
            link(ve.tensor_scalar(r_, v_, 0.0, None, ALU.max))
            link(ve.scalar_tensor_tensor(v_, q_, 2.0, r_, ALU.mult, ALU.add))
            ve.tensor_scalar(e_, v_, alog[0:HH, :], -1.0, ALU.mult, ALU.mult).then_inc(S("dt_ready"), 1)
            dve.wait_ge(S("const_step"), 8)
            ve.scalar_tensor_tensor(dist[:].rearrange("p v k -> p (v k)"), dist[:].rearrange("p v k -> p (v k)"), -1.0,
                                    dist[:].rearrange("p v k -> p (v k)"), ALU.mult, ALU.min).then_inc(S("dist_negated"), 1)
            dve.wait_ge(S("acum_done"), 1)
            flat = "p d c h -> p (d c h)"
            ve.tensor_tensor(ddif[:].rearrange(flat), ps[:, 7, :], acum[:].rearrange(flat), ALU.subtract
                             ).then_inc(S("dt_dve_tok"), 1)
            dve.wait_ge(S("tables_done"), 2)
            ve.tensor_tensor(wend[:].rearrange(flat), wend[:].rearrange(flat), dtok[:].rearrange(flat), ALU.mult
                             ).then_inc(S("wend_done"), 1)

            NX = conv_dim // P

            def conv_w_ahead(t, p):
                w_low(t + (U0["xbc"] + 1), (p + U0["xbc"] + 1) % 2)

            def conv(t, p):
                dve.wait_ge(S("moved"), t + 2)
                wait(dve, "xbc_out", t - 1)
                ve.tensor_scalar(cacc[p][:], praw[p][:, 0:L], cw[:, ds(t, 1), 0:1].rearrange("p t a -> p (t a)"),
                                 cb[:, ds(t, 1)], ALU.mult, ALU.add).then_inc(S("conv_step"), 1)
                for j in range(1, taps):
                    dve.wait_ge(S("conv_step"), t * (taps - 1) + j)
                    ins = ve.scalar_tensor_tensor(cacc[p][:], praw[p][:, j:j + L],
                                                  cw[:, ds(t, 1), j:j + 1].rearrange("p t a -> p (t a)"), cacc[p][:],
                                                  ALU.mult, ALU.add)
                    if j < taps - 1:
                        ins.then_inc(S("conv_step"), 1)
                    else:
                        ins.then_inc(S("conv_done"), 1)
            skewed(dve, NX, [(conv_w_ahead, 0), (conv, 1)])

            for t in range(KV):
                w_low(t + U0["kv"] + 1, (t + U0["kv"] + 1) % 2)

            def v_move(t, p):
                dve.wait_ge(S("v_turn"), t + 1)
                ve.tensor_copy(v_all[:, ds(t + 1, 1), :].rearrange("p t e -> p (t e)"), ps[:, 4 + p, 0:kv_dim]
                               ).then_inc(S("v_turned"), 1)
            for t in range(NT):
                v_move(t, t % 2)
            ahead("q", lambda t, p: None)

            def low_q(b):
                dve.wait_ge(S("qs_hi_done"), b * 2 + 1)
                ve.tensor_tensor(qs_lo[:], qT[:, :, ds(b * CHUNK, CHUNK)], qs_hi[:].bitcast(F32), ALU.subtract
                                 ).then_inc(S("qs_done"), 1)
                dve.wait_ge(S("qs_hi_done"), b * 2 + 2)
                ve.tensor_tensor(k_lo[:], k_all[:, :, ds(b * CHUNK, 3 * CHUNK)], k_hi[:].bitcast(F32), ALU.subtract
                                 ).then_inc(S("qs_done"), 1)

            def maxima(b, j, variant):
                q = j % 2
                if not (isinstance(b, int) and b == 0 and j < 2):
                    dve.wait_ge(S("p_turned"), b * KV + j)
                for r in range(QR):
                    slope = 2.0 ** (-8.0 * (j * QR + r + 1) / QH)
                    dve.wait_ge(S("scored"), b * QH + (j * QR + r + 1))
                    ve.scalar_tensor_tensor(prob[q][:, r, :], dist[:, variant, :], slope / SCALE, ps[:, 2 + r % 2, 0:3 * CHUNK],
                                            ALU.mult, ALU.add).then_inc(S("biased"), 1)
                dve.wait_ge(S("biased"), b * QH + (j * QR + QR))
                ve.tensor_reduce(soft[:, q, 0, :], prob[q][:], AX_X, ALU.max).then_inc(S("max_step"), 1)
                n = b * (3 * KV) + 3 * j
                dve.wait_ge(S("max_step"), n + 1)
                ve.scalar_tensor_tensor(soft[:, q, 1, :], soft[:, q, 0, :], SCALE, sink[:, j * QR:(j + 1) * QR],
                                        ALU.mult, ALU.max).then_inc(S("max_step"), 1)
                dve.wait_ge(S("max_step"), n + 2)
                ve.tensor_scalar(soft[:, q, 2, :], soft[:, q, 1, :], -1.0, None, ALU.mult).then_inc(S("max_step"), 1)
                ve.tensor_tensor(soft[:, q, 5, :], sink[:, j * QR:(j + 1) * QR], soft[:, q, 1, :], ALU.subtract
                                 ).then_inc(S("max_done"), 1)

            def denominators(b, j):
                q = j % 2
                dve.wait_ge(S("exp_done"), b * (KV * (QR + 1)) + (j + 1) * (QR + 1))
                ve.tensor_tensor(soft[:, q, 3, :], soft[:, q, 3, :], soft[:, q, 5, :], ALU.add).then_inc(S("den_done"), 1)
                dve.wait_ge(S("den_done"), b * KV + (j + 1))
                ve.reciprocal(soft[:, q, 4, :], soft[:, q, 3, :]).then_inc(S("rden_done"), 1)

            def move_o(b, g):
                dve.wait_ge(S("pv_done"), b * KV + 2 * (g + 1))
                ve.tensor_copy(qT[:, g * QR:(g + 1) * QR, ds(b * CHUNK, CHUNK)],
                               ps[:, 7, :].rearrange("p (r l) -> p r l", r=QR)).then_inc(S("o_moved"), 1)

            dve.wait_ge(S("dist_done"), 1)
            low_q(0)
            maxima(0, 0, 0)

            def dve_block(b, variant, after):
                for j in range(KV):
                    if j < KV - 1:
                        maxima(b, j + 1, variant)
                    elif after is not None:
                        maxima(b + 1, 0, after)
                    denominators(b, j)
                    if j < KV - 1 or after is not None:
                        w_low(b * KV + (U0["zg"] + j + 1), (U0["zg"] + j + 1) % 2)
                    if j == 0 and not (isinstance(b, int) and b == 0):
                        move_o(b - 1, 1)
                    if j == 2:
                        move_o(b, 0)
                    if j == 2 and after is not None:
                        low_q(b + 1)
            dve_block(0, 0, 1)
            with dve.Fori(1, NT - 2) as b:
                dve_block(b, 1, 1)
            dve_block(NT - 2, 1, 2)
            dve_block(NT - 1, 2, None)
            move_o(NT - 1, 1)

            def o_low(t, p):
                dve.wait_ge(S("o_hi_done"), t + 1)
                ve.tensor_tensor(act_lo[:, ds(t, 1), :], qT[:, ds(t, 1), :], act_hi[:, ds(t, 1), :].bitcast(F32), ALU.subtract
                                 ).then_inc(S("o_done"), 1)
            pairs(dve, KT, o_low)

            def attn_gate(t, j):
                dve.wait_ge(S("mm_done"), t + (U0["attn"] + 1))
                dve.wait_ge(S(f"tile_landed{j}"), (t - j) * 8 + (8 * NT + 16))
                ve.tensor_tensor(gated[j][:], ps[:, 6:8, :].rearrange("p a l -> p (a l)"), gated[j][:], ALU.mult
                                 ).then_inc(S("attn_gated"), 1)

            def heads(tab, d, c, g):
                return tab[:, d, ds(c, 1), ds(g * R, R)].rearrange("p c r -> p (c r)")

            def wide(ap, n):
                return ap.unsqueeze(2).to_broadcast((P, R, n))
            dve.wait_ge(S("wend_done"), 1)
            with dve.Fori(0, G) as g:
                dve.wait_ge(S("y_done"), g * NT + 2)
                dve.wait_ge(S("h_fwd_done"), g * NT)
                ve.memset(h_fwd[0][:], 0.0).then_inc(S("h_cleared"), 1)
                for i in range(XT):
                    ve.tensor_scalar(ddiag[:, i, :], ident[:], dcol[:, ds(g * XT + i, 1)], None, ALU.mult
                                     ).then_inc(S("ddiag_done"), 1)

                def back_x(i, p):
                    m = g * NT + i
                    c = i * -1 + (NT - 1)
                    dve.wait_ge(S("x_read"), g * (2 * NT) + (i + 3))
                    dve.wait_ge(S("back_state"), m + 1)
                    ve.tensor_tensor(xend[p][:], ps[:, 0, :].rearrange("p (r e) -> p r e", e=HEAD),
                                     wide(heads(wend, 1, c, g), HEAD), ALU.mult).then_inc(S("back_x"), 1)

                def back_h(i, p):
                    m = g * NT + i
                    c = i * -1 + (NT - 1)
                    dve.wait_ge(S("back_state"), m + 3)
                    dve.wait_ge(S("h_decayed"), m + 1)
                    dve.wait_ge(S("hb_done"), g * NT)
                    ve.tensor_tensor(h_back[:, ds(c, 1), :].rearrange("p c e -> p (c e)"), ps[:, 3, :],
                                     h_tmp[:].rearrange("p r e -> p (r e)"), ALU.add).then_inc(S("h_back_done"), 1)
                skewed(dve, NT, [(back_x, 0), (back_h, 1)])
                for j in range(2):
                    w_low(g * 2 + (U0["attn"] + j), (U0["attn"] + j) % 2)

                def fwd_a(c, p):
                    n = g * NT + c
                    dve.wait_ge(S("fwd_turned"), n + 1)
                    ve.tensor_tensor(gm[p][:], ps[:, 2, 0:CHUNK].unsqueeze(1).to_broadcast((P, 2, CHUNK)), tri[:], ALU.mult
                                     ).then_inc(S("gm_done"), 1)
                    dve.wait_ge(S("seg_landed"), n * 16 + 16)
                    dve.wait_ge(S("y_done"), n + 1)
                    ve.tensor_tensor(seg[p][:, 0, :, :], cum_all[:, 0, :, :], wide(heads(acum, 0, c, g), CHUNK), ALU.subtract
                                     ).then_inc(S("seg_f_done"), 1)
                    dve.wait_ge(S("seg_exp"), n + 2)
                    ve.tensor_tensor(cdec[p][:, 0, :, :], cdec[p][:, 0, :, :], cin[p][:].unsqueeze(1).to_broadcast((P, R, CHUNK)),
                                     ALU.mult).then_inc(S("c_read_dve"), 1)
                    dve.wait_ge(S("seg_f_done"), n + 2)
                    ve.tensor_scalar(seg[p][:, 0, :, :], seg[p][:, 0, :, :], 0.0, None, ALU.min).then_inc(S("seg_step"), 1)
                    dve.wait_ge(S("seg_step"), n + 1)
                    dve.wait_ge(S("seg_b_done"), n + 2)
                    ve.scalar_tensor_tensor(seg[p][:, 0, :, :], seg[p][:, 1, :, :], 0.0, seg[p][:, 0, :, :], ALU.min, ALU.add
                                            ).then_inc(S("arg_done"), 1)

                def fwd_b(c, p):
                    n = g * NT + c
                    dve.wait_ge(S("decay_done"), n + 1)
                    dve.wait_ge(S("gm_done"), n + 1)
                    ve.tensor_tensor(seg[p][:, 1, :, :], seg[p][:, 0, :, :],
                                     gm[p][:, 1, :].unsqueeze(1).to_broadcast((P, R, CHUNK)), ALU.mult).then_inc(S("mask_step"), 1)
                    dve.wait_ge(S("mask_step"), n + 1)
                    ve.tensor_tensor(seg[p][:, 0, :, :], seg[p][:, 0, :, :],
                                     gm[p][:, 0, :].unsqueeze(1).to_broadcast((P, R, CHUNK)), ALU.mult).then_inc(S("mask_done"), 1)
                    dve.wait_ge(S("h_cleared"), g + 1)
                    dve.wait_ge(S("h_fwd_done"), n)
                    ve.tensor_tensor(h_tmp[:], h_fwd[p][:], wide(heads(dec, 0, c, g), HEAD), ALU.mult).then_inc(S("h_step"), 1)
                    dve.wait_ge(S("h_step"), n + 1)
                    dve.wait_ge(S("fwd_state"), n + 3)
                    dve.wait_ge(S("y_done"), n + 2)
                    ve.tensor_tensor(h_fwd[1 - p][:].rearrange("p r e -> p (r e)"), ps[:, 3, :],
                                     h_tmp[:].rearrange("p r e -> p (r e)"), ALU.add).then_inc(S("h_fwd_done"), 1)

                def fwd_c(c, p):
                    n = g * NT + c
                    dve.wait_ge(S("y_done"), n + 3)
                    dve.wait_ge(S(f"z_landed{p}"), n * 8 + (16 - 8 * p))
                    ve.tensor_tensor(zin[p][:], ps[:, 4 + p, :].rearrange("p (t l) -> p t l", t=XT), zin[p][:], ALU.mult
                                     ).then_inc(S("y_gated"), 1)
                skewed(dve, NT, [(fwd_b, 1), (fwd_a, 0), (fwd_c, 2)])
                attn_gate(g * 2, 0)
                attn_gate(g * 2 + 1, 1)
            w_low(U0["ssd"], U0["ssd"] % 2)
            w_low(U0["ssd"] + 1, (U0["ssd"] + 1) % 2)

            dve.wait_ge(S("stored0"), ST["attn end"])
            dve.wait_ge(S("stored1"), ST["attn end"])

            def y_low_step(t, q):
                dve.wait_ge(S("y_hi_done"), t + 1)
                ve.scalar_tensor_tensor(y_lo[:, ds(t, 1), :].rearrange("p t l -> p (t l)"), y_raw[q][:], ncol[:, ds(t, 1)],
                                        y_hi[:, ds(t, 1), :].rearrange("p t l -> p (t l)").bitcast(F32),
                                        ALU.mult, ALU.subtract).then_inc(S("y_lo_done"), 1)
            fours(dve, NI, y_low_step)
            dve.wait_ge(S("sq_summed"), NI)
            ve.tensor_scalar(yscale[:], ps[:, 4:6, :].rearrange("p a l -> p (a l)"), 1.0 / inner, EPS, ALU.mult, ALU.add
                             ).then_inc(S("sq_mean"), 1)
            dve.wait_ge(S("y_root"), 1)
            ve.reciprocal(yscale[:], yscale[:]).then_inc(S("yscale_done"), 1)
            dve.wait_ge(S("yscale_done"), 1)

            def merge_out(t, p):
                dve.wait_ge(S("mm_done"), t * 2 + (U0["ssd"] + 2))
                dve.wait_ge(S("merge_landed"), t * 32 + 32)
                wait(dve, "mix_stored", t * 16)
                ve.tensor_tensor(mout[:], out_ps("ssd", p).rearrange("p a l -> p (a l)"), yscale[:], ALU.mult
                                 ).then_inc(S("merge_step"), 1)
                dve.wait_ge(S("merge_step"), t * 2 + 1)
                ve.tensor_tensor(mout[:], mout[:], mga[:], ALU.mult).then_inc(S("merge_step"), 1)
                dve.wait_ge(S("merge_step"), t * 2 + 2)
                ve.tensor_tensor(mout[:], mout[:], mat[:], ALU.add).then_inc(S("merge_out"), 1)

            def merge_step(t, p):
                w_low(t * 2 + (U0["ssd"] + 2), U0["ssd"] % 2)
                merge_out(t, p)
                w_low(t * 2 + (U0["ssd"] + 3), (U0["ssd"] + 1) % 2)
            pairs(dve, KT, merge_step)

            def m_low(t, p):
                dve.wait_ge(S("mix_hi_done"), t + 1)
                ve.tensor_tensor(act_lo[:, ds(t, 1), :].rearrange("p t l -> p (t l)"), mraw[p][:],
                                 act_hi[:, ds(t, 1), :].rearrange("p t l -> p (t l)").bitcast(F32), ALU.subtract
                                 ).then_inc(S("mix_lo_done"), 1)
            pairs(dve, KT, m_low)
            with dve.Fori(0, (KT - 2) // 2) as i:
                for j in range(2):
                    w_low(i * 2 + (U0["mix"] + 2 + j), (U0["mix"] + j) % 2)
            w_low(U0["ffn_in"], U0["ffn_in"] % 2)

            def n_a(n0):
                def part(t, p):
                    dve.wait_ge(S("n_squared"), t + (n0 + NT + 1))
                    mean(stat[:, p, 1:2], stat[:, p, 0:1], "n_mean")
                    dve.wait_ge(S("n_root"), t + (n0 + NT + 1))
                    ve.reciprocal(stat[:, p, 3:4], stat[:, p, 2:3]).then_inc(S("n_rstd"), 1)
                    dve.wait_ge(S("n_rstd"), t + (n0 + NT + 1))
                    if n0 == 0:
                        wait(dve, "h2_turned", t - 1)
                    ve.scalar_tensor_tensor(n2[p][:], ps[:, 2 * p:2 * p + 2, :].rearrange("p a l -> p (a l)"), stat[:, p, 3:4],
                                            norm_a[:], ALU.mult, ALU.mult).then_inc(S("n_scaled"), 1)
                    dve.wait_ge(S("n_scaled"), t + (n0 + 1))
                    dve.wait_ge(S(f"n_x_landed{p}"), (t - p) * 8 + (8 * n0 + 16))
                    name = "out" if n0 else "x1"
                    wait(dve, f"stored{p}", (t - p) * 8 + ST[name])
                    ve.tensor_tensor(n1[p][:], n2[p][:], nx[p][:], ALU.add).then_inc(S("n_added"), 1)
                return part

            def n_b(t, p):
                dve.wait_ge(S("n2_squared_b"), t + 1)
                mean(stat[:, p, 5:6], stat[:, p, 4:5], "n2_mean_b")
                dve.wait_ge(S("n2_root_b"), t + 1)
                ve.reciprocal(stat[:, p, 7:8], stat[:, p, 6:7]).then_inc(S("n2_rstd_b"), 1)
                dve.wait_ge(S("n2_rstd_b"), t + 1)
                ve.scalar_tensor_tensor(n2[p][:], n1[p][:], stat[:, p, 7:8], norm_b[:], ALU.mult, ALU.mult
                                        ).then_inc(S("h2_done"), 1)

            def n_c(t, p):
                dve.wait_ge(S("h2_hi_done"), t + 1)
                cols = ds(t * CHUNK, CHUNK)
                ve.tensor_tensor(h2_lo[:, :, cols], ps[:, 4 + 2 * p:6 + 2 * p, :].rearrange("p a (b l) -> p (a b) l", l=CHUNK),
                                 h2_hi[:, :, cols].bitcast(F32), ALU.subtract).then_inc(S("h2_lo_done"), 1)
            dve.wait_ge(S("norm2_landed"), 32)
            skewed(dve, NT, [(n_a(0), 0), (n_b, 1), (n_c, 2)])

            dve.wait_ge(S("stored0"), ST["x1 end"])
            dve.wait_ge(S("stored1"), ST["x1 end"])

            def f_step(t):
                dve.wait_ge(S("g_done"), t + 1)
                dve.wait_ge(S("mm_done"), t * 2 + (U0["ffn_in"] + 2))
                ve.tensor_tensor(f_act[:, ds(t, 1), :].rearrange("p t l -> p (t l)"),
                                 pair_of(O0["ffn_in"] + 1).rearrange("p a l -> p (a l)"), gact[:], ALU.mult
                                 ).then_inc(S("gact_read"), 1)
            w_low(U0["ffn_in"] + 1, (U0["ffn_in"] + 1) % 2)
            with dve.Fori(0, FT - 1) as t:
                w_low(t * 2 + (U0["ffn_in"] + 2), U0["ffn_in"] % 2)
                f_step(t)
                w_low(t * 2 + (U0["ffn_in"] + 3), (U0["ffn_in"] + 1) % 2)
            w_low(U0["ffn_out"], U0["ffn_out"] % 2, FK[0])
            f_step(FT - 1)
            w_low(U0["ffn_out"] + 1, (U0["ffn_out"] + 1) % 2, FK[1])
            for half in range(2):
                cols = slice(half * HALF, (half + 1) * HALF)
                with dve.Fori(0, FT) as k:
                    dve.wait_ge(S("f_hi_done"), k + (half * FT + 1))
                    ve.tensor_tensor(f_lo[:, ds(k, 1), cols].rearrange("p t l -> p (t l)"),
                                     f_act[:, ds(k, 1), cols].rearrange("p t l -> p (t l)"),
                                     f_hi[:, ds(k, 1), :].rearrange("p t l -> p (t l)").bitcast(F32), ALU.subtract
                                     ).then_inc(S("f_lo_done"), 1)

                def ffn_low(t, p, half=half, last=False):
                    for j in ((2,) if last else (2, 3, 4)):
                        w_low(t * 3 + (U0["ffn_out"] + 3 * KT * half + j), (U0["ffn_out"] + p + j) % 2, FK[j % 3])
                if half == 0:
                    pairs(dve, KT, ffn_low)
                else:
                    pairs(dve, KT - 2, ffn_low)
                    ffn_low(KT - 2, 0)
                    ffn_low(KT - 1, 1, last=True)
            dve.wait_ge(S("norm3_landed"), 16)
            skewed(dve, NT, [(n_a(NT), 0)])

        @block.tensor
        def _(pe):
            te = nc.tensor
            pe.sem_inc(S("p_turned"), 1)
            for name in ("x_read", "back_state", "fwd_state", "y_done"):
                pe.sem_inc(S(name), 2)

            def product(dst, p, ks, moving, first=True, last=True, ready=None, kt=KT):
                for k in ks:
                    if ready:
                        ready(k)
                    begin, end = first and k == 0, last and k == kt - 1
                    ins = None
                    for h, d in enumerate(dst):
                        mh, ml = moving(h, k)
                        te.matmul(d, whi[p][:, k, :], mh, start=begin, stop=False)
                        te.matmul(d, whi[p][:, k, :], ml, start=False, stop=False)
                    for h, d in enumerate(dst):
                        ins = te.matmul(d, wlo[p][:, k, :], moving(h, k)[0], start=False, stop=end)
                return ins

            def from_act(h, k):
                cols = slice(h * HALF, (h + 1) * HALF)
                return act_hi[:, k, cols], act_lo[:, k, cols]

            def from_h2(h, k):
                cols = slice(h * HALF, (h + 1) * HALF)
                return h2_hi[:, k, cols], h2_lo[:, k, cols]

            def unit(name, t, p, ready=None, moving=from_act):
                u0, o0 = U0[name], O0[name]
                b = 2 * ((o0 + p) % 2)
                pe.wait_ge(S("w_lo_done"), t + (u0 + 1))
                product([ps[:, b, :], ps[:, b + 1, :]], (u0 + p) % 2, range(KT), moving, ready=ready).then_inc(S("mm_done"), 1)

            pe.wait_ge(S("const_step"), 8)

            def turn_x(t, p):
                pe.wait_ge(S("xn_done"), t + 1)
                wait(pe, "h_done", t - 1)
                for k in range(KT):
                    ins = te.transpose(ps[:, 2 * p + k // 4, (k % 4) * P:(k % 4 + 1) * P], x_n[p][:, k * P:(k + 1) * P], ident[:])
                ins.then_inc(S("x_turned"), 1)
            pairs(pe, NT, turn_x, peel=True)
            pe.wait_ge(S("h_done"), NT)
            unit("dt", 0, 0)

            def xbc_unit(t, p):
                wait(pe, "moved", t)
                unit("xbc", t, p)
            xbc_unit(0, 0)
            pe.wait_ge(S("dt_ready"), 1)
            HH = 2 * H
            for src, bank in ((dt_v, 4), (dt_e, 5)):
                for c in range(NT):
                    ins = te.transpose(ps[:, bank, c * HH:(c + 1) * HH], src[0:HH, c * CHUNK:(c + 1) * CHUNK], ident[0:HH, 0:HH])
            ins.then_inc(S("dt_turned"), 1)
            pe.wait_ge(S("dt_tok"), 2)
            for d in range(2):
                for bank, mat_ in ((6, tri[:, d, :]), (7, ones[:])):
                    ins = te.matmul(ps[:, bank, d * NT * H:(d + 1) * NT * H].rearrange("p (c h) -> p c h", h=H), mat_,
                                    atok[:, :, d, :], start=True, stop=True, skip_group_check=True)
            ins.then_inc(S("dt_summed"), 1)
            pe.wait_ge(S("tables_done"), 2)
            for c in range(NT):
                ins = te.matmul(ps[0:HH, 4 + c // 2, (c % 2) * 256:(c % 2 + 1) * 256], atok[:, c, :, :].rearrange("p d h -> p (d h)"),
                                tri[:].rearrange("p d l -> p (d l)"), start=True, stop=True, skip_group_check=True)
            ins.then_inc(S("rows_summed"), 1)
            xbc_unit(1, 1)
            pairs(pe, conv_dim // P, xbc_unit, first=2)

            for t in range(KV):
                pe.wait_ge(S("moved"), O0["kv"] + t - 1)
                unit("kv", t, t % 2)

            def q_unit(t, p):
                wait(pe, "moved", t + (O0["q"] - 1))
                unit("q", t, p)
            pe.wait_ge(S("moved"), O0["q"])
            for t in range(NT):
                wait(pe, "v_turned", t - 1)
                for j in range(2):
                    ins = te.transpose(ps[:, 4 + t % 2, j * P:(j + 1) * P], stage[j][:, t * CHUNK:(t + 1) * CHUNK], ident[:])
                ins.then_inc(S("v_turn"), 1)
            pairs(pe, q_dim // P, q_unit)

            def score(b, j, heads):
                half = slice((j % 2) * HEAD, (j % 2 + 1) * HEAD)
                g = j // 2
                pe.wait_ge(S("qs_done"), b * 2 + 2)
                for r in heads:
                    i = g * QR + r
                    dst = ps[:, 2 + r % 2, 0:3 * CHUNK]
                    if not (isinstance(b, int) and b == 0 and j == 0 and r < 2):
                        pe.wait_ge(S("biased"), b * QH + (j * QR + r - 1))
                    te.matmul(dst, qs_hi[half, i, :], k_hi[half, g, :], start=True, stop=False)
                    te.matmul(dst, qs_hi[half, i, :], k_lo[half, g, :], start=False, stop=False)
                    te.matmul(dst, qs_lo[half, i, :], k_hi[half, g, :], start=False, stop=True).then_inc(S("scored"), 1)

            def turn_p(b, j):
                pe.wait_ge(S("rdiag_done"), b * KV + (j + 1))
                pe.wait_ge(S("pT_done"), b * KV + (j + 1))
                for kb in range(3):
                    for r in range(QR):
                        ins = te.matmul(ps[:, 4 + kb, r * CHUNK:(r + 1) * CHUNK], prob[j % 2][:, r, kb * CHUNK:(kb + 1) * CHUNK],
                                        rdiag[:, r, :], start=True, stop=True, skip_group_check=True)
                ins.then_inc(S("p_turned"), 1)

            def weigh_v(b, j):
                pe.wait_ge(S("v_win_done"), b + 1)
                pe.wait_ge(S("pT_done"), b * KV + (j + 2))
                if j % 2 == 0:
                    pe.wait_ge(S("o_moved"), b * 2 + (j // 2 + 1))
                for kb in range(3):
                    ins = te.matmul(ps[(j % 2) * HEAD:(j % 2 + 1) * HEAD, 7, :], v_win[:, kb, j * HEAD:(j + 1) * HEAD],
                                    probT[:, kb, :], start=kb == 0, stop=kb == 2)
                ins.then_inc(S("pv_done"), 1)

            pe.wait_ge(S("pads_done"), 4)
            pe.wait_ge(S("moved"), O0["zg"])
            score(0, 0, range(QR))
            score(0, 1, range(QR))

            def zg_part(b, j, ks):
                if ks[0] == 0:
                    pe.wait_ge(S("w_lo_done"), b * KV + (U0["zg"] + j + 1))
                    pe.wait_ge(S("moved"), b * KV + (O0["zg"] + j))
                ins = product([ps[:, 0, :], ps[:, 1, :]], (U0["zg"] + j) % 2, ks, from_act)
                if ks[-1] == KT - 1:
                    ins.then_inc(S("mm_done"), 1)

            def pe_block(b, last=False):
                for j in range(KV):
                    turn_p(b, j)
                    nb, nj = (b, j + 2) if j < 2 else (b + 1, j - 2)
                    more = j < 2 or not last
                    if more:
                        score(nb, nj, range(0, 2))
                    zg_part(b, j, range(0, KT // 2))
                    if more:
                        score(nb, nj, range(2, QR))
                    zg_part(b, j, range(KT // 2, KT))
                    weigh_v(b, j)
            with pe.Fori(0, NT - 1) as b:
                pe_block(b)
            pe_block(NT - 1, True)

            def o_ready(k):
                pe.wait_ge(S("o_done"), k + 1)

            def attn_unit(t, j):
                pe.wait_ge(S("w_lo_done"), t + (U0["attn"] + 1))
                pe.wait_ge(S("attn_gated"), t + 1)
                product([ps[:, 6, :], ps[:, 7, :]], (U0["attn"] + j) % 2, range(KT), from_act).then_inc(S("mm_done"), 1)

            o_ready(KT - 1)
            with pe.Fori(0, G) as g:
                def turn_back(i, p):
                    m = g * NT + i
                    pe.wait_ge(S(f"back_landed{p}"), g * (32 * NT // 2) + (i * 16 + (32 - 16 * p)))
                    pe.wait_ge(S("back_x"), m)
                    pe.wait_ge(S("back_btok"), m)
                    for k in range(XT):
                        te.transpose(ps[:, 0, k * P:(k + 1) * P], xin[p][:, k, :], ident[:])
                    te.transpose(ps[:, 1, 0:STATE], bin_[p][:], ident[:]).then_inc(S("x_read"), 1)

                def state_back(i, p):
                    m = g * NT + i
                    pe.wait_ge(S("back_x"), m + 1)
                    pe.wait_ge(S("back_btok"), m + 1)
                    pe.wait_ge(S("h_back_done"), m)
                    te.matmul(ps[:, 3, :], btok[p][:], xend[p][:].rearrange("p r e -> p (r e)"), start=True, stop=True
                              ).then_inc(S("back_state"), 1)
                skewed(pe, NT, [(turn_back, 0), (state_back, 1)])
                attn_unit(g * 2, 0)

                def turn_fwd(c, p):
                    n = g * NT + c
                    pe.wait_ge(S(f"fwd_landed{p}"), g * (48 * NT // 2) + (c * 24 + (48 - 24 * p)))
                    pe.wait_ge(S("xtok_done"), n)
                    pe.wait_ge(S("fwd_btok"), n)
                    pe.wait_ge(S("gm_done"), n)
                    pe.wait_ge(S("h_back_done"), g * NT + NT)
                    for k in range(XT):
                        te.transpose(ps[:, 0, k * P:(k + 1) * P], xin[p][:, k, :], ident[:])
                    te.transpose(ps[:, 1, 0:STATE], bin_[p][:], ident[:])
                    te.matmul(ps[:, 2, 0:CHUNK], bin_[p][:], cin[p][:], start=True, stop=True).then_inc(S("fwd_turned"), 1)

                def skip_x(c, p):
                    n = g * NT + c
                    pe.wait_ge(S("y_gated"), n + 1)
                    pe.wait_ge(S("ddiag_done"), g * XT + XT)
                    for k in range(XT):
                        ins = te.matmul(ps[:, 4 + p, k * CHUNK:(k + 1) * CHUNK], ddiag[:, k, :], xin[p][:, k, :],
                                        start=k == 0, stop=False, skip_group_check=True)
                    ins.then_inc(S("x_read"), 1)

                def state(c, p):
                    n = g * NT + c
                    pe.wait_ge(S("xdt_done"), g * (3 * NT) + (c * 3 + 6))
                    pe.wait_ge(S("fwd_btok"), n + 1)
                    pe.wait_ge(S("h_fwd_done"), n)
                    te.matmul(ps[:, 3, :], btok[p][:], xend[p][:].rearrange("p r e -> p (r e)"), start=True, stop=True
                              ).then_inc(S("fwd_state"), 1)

                def sums(c, p):
                    n = g * NT + c
                    pe.wait_ge(S("h_cleared"), g + 1)
                    pe.wait_ge(S("c_read_dve"), n + 3)
                    pe.wait_ge(S("c_read_pool"), n + 3)
                    pe.wait_ge(S("hb_done"), n + 1)
                    pe.wait_ge(S("mask_done"), n + 1)
                    for r in range(R):
                        dst = ps[(r % 2) * HEAD:(r % 2 + 1) * HEAD, 4 + p, (r // 2) * CHUNK:(r // 2 + 1) * CHUNK]
                        for a, (lhs, rhs) in enumerate(((h_fwd[p][:, r, :], cdec[p][:, 0, r, :]),
                                                        (hb_now[p][:, r, :], cdec[p][:, 1, r, :]),
                                                        (xdt[p][:, 1, r, :], seg[p][:, 1, r, :]),
                                                        (xdt[p][:, 0, r, :], seg[p][:, 0, r, :]))):
                            ins = te.matmul(dst, lhs, rhs, start=False, stop=a == 3, skip_group_check=True)
                    ins.then_inc(S("y_done"), 1)
                skewed(pe, NT, [(state, 1), (turn_fwd, 0), (sums, 1), (skip_x, 0)])
                attn_unit(g * 2 + 1, 1)

            def from_y(j):
                def moving(h, k):
                    cols = slice(h * HALF, (h + 1) * HALF)
                    return y_hi[:, j * KT + k, cols], y_lo[:, j * KT + k, cols]
                return moving

            def ssd_out(t, p, ready=None):
                u0 = U0["ssd"]
                b = 2 * ((O0["ssd"] + p) % 2)
                for j in range(2):
                    pe.wait_ge(S("w_lo_done"), t * 2 + (u0 + j + 1))
                    if j == 0:
                        wait(pe, "merge_out", t - 1)
                    product([ps[:, b, :], ps[:, b + 1, :]], (u0 + j) % 2, range(KT), from_y(j), first=j == 0, last=j == 1,
                            ready=(lambda k, j=j: ready(j * KT + k)) if ready else None).then_inc(S("mm_done"), 1)
            pe.wait_ge(S("y_gated"), G * NT + 2)

            def y_ready(k):
                pe.wait_ge(S("y_squared"), k + 1)
                for h in range(2):
                    ins = te.matmul(ps[:, 4 + h, :], ones[:], y_sq[k % 2][:, h * HALF:(h + 1) * HALF], start=k == 0,
                                    stop=k == NI - 1)
                ins.then_inc(S("sq_summed"), 1)
                pe.wait_ge(S("y_lo_done"), k + 1)
            ssd_out(0, 0, ready=y_ready)
            ssd_out(1, 1)
            pairs(pe, KT, ssd_out, first=2)

            def mix_unit(t, p):
                wait(pe, "proj_out", t - 1)
                unit("mix", t, p, ready=(lambda k: pe.wait_ge(S("mix_lo_done"), k + 1)) if isinstance(t, int) and t == 0 else None)
            pe.wait_ge(S("merge_out"), KT)
            mix_unit(0, 0)
            mix_unit(1, 1)
            pairs(pe, KT, mix_unit, first=2)

            def turn_f(n0):
                def part(t, p):
                    pe.wait_ge(S(f"n_f_landed{p}"), (t - p) * 8 + (8 * n0 + 16))
                    wait(pe, "n_scaled", t + (n0 - 1))
                    for k in range(KT):
                        ins = te.transpose(ps[:, 2 * p + k // 4, (k % 4) * P:(k % 4 + 1) * P], nf[p][:, k, :], ident[:])
                    ins.then_inc(S("n_turned"), 1)
                return part

            def turn_h2(t, p):
                pe.wait_ge(S("h2_done"), t + 1)
                wait(pe, "h2_lo_done", t - 1)
                for k in range(KT):
                    ins = te.transpose(ps[:, 4 + 2 * p + k // 4, (k % 4) * P:(k % 4 + 1) * P], n2[p][:, k * P:(k + 1) * P], ident[:])
                ins.then_inc(S("h2_turned"), 1)
            pe.wait_ge(S("proj_out"), KT)
            skewed(pe, NT, [(turn_f(0), 0), (turn_h2, 1)])

            pe.wait_ge(S("h2_lo_done"), NT)
            pe.wait_ge(S("n_scaled"), NT)

            def ffn_pair(t):
                wait(pe, "g_done", t)
                unit("ffn_in", t * 2, 0, moving=from_h2)
                wait(pe, "gact_read", t)
                unit("ffn_in", t * 2 + 1, 1, moving=from_h2)
            with pe.Fori(0, FT) as t:
                ffn_pair(t)

            def ffn_out(t, p, half, ready=None):
                u0 = U0["ffn_out"] + half * 3 * KT
                b = 2 * ((O0["ffn_out"] + p) % 2)
                for j in range(3):
                    pe.wait_ge(S("w_lo_done"), t * 3 + (u0 + j + 1))
                    if j == 0:
                        wait(pe, "ffn_out_done", t + (half * KT - 1))

                    def moving(h, k, j=j):
                        return f_hi[:, FK0[j] + k, :], f_lo[:, FK0[j] + k, half * HALF:(half + 1) * HALF]
                    product([ps[:, b, :]], (u0 + p + j) % 2, range(FK[j]), moving, first=j == 0, last=j == 2, kt=FK[j],
                            ready=(lambda k, j=j: ready(FK0[j] + k)) if ready else None).then_inc(S("mm_done"), 1)
            pe.wait_ge(S("gact_read"), FT)
            for half in range(2):
                ffn_out(0, 0, half, ready=lambda k: pe.wait_ge(S("f_lo_done"), k + half * FT + 1))
                ffn_out(1, 1, half)
                pairs(pe, KT, lambda t, p: ffn_out(t, p, half), first=2)
            pe.wait_ge(S("ffn_out_done"), 2 * KT)
            skewed(pe, NT, [(turn_f(NT), 0)])


_INS = ['x', 'pre_mix_norm', 'w_in', 'conv_w', 'conv_b', 'dt_bias_f', 'dt_bias_b', 'A_log_f', 'A_log_b', 'D_skip',
        'ssd_norm', 'w_ssd_proj', 'attn_sink', 'w_attn_proj', 'w_out', 'post_mix_norm', 'pre_ffn_norm', 'w_ffn_in',
        'w_ffn_out', 'post_ffn_norm']


def kernel(**inputs):
    import numpy as _np
    import concourse.bacc as _bacc
    from concourse import mybir as _mybir
    from concourse.bass_utils import run_bass_kernel_spmd as _run

    nc = _bacc.Bacc("TRN2", target_bir_lowering=False, num_devices=1)
    arrays, args = {}, []
    for name in _INS:
        a = _np.ascontiguousarray(inputs[name])
        arrays[f"in_{name}_dram"] = a
        args.append(nc.dram_tensor(f"in_{name}_dram", a.shape, _mybir.dt.from_np(a.dtype), kind="ExternalInput").ap())
    args.append(nc.dram_tensor("out_dram", inputs['x'].shape, _mybir.dt.float32, kind="ExternalOutput").ap())
    hybrid_encoder_layer(nc, *args)
    r = _run(nc, [arrays], core_ids=[0])
    return r.results[0]["out_dram"]
```

```python
from contextlib import ExitStack

import concourse.bass as bass
from concourse import mybir

ALU = mybir.AluOpType
ACT = mybir.ActivationFunctionType
F32 = mybir.dt.float32
F32R = mybir.dt.float32r
AX_X = mybir.AxisListType.X
ds = bass.ds

P = 128
EPS = 1e-6
HEAD = 64
STATE = 128
CHUNK = 128
WINDOW = 128
MASKED = -1e30
LOG1P_TERMS = 8


def hybrid_encoder_layer(nc, x, pre_mix_norm, w_in, conv_w, conv_b, dt_bias_f, dt_bias_b, A_log_f, A_log_b,
                         D_skip, ssd_norm, w_ssd_proj, attn_sink, w_attn_proj, w_out, post_mix_norm,
                         pre_ffn_norm, w_ffn_in, w_ffn_out, post_ffn_norm, out):
    _, L, D = x.shape
    KT = D // P
    NT = L // CHUNK
    taps, conv_dim = conv_w.shape[1:]
    pad = taps // 2
    inner = w_ssd_proj.shape[1]
    H = D_skip.shape[1]
    G = (conv_dim - inner) // (2 * STATE)
    R = H // G
    XT = R * HEAD // P
    NI = inner // P
    QH = attn_sink.shape[1]
    q_dim = w_attn_proj.shape[1]
    KV = 4
    kv_dim = KV * HEAD
    QR = QH // KV
    F = w_ffn_out.shape[1]
    FT = F // P
    FK = [KT] + 2 * [(FT - KT) // 2]
    FK0 = [0, KT, KT + (FT - KT) // 2]
    HALF = 512
    SCALE = HEAD ** -0.5
    c_z, c_xbc = 0, inner
    c_dt = c_xbc + conv_dim
    c_q = c_dt + 2 * H
    c_k = c_q + q_dim
    c_v = c_k + kv_dim
    c_gate = c_v + kv_dim

    stages = [("dt", 1, 1), ("xbc", conv_dim // P, 1), ("kv", 2 * kv_dim // P, 1), ("q", q_dim // P, 1),
              ("zg", NI + 2 * KT, 1), ("attn", KT, 1), ("ssd", 2 * KT, 2), ("mix", 2 * KT, 1), ("ffn_in", 2 * FT, 1),
              ("ffn_out", 6 * KT, 3)]
    U0, O0, NU = {}, {}, {}
    u = o = 0
    for name, n, per in stages:
        U0[name], O0[name], NU[name] = u, o, n
        u, o = u + n, o + n // per
    ALL_UNITS = u
    ST, n = {}, 0
    for name, tiles in (("xbc", conv_dim // P), ("attn", KT), ("proj", 2 * KT),
                        ("ffn", 2 * KT)):
        ST[name], n = n, n + 8 * tiles
        ST[name + " end"] = n

    w1 = w_in[0].rearrange("(k p) n -> p k n", p=P)
    w_ssd = w_ssd_proj[0].rearrange("(j k p) n -> p j k n", p=P, k=KT)
    w_mix = w_out[0].rearrange("(k p) n -> p k n", p=P)
    w_f1 = w_ffn_in[0].rearrange("(k p) n -> p k n", p=P)
    w_f2 = w_ffn_out[0].rearrange("(k p) n -> p k n", p=P)
    w_at = w_attn_proj[0].rearrange("(g r i p) n -> r g p i n", g=KV // 2, r=2, i=QR)
    x_rows = x[0].rearrange("(t p) d -> t p d", p=P)
    out_rows = out[0].rearrange("(t p) d -> t p d", p=P)

    def dram(name, shape):
        return nc.dram_tensor(name, shape, F32, kind="Internal").ap()

    xbc_d = dram("xbc_d", [conv_dim // P, P, L])
    z_d = dram("z_d", [NI, P, L])
    gate_d = dram("gate_d", [2 * KT, P, L])
    y_d = dram("y_d", [NI, P, L])
    attn_d = dram("attn_d", [KT, P, L])
    proj_d = dram("proj_d", [P, KT, L])
    ffn_d = dram("ffn_d", [P, KT, L])
    x1_d = dram("x1_d", [NT, P, D])
    cum_d = dram("cum_d", [G, NT, 2, R, CHUNK])

    top = [16512]

    def at(name, shape, off, dt=F32):
        return nc.alloc_sbuf_tensor_at(name, shape, dt, offset=off)

    def const(name, shape):
        n = 4
        for s in shape[1:]:
            n *= s
        off = top[0]
        top[0] += (n + 31) // 32 * 32
        return at(name, shape, off)

    ident = const("ident", [P, P])
    tri = const("tri", [P, 2, P])
    ones = const("ones", [P, P])
    dist_off = top[0]
    dist = const("dist", [P, 3, 3 * CHUNK])
    norm_a_off = top[0]
    norm_a = const("norm_a", [P, D])
    norm_off = top[0]
    norm_b = const("norm_b", [P, D])
    cw = const("cw", [P, conv_dim // P, taps])
    cb = const("cb", [P, conv_dim // P])
    dcol = const("dcol", [P, NI])
    ncol = const("ncol", [P, NI])
    sink = const("sink", [P, QH])
    dtb = const("dtb", [P, 1])
    alog = const("alog", [P, 1])
    stat = const("stat", [P, 2, 8])
    soft = const("soft", [P, 2, 6, QR])
    gact = at("gact", [P, L], dist_off)
    slot = KT * P * 4
    wraw = [at(f"wraw{j}", [P, KT, P], top[0] + j * slot) for j in range(2)]
    whi = [at(f"whi{j}", [P, KT, P], top[0] + (2 + j) * slot, F32R) for j in range(2)]
    wlo = [at(f"wlo{j}", [P, KT, P], top[0] + (4 + j) * slot, F32R) for j in range(2)]
    top[0] += 6 * slot
    late = top[0]
    dtok = const("dtok", [P, 2, NT, H])
    acum = const("acum", [P, 2, NT, H])
    wend = const("wend", [P, 2, NT, H])
    dec = const("dec", [P, 2, NT, H])
    base = top[0]
    K = 1024

    act_hi = at("act_hi", [P, KT, L], base, F32R)
    act_lo = at("act_lo", [P, KT, L], base + 32 * K, F32R)
    qT = at("qT", [P, KT, L], base + 64 * K)
    kwin = L + 2 * CHUNK
    k_all = at("k_all", [P, KV // 2, kwin], base + 96 * K)
    k_hi = at("k_hi", [P, KV // 2, 3 * CHUNK], base + 106 * K, F32R)
    k_lo = at("k_lo", [P, KV // 2, 3 * CHUNK], base + 109 * K, F32R)
    v_all = at("v_all", [P, NT + 2, kv_dim], base + 112 * K)
    tmp = base + 122 * K
    x_t = [at(f"x_t{j}", [P, D], tmp + j * 4 * K) for j in range(2)]
    x_n = [at(f"x_n{j}", [P, D], tmp + (2 + j) * 4 * K) for j in range(2)]
    junk = at("junk", [P, D], tmp + 16 * K)
    praw = [at(f"praw{j}", [P, L + 2 * pad], tmp + j * 4128) for j in range(2)]
    cacc = [at(f"cacc{j}", [P, L], tmp + 8256 + j * 4 * K) for j in range(2)]
    stage = [at(f"stage{j}", [P, L], base + (151 + j * 4) * K) for j in range(2)]
    dt_v = at("dt_v", [P, L], base + 64 * K)
    dt_e = at("dt_e", [P, L], base + 68 * K)
    dt_t = at("dt_t", [P, L], base + 72 * K)
    dt_t2 = at("dt_t2", [P, L], base + 76 * K)
    dt_q = at("dt_q", [P, L], base + 80 * K)
    dt_r = at("dt_r", [P, L], base + 84 * K)
    atok = at("atok", [P, NT, 2, H], base + 88 * K)
    rows = at("rows", [P, NT, CHUNK], base + 90 * K)
    ddif = at("ddif", [P, 2, NT, H], base + 94 * K)
    qs_hi = at("qs_hi", [P, KT, CHUNK], base + 122 * K, F32R)
    qs_lo = at("qs_lo", [P, KT, CHUNK], base + 126 * K, F32R)
    prob = [at(f"prob{j}", [P, QR, 3 * CHUNK], base + (130 + 6 * j) * K) for j in range(2)]
    probT = at("probT", [P, 3, QR * CHUNK], base + 142 * K)
    v_win = at("v_win", [P, 3, kv_dim], base + 148 * K)
    rdiag = at("rdiag", [P, QR, CHUNK], norm_off)
    gated = [at(f"gated{j}", [P, L], off) for j, off in enumerate((norm_a_off, dist_off))]
    s0 = base + 64 * K
    h_back = at("h_back", [P, NT + 1, R * HEAD], s0)
    s1 = s0 + 18 * K
    xin = [at(f"xin{j}", [P, XT, CHUNK], s1 + j * 2 * K) for j in range(2)]
    bin_ = [at(f"bin{j}", [P, CHUNK], s1 + 4 * K + j * 512) for j in range(2)]
    cin = [at(f"cin{j}", [P, CHUNK], s1 + 5 * K + j * 512) for j in range(2)]
    zin = [at(f"zin{j}", [P, XT, CHUNK], s1 + 6 * K + j * 2 * K) for j in range(2)]
    cum_all = at("cum_all", [P, 2, R, CHUNK], base + 151 * K)
    s2 = s1 + 10 * K
    seg = [at(f"seg{j}", [P, 2, R, CHUNK], s2 + j * 8 * K) for j in range(2)]
    cdec = [at(f"cdec{j}", [P, 2, R, CHUNK], s2 + (16 + j * 8) * K) for j in range(2)]
    s3 = s2 + 32 * K
    xtok = [at(f"xtok{j}", [P, R, HEAD], s3 + j * 2 * K) for j in range(2)]
    xdt = [at(f"xdt{j}", [P, 2, R, HEAD], s3 + (4 + j * 4) * K) for j in range(2)]
    xend = [at(f"xend{j}", [P, R, HEAD], s3 + (12 + j * 2) * K) for j in range(2)]
    btok = [at(f"btok{j}", [P, STATE], s3 + 16 * K + j * 512) for j in range(2)]
    gm = [at(f"gm{j}", [P, 2, CHUNK], s3 + 17 * K + j * K) for j in range(2)]
    h_fwd = [at(f"h_fwd{j}", [P, R, HEAD], s3 + (19 + 2 * j) * K) for j in range(2)]
    h_tmp = at("h_tmp", [P, R, HEAD], norm_off + 2 * K)
    ddiag = at("ddiag", [P, XT, P], norm_off)
    hb_now = [at(f"hb_now{j}", [P, R, HEAD], s3 + (23 + j * 2) * K) for j in range(2)]
    y_raw = [at(f"y_raw{j}", [P, L], base + (128 + 4 * j) * K) for j in range(4)]
    y_sq = [at(f"y_sq{j}", [P, L], base + (144 + 4 * j) * K) for j in range(2)]
    y_lo = at("y_lo", [P, NI, L], base, F32R)
    y_hi = at("y_hi", [P, NI, L], base + 64 * K, F32R)
    yscale = at("yscale", [P, L], late)
    mga = at("mga", [P, L], norm_a_off)
    mat = at("mat", [P, L], norm_off)
    merged = at("merged", [P, KT, L], base + 128 * K)
    m_hi = at("m_hi", [P, KT, L], late + 64 * K, F32R)
    m_lo = at("m_lo", [P, KT, L], late + 96 * K, F32R)
    pout = [at(f"pout{j}", [P, HALF], late + (164 + 2 * j) * K) for j in range(2)]
    row = [P, 2, HALF]
    n_bufs = [at(f"n_buf{j}", row, late + (128 + 4 * j) * K) for j in range(9)]
    h2_hi = at("h2_hi", [P, KT, L], late, F32R)
    h2_lo = at("h2_lo", [P, KT, L], late + 32 * K, F32R)
    f_act = at("f_act", [P, FT, L], late + 64 * K)
    n_late = [f_act[:, 2 * j:2 * j + 2, 0:HALF] for j in range(9)]
    f_lo = at("f_lo", [P, FT, L], late + 64 * K, F32R)
    f_hi = at("f_hi", [P, FT, HALF], late, F32R)
    f_hi2 = at("f_hi2", [P, KT, HALF], late + 44 * K, F32R)
    fout = [at(f"fout{j}", [P, HALF], late + (60 + 2 * j) * K) for j in range(2)]

    ps = nc.alloc_psum_tensor("ps", [P, 8, 512], F32)

    def norm_bufs(n0):
        b = n_late if n0 else [x[:] for x in n_bufs]
        return b[0:2], b[2:4], b[4:6], b[6:8], b[8]

    def two(ap):
        return ap.rearrange("p (a l) -> p a l", a=2)

    def beside(norm_turn, turns, out):
        out(0)
        out(1)
        for s in range(NT // 2):
            norm_turn(s)
            out(s + 2)
        for t in range(NT // 2 + 2, KT):
            out(t)
        for s in range(NT // 2, turns):
            norm_turn(s)

    def norm_turns(parts):
        def turn(s):
            for part, lag in parts:
                if 0 <= s - lag < NT:
                    part(s - lag, (s - lag) % 2)
        return turn

    sems = {}

    def S(name):
        if name not in sems:
            sems[name] = nc.alloc_semaphore(name)
        return sems[name]

    def wait(eng, name, value):
        if not (isinstance(value, int) and value <= 0):
            eng.wait_ge(S(name), value)

    def pairs(eng, n, step, first=0, peel=False):
        if peel:
            step(0, 0)
            step(1, 1)
            first = 2
        turns = (n - first) // 2
        if turns > 0:
            with eng.Fori(0, turns) as i:
                for j in range(2):
                    step(i * 2 + (first + j), (first + j) % 2)
        for t in range(first + 2 * max(turns, 0), n):
            step(t, t % 2)

    def fours(eng, n, step):
        for t in range(4):
            step(t, t)
        with eng.Fori(1, n // 4) as i:
            for j in range(4):
                step(i * 4 + j, j)

    def skewed(eng, n, parts, lead=0, between=None):
        depth = max(lag for _, lag in parts)
        lead = max(lead, depth + depth % 2)
        for s in range(lead):
            for part, lag in parts:
                if 0 <= s - lag < n:
                    part(s - lag, (s - lag) % 2)
        if between:
            between()
        with eng.Fori(0, (n - lead) // 2) as i:
            for j in range(2):
                for part, lag in parts:
                    part(i * 2 + (lead + j - lag), (lead + j - lag) % 2)
        for s in range(n, n + depth):
            for part, lag in parts:
                if s - lag < n:
                    part(s - lag, (s - lag) % 2)

    def skewed_flat(n, parts):
        depth = max(lag for _, lag in parts)
        for s in range(n + depth):
            for part, lag in parts:
                if 0 <= s - lag < n:
                    part(s - lag, (s - lag) % 2)

    def pair_of(o):
        return ps[:, 2 * (o % 2):2 * (o % 2) + 2, :]

    block = nc.Block()
    with block:

        @block.sync
        def _(sp):
            def slot_free(v, p):
                wait(sp, "w_lo_done", v - 1)

            def landed(p):
                return S(f"w_landed{p}")

            def w_plain(src, first):
                def load(v, p, t):
                    slot_free(v, p)
                    sp.dma_start(wraw[p][:, 0:KT, :], src[:, :, ds(t * P + first, P)]).then_inc(landed(p), 64)
                return load

            def w_query(v, p, t, half):
                slot_free(v, p)
                for r in range(2):
                    sp.dma_start(wraw[p][:, 0:KT, r * HEAD:(r + 1) * HEAD],
                                 w1[:, :, ds(t * HEAD + (c_q + (2 * half + r) * QR * HEAD), HEAD)]
                                 ).then_inc(landed(p), 32)

            def w_attn(v, p, t):
                slot_free(v, p)
                for r in range(2):
                    for g in range(2):
                        sp.dma_start(wraw[p][r * HEAD:(r + 1) * HEAD, g * QR:(g + 1) * QR, :],
                                     w_at[r, g][:, :, ds(t * P, P)]).then_inc(landed(p), 16)

            def w_ssd_half(v, p, t, j):
                slot_free(v, p)
                sp.dma_start(wraw[p][:, 0:KT, :], w_ssd[:, j, :, ds(t * P, P)]).then_inc(landed(p), 64)

            def w_ffn_part(v, p, t, j):
                slot_free(v, p)
                sp.dma_start(wraw[p][:, 0:FK[j], :], w_f2[:, FK0[j]:FK0[j] + FK[j], ds(t * P, P)]).then_inc(landed(p), 64)

            loads = {
                "dt": lambda v, p, t, j: w_plain(w1, c_dt)(v, p, t),
                "xbc": lambda v, p, t, j: w_plain(w1, c_xbc)(v, p, t),
                "kv": lambda v, p, t, j: w_plain(w1, c_k)(v, p, t),
                "q": None,
                "attn": lambda v, p, t, j: w_attn(v, p, t),
                "mix": lambda v, p, t, j: w_plain(w_mix, 0)(v, p, t),
            }

            def weights(stage_name, lo, hi, peel=False):
                load = loads[stage_name]
                u0 = U0[stage_name]

                def step(t, p):
                    load(t + u0, (p + u0) % 2, t, 0)
                pairs(sp, hi, step, first=lo, peel=peel)

            def small(dst, src):
                sp.dma_start(dst, src).then_inc(S("small_landed"), 16)

            weights("dt", 0, 1)
            sp.dma_start(norm_a[:], pre_mix_norm[0:1, :].to_broadcast((P, D))).then_inc(S("norm_landed"), 16)

            def x_load(t, p):
                wait(sp, "xn_done", t - 1)
                sp.dma_start(x_t[p][:], x_rows[ds(t, 1), :, :].rearrange("t p d -> p (t d)")).then_inc(S(f"tile_landed{p}"), 16)
            for t in range(2):
                x_load(t, t)
            pairs(sp, NT, x_load, first=2)
            with nc.allow_non_contiguous_dma(reason="a few KB of columns"):
                small(dtb[0:H, :], dt_bias_f.rearrange("a h -> h a"))
                small(dtb[H:2 * H, :], dt_bias_b.rearrange("a h -> h a"))
                small(alog[0:H, :], A_log_f.rearrange("a h -> h a"))
                small(alog[H:2 * H, :], A_log_b.rearrange("a h -> h a"))
                for j in range(taps):
                    small(cw[:, :, j], conv_w[0, j].rearrange("(t p) -> p t", p=P))
                small(cb[:], conv_b[0].rearrange("(t p) -> p t", p=P))
                small(ncol[:], ssd_norm[0].rearrange("(t p) -> p t", p=P))
                for r in range(2):
                    small(dcol[r * HEAD:(r + 1) * HEAD, :],
                          D_skip[0].rearrange("(t r) -> r t", r=2)[r:r + 1, :].to_broadcast((HEAD, NI)))
            small(sink[:], attn_sink[0:1, :].to_broadcast((P, QH)))

            weights("xbc", 0, NU["xbc"], peel=True)
            weights("kv", 0, NU["kv"])
            for half in range(2):
                def query_step(t, p, half=half):
                    v = t + (U0["q"] + half * QR)
                    w_query(v, (p + U0["q"]) % 2, t, half)
                pairs(sp, QR, query_step)

            with sp.Fori(0, NT) as b:
                for j in range(KV):
                    src = w_plain(w1, (c_z if j < 2 else c_gate) + (j % 2) * P)
                    src(b * KV + (U0["zg"] + j), (U0["zg"] + j) % 2, b * 2)

            wait(sp, "cum_stored", 16 * 2 * G)
            wait(sp, "zg_stored0", 16 + 8 * (NI + 2 * KT))
            wait(sp, "zg_stored1", 16 + 8 * (NI + 2 * KT))
            def attn_weights(t):
                for j in range(2):
                    w_attn(t + (U0["attn"] + j), (U0["attn"] + j) % 2, t + j)
            attn_weights(0)
            wait(sp, "o_done", KT)

            def ssd_loads(g, last=False):
                def back_load(i, p):
                    tok = ds(i * -CHUNK + (NT - 1) * CHUNK, CHUNK)
                    sp.wait_ge(S("x_read"), g * (2 * NT) + (i + 1))
                    sp.dma_start(xin[p][:], xbc_d[ds(g * XT, XT), :, tok].rearrange("t p l -> p t l")
                                 ).then_inc(S(f"back_landed{p}"), 16)
                    sp.dma_start(bin_[p][:], xbc_d[ds(g + NI, 1), :, tok].rearrange("t p l -> p (t l)")
                                 ).then_inc(S(f"back_landed{p}"), 16)
                pairs(sp, NT, back_load)
                for j in range(2):
                    sp.wait_ge(S(f"stored{j}"), g * 16 + ST["attn"])
                    sp.dma_start(gated[j][:], gate_d[ds(g * 2 + (KT + j), 1), :, :].rearrange("t p l -> p (t l)")
                                 ).then_inc(S(f"tile_landed{j}"), 16)

                def fwd_load(c, p):
                    n = g * NT + c
                    tok = ds(c * CHUNK, CHUNK)
                    sp.wait_ge(S("seg_exp"), n + 1)
                    sp.wait_ge(S("seg_f_done"), n + 1)
                    sp.wait_ge(S("seg_b_done"), n + 1)
                    sp.dma_start(cum_all[:].rearrange("p d r l -> p (d r l)"),
                                 cum_d[ds(g, 1), ds(c, 1)].rearrange("g c d r l -> (g c) (d r l)").to_broadcast((P, 2 * R * CHUNK))
                                 ).then_inc(S("seg_landed"), 16)
                    sp.wait_ge(S("c_read_dve"), n + 1)
                    sp.wait_ge(S("c_read_pool"), n + 1)
                    sp.dma_start(cin[p][:], xbc_d[ds(g + (NI + G), 1), :, tok].rearrange("t p l -> p (t l)")
                                 ).then_inc(S(f"fwd_landed{p}"), 16)
                    sp.wait_ge(S("x_read"), g * (2 * NT) + (c + (NT + 1)))
                    sp.dma_start(xin[p][:], xbc_d[ds(g * XT, XT), :, tok].rearrange("t p l -> p t l")
                                 ).then_inc(S(f"fwd_landed{p}"), 16)
                    sp.dma_start(bin_[p][:], xbc_d[ds(g + NI, 1), :, tok].rearrange("t p l -> p (t l)")
                                 ).then_inc(S(f"fwd_landed{p}"), 16)

                def z_load(c, p):
                    n = g * NT + c
                    tok = ds(c * CHUNK, CHUNK)
                    sp.wait_ge(S(f"y_stored{p}"), n * 8 + (16 - 8 * p))
                    sp.dma_start(zin[p][:], z_d[ds(g * XT, XT), :, tok].rearrange("t p l -> p t l")
                                 ).then_inc(S(f"z_landed{p}"), 16)
                skewed(sp, NT, [(fwd_load, 0), (z_load, 1)], between=None if last else lambda: attn_weights(g * 2 + 2))
            with sp.Fori(0, G - 1) as g:
                ssd_loads(g)
            ssd_loads(G - 1, last=True)

            for t in range(2):
                w_ssd_half(U0["ssd"] + t, (U0["ssd"] + t) % 2, 0, t)
            for j in range(2):
                wait(sp, f"y_stored{j}", 16 + 8 * G * NT)
                wait(sp, f"stored{j}", ST["attn end"])
            wait(sp, "h_fwd_done", G * NT + 1)

            def y_load(t, q):
                wait(sp, "y_lo_done", t - 3)
                wait(sp, "y_squared", t - 3)
                sp.dma_start(y_raw[q][:], y_d[ds(t, 1), :, :].rearrange("t p l -> p (t l)")).then_inc(S(f"y_landed{q}"), 16)
            fours(sp, NI, y_load)

            def merge_load(t):
                wait(sp, "merge_out", t)
                sp.dma_start(mga[:], gate_d[ds(t, 1), :, :].rearrange("t p l -> p (t l)")).then_inc(S("merge_landed"), 16)
                sp.dma_start(mat[:], attn_d[ds(t, 1), :, :].rearrange("t p l -> p (t l)")).then_inc(S("merge_landed"), 16)
            merge_load(0)
            with sp.Fori(1, KT) as t:
                for j in range(2):
                    w_ssd_half(t * 2 + (U0["ssd"] + j), (U0["ssd"] + j) % 2, t, j)
                merge_load(t)
            weights("mix", 0, 2)

            weights("mix", 2, KT)

            def mix_weights(t):
                v = U0["mix"] + KT + t
                w_plain(w_mix, 0)(v, v % 2, t)

            def ffn_in_weights(v, p, t, j):
                w_plain(w_f1, j * F)(v, p, t)

            def norm_load(src, add, n0, t):
                p = t % 2
                nf, nx = norm_bufs(n0)[0:2]
                wait(sp, "n_turned", t + (n0 - 1))
                for a in range(2):
                    sp.dma_start(nf[p][:, a, :].rearrange("p (k l) -> p k l", l=CHUNK),
                                 src[:, a * KT // 2:(a + 1) * KT // 2, t * CHUNK:(t + 1) * CHUNK]
                                 ).then_inc(S(f"n_f_landed{p}"), 16)
                wait(sp, "n_added", t + (n0 - 1))
                sp.dma_start(nx[p], two(add[t])).then_inc(S(f"n_x_landed{p}"), 16)
            mix_weights(0)
            mix_weights(1)
            wait(sp, "merge_out", KT)
            sp.dma_start(norm_a[:], post_mix_norm[0:1, :].to_broadcast((P, D))).then_inc(S("norm_landed"), 16)
            sp.dma_start(norm_b[:], pre_ffn_norm[0:1, :].to_broadcast((P, D))).then_inc(S("norm_landed"), 16)
            for j in range(2):
                wait(sp, f"stored{j}", ST["proj"] + 8 * KT)
            for t in range(NT // 2):
                mix_weights(t + 2)
                norm_load(proj_d, x_rows, 0, t)
            for t in range(NT // 2 + 2, KT):
                mix_weights(t)
            for j in range(2):
                ffn_in_weights(U0["ffn_in"] + j, (U0["ffn_in"] + j) % 2, 0, j)
            for j in range(2):
                wait(sp, f"stored{j}", ST["proj end"])
            for t in range(NT // 2, NT):
                norm_load(proj_d, x_rows, 0, t)

            def ffn_pair(t, last):
                for j in range(2):
                    ffn_in_weights(t * 2 + (U0["ffn_in"] + j), (U0["ffn_in"] + j) % 2, t, j)
            with sp.Fori(1, FT) as t:
                ffn_pair(t, False)
            def ffn_out_weights(t, p, half=0):
                for j in range(3):
                    w_ffn_part(t * 3 + (U0["ffn_out"] + 3 * KT * half + j), (U0["ffn_out"] + p + j) % 2, t, j)
            pairs(sp, KT, ffn_out_weights)

            ffn_out_weights(0, 0, half=1)
            ffn_out_weights(1, 1, half=1)
            sp.dma_start(norm_a[:], post_ffn_norm[0:1, :].to_broadcast((P, D))).then_inc(S("norm_landed"), 16)
            for j in range(2):
                wait(sp, f"stored{j}", ST["ffn"] + 8 * KT)
                wait(sp, f"x1_stored{j}", 16 * NT // 2)
            for t in range(NT // 2):
                ffn_out_weights(t + 2, t % 2, half=1)
                norm_load(ffn_d, x1_d, NT, t)
            for t in range(NT // 2 + 2, KT):
                ffn_out_weights(t, t % 2, half=1)
            for j in range(2):
                wait(sp, f"stored{j}", ST["ffn end"])
            for t in range(NT // 2, NT):
                norm_load(ffn_d, x1_d, NT, t)

        @block.gpsimd
        def _(pool):
            gp = nc.gpsimd
            pool.sem_inc(S("c_read_pool"), 2)
            pool.sem_inc(S("seg_b_done"), 1)
            pool.sem_inc(S("xdt_done"), 4)
            one = pool.to_reg(1.0)
            zero = pool.to_reg(0.0)
            masked = pool.to_reg(MASKED)

            def step(ins):
                step.n += 1
                ins.then_inc(S("const_step"), 1)
                pool.wait_ge(S("const_step"), step.n)
            step.n = 0
            gp.memset(ones[:], 1.0).then_inc(S("const_step"), 1)
            gp.memset(ident[:], 0.0).then_inc(S("const_step"), 1)
            step.n = 2
            pool.wait_ge(S("const_step"), 2)
            step(gp.affine_select(out=ident[:], in_=ident[:], pattern=[[-1, P]], compare_op=ALU.not_equal, fill=one,
                                  base=0, channel_multiplier=1))
            step(gp.affine_select(out=tri[:, 0, :], in_=ones[:], pattern=[[1, P]], compare_op=ALU.is_ge, fill=zero,
                                  base=0, channel_multiplier=-1))
            step(gp.affine_select(out=tri[:, 1, :], in_=ones[:], pattern=[[-1, P]], compare_op=ALU.is_ge, fill=zero,
                                  base=0, channel_multiplier=1))
            W3 = 3 * CHUNK
            for v in range(3):
                step(gp.iota(dist[:, v, :], pattern=[[-1, W3]], base=CHUNK, channel_multiplier=1,
                             allow_small_or_imprecise_dtypes=True))
            gp.memset(k_all[:, :, 0:CHUNK], 0.0).then_inc(S("pads_done"), 1)
            gp.memset(k_all[:, :, L + CHUNK:kwin], 0.0).then_inc(S("pads_done"), 1)
            gp.memset(v_all[:, 0, :], 0.0).then_inc(S("pads_done"), 1)
            gp.memset(v_all[:, NT + 1, :], 0.0).then_inc(S("pads_done"), 1)
            pool.wait_ge(S("dist_negated"), 1)
            for v in range(3):
                step(gp.affine_select(out=dist[:, v, :], in_=dist[:, v, :], pattern=[[1, W3]], compare_op=ALU.is_ge,
                                      fill=masked, base=WINDOW - CHUNK, channel_multiplier=-1))
                step(gp.affine_select(out=dist[:, v, :], in_=dist[:, v, :], pattern=[[-1, W3]], compare_op=ALU.is_ge,
                                      fill=masked, base=WINDOW + CHUNK, channel_multiplier=1))
            step(gp.affine_select(out=dist[:, 0, :], in_=dist[:, 0, :], pattern=[[1, W3]], compare_op=ALU.is_ge,
                                  fill=masked, base=-CHUNK, channel_multiplier=0))
            gp.affine_select(out=dist[:, 2, :], in_=dist[:, 2, :], pattern=[[-1, W3]], compare_op=ALU.is_ge,
                             fill=masked, base=2 * CHUNK - 1, channel_multiplier=0).then_inc(S("dist_done"), 1)

            pool.wait_ge(S("rows_done"), 2)
            for d in range(2):
                for g in range(G):
                    pool.dma_start(cum_d[g, :, d, :, :].rearrange("c r l -> r c l"),
                                   rows[d * H + g * R:d * H + (g + 1) * R, :, :]).then_inc(S("cum_stored"), 16)

            def store(dst, buf, done, n0=0):
                def s(t, p):
                    pool.wait_ge(S(done), t + (n0 + 1))
                    pool.dma_start(dst(t), buf[p][:]).then_inc(S(f"stored{p}"), 16)
                return s

            def tile_of(d):
                return lambda t: d[ds(t, 1), :, :].rearrange("t p l -> p (t l)")
            pairs(pool, conv_dim // P, store(tile_of(xbc_d), stage, "xbc_out"))

            def diagonals(b, j):
                pool.wait_ge(S("rden_done"), b * KV + (j + 1))
                pool.wait_ge(S("p_turned"), b * KV + (j + 1))
                gp.tensor_tensor(rdiag[:], ident[:].unsqueeze(1).to_broadcast((P, QR, CHUNK)),
                                 soft[:, j % 2, 4, :].unsqueeze(2).to_broadcast((P, QR, CHUNK)), ALU.mult
                                 ).then_inc(S("rdiag_done"), 1)

            def attn_block(b):
                diagonals(b, 0)
                wait(pool, "pv_done", b * KV + 1)
                gp.tensor_copy(v_win[:], v_all[:, ds(b, 3), :]).then_inc(S("v_win_done"), 1)
                for j in range(1, KV):
                    diagonals(b, j)
            pool.wait_ge(S("pads_done"), 4)
            pool.wait_ge(S("v_turned"), NT)
            attn_block(0)
            with pool.Fori(1, NT) as b:
                attn_block(b)

            def heads(tab, d, c, g):
                return tab[:, d, ds(c, 1), ds(g * R, R)].rearrange("p c r -> p (c r)")

            def wide(ap, n):
                return ap.unsqueeze(2).to_broadcast((P, R, n))
            pool.wait_ge(S("o_done"), KT)
            gp.memset(h_back[:, NT, :], 0.0).then_inc(S("h_zero"), 1)
            pool.wait_ge(S("h_zero"), 1)
            with pool.Fori(0, G) as g:
                def back(i, p):
                    m = g * NT + i
                    c = i * -1 + (NT - 1)
                    pool.wait_ge(S("h_fwd_done"), g * NT + 1)
                    pool.wait_ge(S("h_back_done"), m + 1)
                    gp.tensor_tensor(h_tmp[:], h_back[:, ds(c + 1, 1), :].rearrange("p c (r e) -> p (c r) e", e=HEAD),
                                     wide(heads(dec, 1, c, g), HEAD), ALU.mult).then_inc(S("h_decayed"), 1)
                pairs(pool, NT, back)

                def fwd_a(c, p):
                    n = g * NT + c
                    pool.wait_ge(S("y_done"), n + 1)
                    pool.wait_ge(S("seg_landed"), n * 16 + 16)
                    gp.tensor_tensor(seg[p][:, 1, :, :], cum_all[:, 1, :, :], wide(heads(acum, 1, c, g), CHUNK), ALU.subtract
                                     ).then_inc(S("seg_b_done"), 1)
                    pool.wait_ge(S(f"fwd_landed{p}"), g * (48 * NT // 2) + (c * 24 + (48 - 24 * p)))
                    pool.wait_ge(S("seg_exp"), n + 2)
                    gp.tensor_tensor(cdec[p][:, 1, :, :], cdec[p][:, 1, :, :], cin[p][:].unsqueeze(1).to_broadcast((P, R, CHUNK)),
                                     ALU.mult).then_inc(S("c_read_pool"), 1)
                    pool.wait_ge(S("xtok_done"), n + 2)
                    for d in range(2):
                        gp.tensor_tensor(xdt[p][:, d, :, :], xtok[p][:], wide(heads(dtok, d, c, g), HEAD), ALU.mult
                                         ).then_inc(S("xdt_done"), 1)
                    gp.tensor_tensor(xend[p][:], xtok[p][:], wide(heads(wend, 0, c, g), HEAD), ALU.mult
                                     ).then_inc(S("xdt_done"), 1)
                pairs(pool, NT, fwd_a)
                for j in range(2):
                    pool.wait_ge(S("attn_gated"), g * 2 + (j + 2))
                    pool.dma_start(attn_d[ds(g * 2 + j, 1), :, :].rearrange("t p l -> p (t l)"), gated[j][:]
                                   ).then_inc(S(f"stored{j}"), 16)

            def proj_store(t, p, half=0):
                pool.wait_ge(S("proj_out"), t + (half * KT + 1))
                pool.dma_start(proj_d[:, ds(t, 1), half * HALF:(half + 1) * HALF].rearrange("p t l -> p (t l)"), pout[p][:]
                               ).then_inc(S(f"stored{p}"), 16)

            def row_store(dst, n0, name):
                def s(t, p):
                    pool.wait_ge(S("n_added"), t + (n0 + 1))
                    pool.dma_start(two(dst[t]), norm_bufs(n0)[2][p]).then_inc(S(f"{name}_stored{p}"), 16)
                return s

            def ffn_store(t, p, half=0):
                pool.wait_ge(S("ffn_out_done"), t + (half * KT + 1))
                pool.dma_start(ffn_d[:, ds(t, 1), half * HALF:(half + 1) * HALF].rearrange("p t l -> p (t l)"),
                               fout[p][:]).then_inc(S(f"stored{p}"), 16)
            pairs(pool, KT, proj_store)
            beside(norm_turns([(row_store(x1_d, 0, "x1"), 0)]), NT, lambda t: proj_store(t, t % 2, 1))
            pairs(pool, KT, ffn_store)
            beside(norm_turns([(row_store(out_rows, NT, "out"), 0)]), NT, lambda t: ffn_store(t, t % 2, 1))
            pool.wait_ge(S("out_stored0"), 16 * NT // 2)
            pool.wait_ge(S("out_stored1"), 16 * NT // 2)

        @block.scalar
        def _(act):
            sc = nc.scalar

            def w_hi(v, p, kt=KT):
                act.wait_ge(S(f"w_landed{p}"), (v - p) * 32 + 64)
                wait(act, "mm_done", v - 1)
                sc.copy(whi[p][:, 0:kt, :], wraw[p][:, 0:kt, :]).then_inc(S("w_hi_done"), 1)

            def ahead(name, work, n=None, first=0):
                u0 = U0[name]

                def step(t, p):
                    w_hi(t + (u0 + 1), (p + u0 + 1) % 2)
                    work(t, p)
                pairs(act, NU[name] if n is None else n, step, first=first)

            def unit_done(name, t, per=1):
                act.wait_ge(S("mm_done"), t * per + (U0[name] + per))

            def out_ps(name, p):
                return pair_of(O0[name] + p)

            for name in ("pT_done", "seg_exp", "hb_done", "back_btok", "fwd_btok", "g_done", "xtok_done"):
                act.sem_inc(S(name), 1)
            w_hi(0, 0)

            def sq_x(t, p):
                act.wait_ge(S(f"tile_landed{p}"), (t - p) * 8 + 16)
                sc.activation(junk[:], x_t[p][:], ACT.Square, accum_out=stat[:, p, 0:1]).then_inc(S("n_squared"), 1)
                act.wait_ge(S("n_mean"), t + 1)
                sc.activation(stat[:, p, 2:3], stat[:, p, 1:2], ACT.Sqrt).then_inc(S("n_root"), 1)

            def hi_h(t, p):
                act.wait_ge(S("x_turned"), t + 1)
                sc.copy(act_hi[:, :, ds(t * CHUNK, CHUNK)],
                        ps[:, 2 * p:2 * p + 2, :].rearrange("p a (b l) -> p (a b) l", l=CHUNK)).then_inc(S("h_hi_done"), 1)
            skewed(act, NT, [(sq_x, 0), (hi_h, 1)])

            HH = 2 * H
            w_hi(1, 1)
            act.wait_ge(S("small_landed"), 16 * (4 + taps + 2 + 2 + 1))
            act.wait_ge(S("mm_done"), 1)
            sc.activation(dt_v[0:HH, :], ps[0:HH, 0:2, :].rearrange("p a l -> p (a l)"), ACT.Identity, bias=dtb[0:HH, :]
                          ).then_inc(S("moved"), 1)
            sc.activation(alog[0:HH, :], alog[0:HH, :], ACT.Exp).then_inc(S("dt_act"), 1)
            act.wait_ge(S("dt_dve"), 1)
            sc.activation(dt_e[0:HH, :], dt_e[0:HH, :], ACT.Exp).then_inc(S("dt_act"), 1)
            w_hi(2, 0)
            act.wait_ge(S("dt_turned"), 1)
            sc.copy(dtok[:], ps[:, 4, :].rearrange("p (c d h) -> p d c h", c=NT, d=2)).then_inc(S("dt_tok"), 1)
            sc.copy(atok[:].rearrange("p c d h -> p (c d h)"), ps[:, 5, :]).then_inc(S("dt_tok"), 1)
            act.wait_ge(S("dt_summed"), 1)
            sc.copy(acum[:].rearrange("p d c h -> p (d c h)"), ps[:, 6, :]).then_inc(S("acum_done"), 1)
            act.wait_ge(S("dt_dve_tok"), 1)
            sc.activation(dec[:].rearrange("p d c h -> p (d c h)"), ps[:, 7, :], ACT.Exp).then_inc(S("tables_done"), 1)
            sc.activation(wend[:].rearrange("p d c h -> p (d c h)"), ddif[:].rearrange("p d c h -> p (d c h)"), ACT.Exp
                          ).then_inc(S("tables_done"), 1)
            act.wait_ge(S("rows_summed"), 1)
            psr = ps[:, 4:8, :].rearrange("p a (c d l) -> p (a c) d l", d=2, l=CHUNK)
            for d in range(2):
                sc.copy(rows[d * H:(d + 1) * H, :, :], psr[d * H:(d + 1) * H, :, d, :]).then_inc(S("rows_done"), 1)

            NX = conv_dim // P

            def xbc_raw(t, p):
                if not (isinstance(t, int) and t == 0):
                    w_hi(t + (U0["xbc"] + 1), (p + U0["xbc"] + 1) % 2)
                unit_done("xbc", t)
                wait(act, "conv_done", t - 1)
                sc.copy(praw[p][:, pad:pad + L], out_ps("xbc", p).rearrange("p a l -> p (a l)")).then_inc(S("moved"), 1)

            def xbc_silu(t, p):
                act.wait_ge(S("conv_done"), t + 1)
                wait(act, f"stored{p}", (t - p) * 8)
                sc.activation(stage[p][:], cacc[p][:], ACT.Silu).then_inc(S("xbc_out"), 1)
            act.wait_ge(S("praw_zeroed"), 4)
            skewed(act, NX, [(xbc_raw, 0), (xbc_silu, 1)], lead=4)

            for t in range(KV):
                w_hi(t + U0["kv"] + 1, (t + U0["kv"] + 1) % 2)
                unit_done("kv", t)
                if t < KV // 2:
                    sc.copy(k_all[:, t, CHUNK:CHUNK + L], out_ps("kv", t % 2).rearrange("p a l -> p (a l)")
                            ).then_inc(S("moved"), 1)
                else:
                    if t == KV // 2:
                        act.wait_ge(S("stored0"), ST["xbc end"])
                        act.wait_ge(S("stored1"), ST["xbc end"])
                    sc.copy(stage[t % 2][:], out_ps("kv", t % 2).rearrange("p a l -> p (a l)")).then_inc(S("moved"), 1)

            def q_work(t, p):
                unit_done("q", t)
                sc.copy(qT[:, ds(t, 1), :].rearrange("p t l -> p (t l)"),
                        out_ps("q", p).rearrange("p a l -> p (a l)")).then_inc(S("moved"), 1)
            act.wait_ge(S("cum_stored"), 16 * 2 * G)
            ahead("q", q_work)

            def zg_unit(b, j):
                t = b * KV + j
                p = j % 2
                act.wait_ge(S("mm_done"), t + (U0["zg"] + 1))
                act.wait_ge(S(f"zg_stored{p}"), (t - p) * 8 + 16)
                sc.activation(stage[p][:], ps[:, 0:2, :].rearrange("p a l -> p (a l)"), ACT.Silu if j < 2 else ACT.Sigmoid
                              ).then_inc(S("moved"), 1)
                act.wait_ge(S("moved"), t + (O0["zg"] + 1))
                act.dma_start((z_d if j < 2 else gate_d)[ds(b * 2 + p, 1), :, :].rearrange("t p l -> p (t l)"), stage[p][:]
                              ).then_inc(S(f"zg_stored{p}"), 16)

            def stage_q(b):
                wait(act, "scored", b * QH)
                sc.copy(qs_hi[:], qT[:, :, ds(b * CHUNK, CHUNK)]).then_inc(S("qs_hi_done"), 1)
                sc.copy(k_hi[:], k_all[:, :, ds(b * CHUNK, 3 * CHUNK)]).then_inc(S("qs_hi_done"), 1)

            def exps(b, j):
                q = j % 2
                act.wait_ge(S("max_done"), b * KV + (j + 1))
                for r in range(QR):
                    sc.activation(prob[q][:, r, :], prob[q][:, r, :], ACT.Exp, bias=soft[:, q, 2, r:r + 1], scale=SCALE,
                                  accum_out=soft[:, q, 3, r:r + 1]).then_inc(S("exp_done"), 1)
                sc.activation(soft[:, q, 5, :], soft[:, q, 5, :], ACT.Exp).then_inc(S("exp_done"), 1)

            def move_pT(b, j):
                act.wait_ge(S("p_turned"), b * KV + (j + 2))
                act.wait_ge(S("pv_done"), b * KV + j + 1)
                sc.copy(probT[:], ps[:, 4:7, :]).then_inc(S("pT_done"), 1)

            act.wait_ge(S("moved"), O0["zg"])
            act.wait_ge(S("v_turned"), NT)
            for j in range(2):
                act.sem_inc(S(f"zg_stored{j}"), 16)
            stage_q(0)
            exps(0, 0)

            def act_block(b, last=False):
                for j in range(KV):
                    if j == 2 and not last:
                        stage_q(b + 1)
                    if not (last and j == KV - 1):
                        w_hi(b * KV + (U0["zg"] + j + 1), (U0["zg"] + j + 1) % 2)
                    if j < KV - 1:
                        exps(b, j + 1)
                    elif not last:
                        exps(b + 1, 0)
                    move_pT(b, j)
                    zg_unit(b, j)
            with act.Fori(0, NT - 1) as b:
                act_block(b)
            act_block(NT - 1, True)

            act.wait_ge(S("o_moved"), 2 * NT + 1)
            act.wait_ge(S("pv_done"), KV * NT + 1)

            def o_hi(t, p):
                sc.copy(act_hi[:, ds(t, 1), :], qT[:, ds(t, 1), :]).then_inc(S("o_hi_done"), 1)
            pairs(act, KT, o_hi)

            act.wait_ge(S("o_done"), KT)
            for j in range(2):
                act.sem_inc(S(f"y_stored{j}"), 16)
            w_hi(U0["attn"], U0["attn"] % 2)

            def ssd_group(g, last=False):
                act.wait_ge(S("y_done"), g * NT + 2)

                def back(i, p):
                    m = g * NT + i
                    act.wait_ge(S("x_read"), g * (2 * NT) + (i + 3))
                    act.wait_ge(S("back_state"), m + 1)
                    sc.copy(btok[p][:], ps[:, 1, 0:STATE]).then_inc(S("back_btok"), 1)
                pairs(act, NT, back)
                w_hi(g * 2 + (U0["attn"] + 1), (U0["attn"] + 1) % 2)

                def fwd_exp(c, p):
                    n = g * NT + c
                    act.wait_ge(S("seg_landed"), n * 16 + 16)
                    act.wait_ge(S("y_done"), n + 1)
                    sc.activation(cdec[p][:].rearrange("p d r l -> p (d r l)"), cum_all[:].rearrange("p d r l -> p (d r l)"),
                                  ACT.Exp).then_inc(S("seg_exp"), 1)
                    act.wait_ge(S("fwd_turned"), n + 1)
                    act.wait_ge(S("h_back_done"), g * NT + NT + 1)
                    act.wait_ge(S("xdt_done"), g * (3 * NT) + c * 3 + 1)
                    sc.copy(xtok[p][:].rearrange("p r e -> p (r e)"), ps[:, 0, :]).then_inc(S("xtok_done"), 1)
                    act.wait_ge(S("fwd_state"), n + 1)
                    sc.copy(btok[p][:], ps[:, 1, 0:STATE]).then_inc(S("fwd_btok"), 1)
                    sc.copy(hb_now[p][:].rearrange("p r e -> p (r e)"),
                            h_back[:, ds(c + 1, 1), :].rearrange("p c e -> p (c e)")).then_inc(S("hb_done"), 1)

                def fwd_mask(c, p):
                    n = g * NT + c
                    act.wait_ge(S("arg_done"), n + 1)
                    sc.activation(seg[p][:, 0, :, :], seg[p][:, 0, :, :], ACT.Exp).then_inc(S("decay_done"), 1)

                def y_store(c, p):
                    n = g * NT + c
                    act.wait_ge(S("y_gated"), n + 3)
                    act.dma_start(y_d[ds(g * XT, XT), :, ds(c * CHUNK, CHUNK)].rearrange("t p l -> p t l"), zin[p][:]
                                  ).then_inc(S(f"y_stored{p}"), 16)
                skewed(act, NT, [(fwd_exp, 0), (y_store, 2), (fwd_mask, 0)], lead=4,
                       between=None if last else lambda: w_hi(g * 2 + (U0["attn"] + 2), U0["attn"] % 2))
            with act.Fori(0, G - 1) as g:
                ssd_group(g)
            ssd_group(G - 1, last=True)
            w_hi(U0["ssd"], U0["ssd"] % 2)
            w_hi(U0["ssd"] + 1, (U0["ssd"] + 1) % 2)

            act.wait_ge(S("y_gated"), G * NT + 2)
            act.wait_ge(S("y_done"), G * NT + 2)
            act.wait_ge(S("h_fwd_done"), G * NT + 1)
            act.wait_ge(S("attn_gated"), KT + 1)

            def y_hi_step(t, q):
                act.wait_ge(S(f"y_landed{q}"), (t - q) * 4 + 16)
                sc.activation(y_hi[:, ds(t, 1), :].rearrange("p t l -> p (t l)"), y_raw[q][:], ACT.Copy,
                              scale=ncol[:, ds(t, 1)]).then_inc(S("y_hi_done"), 1)
                wait(act, "sq_summed", t - 1)
                sc.activation(y_sq[q % 2][:], y_raw[q][:], ACT.Square).then_inc(S("y_squared"), 1)
            fours(act, NI, y_hi_step)
            act.wait_ge(S("sq_mean"), 1)
            sc.activation(yscale[:], yscale[:], ACT.Sqrt).then_inc(S("y_root"), 1)
            with act.Fori(0, KT) as t:
                w_hi(t * 2 + (U0["ssd"] + 2), U0["ssd"] % 2)
                w_hi(t * 2 + (U0["ssd"] + 3), (U0["ssd"] + 1) % 2)

            act.wait_ge(S("mm_done"), U0["mix"])
            act.wait_ge(S("merge_out"), KT)

            def split_m(t, p):
                sc.copy(m_hi[:, ds(t, 1), :], merged[:, ds(t, 1), :]).then_inc(S("mix_hi_done"), 1)
            pairs(act, KT, split_m)

            def n_a(n0):
                def part(t, p):
                    act.wait_ge(S("n_turned"), t + (n0 + 1))
                    sc.activation(norm_bufs(n0)[4], ps[:, 2:4, :], ACT.Square, accum_out=stat[:, p, 0:1]
                                  ).then_inc(S("n_squared"), 1)
                    act.wait_ge(S("n_mean"), t + (n0 + NT + 1))
                    sc.activation(stat[:, p, 2:3], stat[:, p, 1:2], ACT.Sqrt).then_inc(S("n_root"), 1)
                return part

            def n_b(t, p):
                act.wait_ge(S("n_added"), t + 1)
                sc.activation(norm_bufs(0)[4], norm_bufs(0)[2][p], ACT.Square, accum_out=stat[:, p, 4:5]
                              ).then_inc(S("n2_squared_b"), 1)
                act.wait_ge(S("n2_mean_b"), t + 1)
                sc.activation(stat[:, p, 6:7], stat[:, p, 5:6], ACT.Sqrt).then_inc(S("n2_root_b"), 1)

            def n_c(t, p):
                act.wait_ge(S("h2_turned"), t + 1)
                sc.copy(h2_hi[:, :, ds(t * CHUNK, CHUNK)],
                        ps[:, 4 + 2 * p:6 + 2 * p, :].rearrange("p a (b l) -> p (a b) l", l=CHUNK)
                        ).then_inc(S("h2_hi_done"), 1)

            def p_step(t, p, half=0):
                m = t + half * KT
                if not (half and t == KT - 1):
                    w_hi(m + (U0["mix"] + 2), (p + U0["mix"]) % 2)
                act.wait_ge(S("mm_done"), m + (U0["mix"] + 1))
                wait(act, f"stored{p}", (m - p) * 8 + ST["proj"])
                sc.copy(pout[p][:], ps[:, (O0["mix"] + p) % 2, :]).then_inc(S("proj_out"), 1)
            pairs(act, KT, p_step)
            beside(norm_turns([(n_c, 3), (n_b, 1), (n_a(0), 0)]), NT + 3, lambda t: p_step(t, t % 2, 1))

            def f_step(t, last=False):
                wait(act, "gact_read", t + 1)
                act.wait_ge(S("mm_done"), t * 2 + (U0["ffn_in"] + 1))
                sc.activation(gact[:], pair_of(O0["ffn_in"]).rearrange("p a l -> p (a l)"), ACT.Silu).then_inc(S("g_done"), 1)

            w_hi(U0["ffn_in"] + 1, (U0["ffn_in"] + 1) % 2)
            with act.Fori(0, FT - 1) as t:
                f_step(t)
                w_hi(t * 2 + (U0["ffn_in"] + 2), U0["ffn_in"] % 2)
                w_hi(t * 2 + (U0["ffn_in"] + 3), (U0["ffn_in"] + 1) % 2)
            f_step(FT - 1)
            w_hi(U0["ffn_out"], U0["ffn_out"] % 2, FK[0])
            w_hi(U0["ffn_out"] + 1, (U0["ffn_out"] + 1) % 2, FK[1])
            act.wait_ge(S("mm_done"), U0["ffn_out"])
            act.wait_ge(S("gact_read"), FT + 1)
            for half in range(2):
                def split_f(dst, k0, k1, half=half):
                    with act.Fori(k0, k1) as k:
                        sc.copy(dst[:, ds(k, 1), :], f_act[:, ds(k, 1), half * HALF:(half + 1) * HALF]
                                ).then_inc(S("f_hi_done"), 1)
                if half == 0:
                    split_f(f_hi, 0, FT)
                else:
                    act.wait_ge(S("mm_done"), U0["ffn_out"] + 3 * KT)
                    split_f(f_hi, KT, FT)

                def ffn_work(t, p, half=half):
                    act.wait_ge(S("mm_done"), t * 3 + (U0["ffn_out"] + 3 * KT * half + 3))
                    wait(act, f"stored{p}", (t - p) * 8 + (ST["ffn"] + 8 * KT * half))
                    sc.copy(fout[p][:], ps[:, (O0["ffn_out"] + p) % 2, :]).then_inc(S("ffn_out_done"), 1)

                def ffn_hi(t, p, j, half=half):
                    w_hi(t * 3 + (U0["ffn_out"] + 3 * KT * half + j), (U0["ffn_out"] + p + j) % 2, FK[j % 3])

                def ffn_step(t, p, last=False):
                    ffn_hi(t, p, 2)
                    if not last:
                        ffn_hi(t, p, 3)
                    ffn_work(t, p)
                    if not last:
                        ffn_hi(t, p, 4)
                if half == 0:
                    for t in range(2):
                        ffn_step(t, t)
                    split_f(f_hi2, 0, KT, half=1)
                    pairs(act, KT, ffn_step, first=2)
                else:
                    beside(norm_turns([(n_a(NT), 0)]), NT, lambda t: ffn_step(t, t % 2, last=t == KT - 1))

        @block.vector
        def _(dve):
            ve = nc.vector
            dve.sem_inc(S("c_read_dve"), 2)
            dve.sem_inc(S("y_gated"), 2)
            for name in ("seg_f_done", "o_moved", "attn_gated", "gact_read", "h_fwd_done", "back_x", "gm_done",
                         "h_back_done", "h2_lo_done"):
                dve.sem_inc(S(name), 1)

            def w_low(v, p, kt=KT):
                dve.wait_ge(S("w_hi_done"), v + 1)
                ve.tensor_tensor(wlo[p][:, 0:kt, :], wraw[p][:, 0:kt, :], whi[p][:, 0:kt, :].bitcast(F32), ALU.subtract
                                 ).then_inc(S("w_lo_done"), 1)

            def ahead(name, work, n=None, first=0):
                u0 = U0[name]

                def step(t, p):
                    w_low(t + (u0 + 1), (p + u0 + 1) % 2)
                    work(t, p)
                pairs(dve, NU[name] if n is None else n, step, first=first)

            def out_ps(name, p):
                return pair_of(O0[name] + p)

            w_low(0, 0)

            dve.wait_ge(S("norm_landed"), 16)

            def mean(dst, src, done):
                ve.tensor_scalar(dst, src, 1.0 / D, EPS, ALU.mult, ALU.add).then_inc(S(done), 1)

            def x_norm(t, p):
                dve.wait_ge(S("n_squared"), t + 1)
                mean(stat[:, p, 1:2], stat[:, p, 0:1], "n_mean")
                dve.wait_ge(S("n_root"), t + 1)
                ve.reciprocal(stat[:, p, 3:4], stat[:, p, 2:3]).then_inc(S("n_rstd"), 1)
                dve.wait_ge(S("n_rstd"), t + 1)
                wait(dve, "x_turned", t - 1)
                ve.scalar_tensor_tensor(x_n[p][:], x_t[p][:], stat[:, p, 3:4], norm_a[:], ALU.mult, ALU.mult
                                        ).then_inc(S("xn_done"), 1)

            def h_low(t, p):
                dve.wait_ge(S("h_hi_done"), t + 1)
                cols = ds(t * CHUNK, CHUNK)
                ve.tensor_tensor(act_lo[:, :, cols], ps[:, 2 * p:2 * p + 2, :].rearrange("p a (b l) -> p (a b) l", l=CHUNK),
                                 act_hi[:, :, cols].bitcast(F32), ALU.subtract).then_inc(S("h_done"), 1)
            skewed(dve, NT, [(x_norm, 0), (h_low, 1)])

            HH = 2 * H
            w_low(1, 1)
            dve.wait_ge(S("small_landed"), 16 * (4 + taps + 2 + 2 + 1))
            count = [0]

            def link(ins):
                count[0] += 1
                ins.then_inc(S("dt_dve"), 1)
                dve.wait_ge(S("dt_dve"), count[0])
            for j in range(2):
                ve.memset(praw[j][:, 0:pad], 0.0).then_inc(S("praw_zeroed"), 1)
                ve.memset(praw[j][:, pad + L:], 0.0).then_inc(S("praw_zeroed"), 1)
            dve.wait_ge(S("moved"), 1)
            v_, e_, t_, t2_, q_, r_ = (a[0:HH, :] for a in (dt_v, dt_e, dt_t, dt_t2, dt_q, dt_r))
            link(ve.scalar_tensor_tensor(e_, v_, -1.0, v_, ALU.mult, ALU.min))
            dve.wait_ge(S("dt_act"), 2)
            link(ve.tensor_scalar(r_, e_, 2.0, None, ALU.add))
            w_low(2, 0)
            link(ve.reciprocal(q_, r_))
            link(ve.tensor_tensor(t_, e_, q_, ALU.mult))
            link(ve.tensor_tensor(t2_, t_, t_, ALU.mult))
            link(ve.tensor_scalar(q_, t2_, 1.0 / (2 * LOG1P_TERMS + 1), None, ALU.mult))
            for k in range(LOG1P_TERMS - 1, 0, -1):
                link(ve.scalar_tensor_tensor(q_, q_, 1.0 / (2 * k + 1), t2_, ALU.add, ALU.mult))
            link(ve.scalar_tensor_tensor(q_, q_, 1.0, t_, ALU.add, ALU.mult))
            link(ve.tensor_scalar(r_, v_, 0.0, None, ALU.max))
            link(ve.scalar_tensor_tensor(v_, q_, 2.0, r_, ALU.mult, ALU.add))
            ve.tensor_scalar(e_, v_, alog[0:HH, :], -1.0, ALU.mult, ALU.mult).then_inc(S("dt_ready"), 1)
            dve.wait_ge(S("const_step"), 8)
            ve.scalar_tensor_tensor(dist[:].rearrange("p v k -> p (v k)"), dist[:].rearrange("p v k -> p (v k)"), -1.0,
                                    dist[:].rearrange("p v k -> p (v k)"), ALU.mult, ALU.min).then_inc(S("dist_negated"), 1)
            dve.wait_ge(S("acum_done"), 1)
            flat = "p d c h -> p (d c h)"
            ve.tensor_tensor(ddif[:].rearrange(flat), ps[:, 7, :], acum[:].rearrange(flat), ALU.subtract
                             ).then_inc(S("dt_dve_tok"), 1)
            dve.wait_ge(S("tables_done"), 2)
            ve.tensor_tensor(wend[:].rearrange(flat), wend[:].rearrange(flat), dtok[:].rearrange(flat), ALU.mult
                             ).then_inc(S("wend_done"), 1)

            NX = conv_dim // P

            def conv_w_ahead(t, p):
                if not (isinstance(t, int) and t == 0):
                    w_low(t + (U0["xbc"] + 1), (p + U0["xbc"] + 1) % 2)

            def conv(t, p):
                dve.wait_ge(S("moved"), t + 2)
                wait(dve, "xbc_out", t - 1)
                ve.tensor_scalar(cacc[p][:], praw[p][:, 0:L], cw[:, ds(t, 1), 0:1].rearrange("p t a -> p (t a)"),
                                 cb[:, ds(t, 1)], ALU.mult, ALU.add).then_inc(S("conv_step"), 1)
                for j in range(1, taps):
                    dve.wait_ge(S("conv_step"), t * (taps - 1) + j)
                    ins = ve.scalar_tensor_tensor(cacc[p][:], praw[p][:, j:j + L],
                                                  cw[:, ds(t, 1), j:j + 1].rearrange("p t a -> p (t a)"), cacc[p][:],
                                                  ALU.mult, ALU.add)
                    if j < taps - 1:
                        ins.then_inc(S("conv_step"), 1)
                    else:
                        ins.then_inc(S("conv_done"), 1)
            skewed(dve, NX, [(conv_w_ahead, 0), (conv, 1)], lead=4)

            for t in range(KV):
                w_low(t + U0["kv"] + 1, (t + U0["kv"] + 1) % 2)

            def v_move(t, p):
                dve.wait_ge(S("v_turn"), t + 1)
                ve.tensor_copy(v_all[:, ds(t + 1, 1), :].rearrange("p t e -> p (t e)"), ps[:, 4 + p, 0:kv_dim]
                               ).then_inc(S("v_turned"), 1)
            for t in range(NT):
                v_move(t, t % 2)
            ahead("q", lambda t, p: None)

            def low_q(b):
                dve.wait_ge(S("qs_hi_done"), b * 2 + 1)
                ve.tensor_tensor(qs_lo[:], qT[:, :, ds(b * CHUNK, CHUNK)], qs_hi[:].bitcast(F32), ALU.subtract
                                 ).then_inc(S("qs_done"), 1)
                dve.wait_ge(S("qs_hi_done"), b * 2 + 2)
                ve.tensor_tensor(k_lo[:], k_all[:, :, ds(b * CHUNK, 3 * CHUNK)], k_hi[:].bitcast(F32), ALU.subtract
                                 ).then_inc(S("qs_done"), 1)

            def maxima(b, j, variant):
                q = j % 2
                if not (isinstance(b, int) and b == 0 and j < 2):
                    dve.wait_ge(S("p_turned"), b * KV + j)
                for r in range(QR):
                    slope = 2.0 ** (-8.0 * (j * QR + r + 1) / QH)
                    dve.wait_ge(S("scored"), b * QH + (j * QR + r + 1))
                    ve.scalar_tensor_tensor(prob[q][:, r, :], dist[:, variant, :], slope / SCALE, ps[:, 2 + r % 2, 0:3 * CHUNK],
                                            ALU.mult, ALU.add).then_inc(S("biased"), 1)
                dve.wait_ge(S("biased"), b * QH + (j * QR + QR))
                ve.tensor_reduce(soft[:, q, 0, :], prob[q][:], AX_X, ALU.max).then_inc(S("max_step"), 1)
                n = b * (3 * KV) + 3 * j
                dve.wait_ge(S("max_step"), n + 1)
                ve.scalar_tensor_tensor(soft[:, q, 1, :], soft[:, q, 0, :], SCALE, sink[:, j * QR:(j + 1) * QR],
                                        ALU.mult, ALU.max).then_inc(S("max_step"), 1)
                dve.wait_ge(S("max_step"), n + 2)
                ve.tensor_scalar(soft[:, q, 2, :], soft[:, q, 1, :], -1.0, None, ALU.mult).then_inc(S("max_step"), 1)
                ve.tensor_tensor(soft[:, q, 5, :], sink[:, j * QR:(j + 1) * QR], soft[:, q, 1, :], ALU.subtract
                                 ).then_inc(S("max_done"), 1)

            def denominators(b, j):
                q = j % 2
                dve.wait_ge(S("exp_done"), b * (KV * (QR + 1)) + (j + 1) * (QR + 1))
                ve.tensor_tensor(soft[:, q, 3, :], soft[:, q, 3, :], soft[:, q, 5, :], ALU.add).then_inc(S("den_done"), 1)
                dve.wait_ge(S("den_done"), b * KV + (j + 1))
                ve.reciprocal(soft[:, q, 4, :], soft[:, q, 3, :]).then_inc(S("rden_done"), 1)

            def move_o(b, g):
                dve.wait_ge(S("pv_done"), b * KV + 2 * (g + 1) + 1)
                ve.tensor_copy(qT[:, g * QR:(g + 1) * QR, ds(b * CHUNK, CHUNK)],
                               ps[:, 7, :].rearrange("p (r l) -> p r l", r=QR)).then_inc(S("o_moved"), 1)

            dve.wait_ge(S("dist_done"), 1)
            low_q(0)
            maxima(0, 0, 0)

            def dve_block(b, variant, after):
                for j in range(KV):
                    if j < KV - 1:
                        maxima(b, j + 1, variant)
                    elif after is not None:
                        maxima(b + 1, 0, after)
                    denominators(b, j)
                    if j == 2 and after is not None:
                        low_q(b + 1)
                    if j < KV - 1 or after is not None:
                        w_low(b * KV + (U0["zg"] + j + 1), (U0["zg"] + j + 1) % 2)
                    if j == 0 and not (isinstance(b, int) and b == 0):
                        move_o(b - 1, 1)
                    if j == 2:
                        move_o(b, 0)
            dve_block(0, 0, 1)
            with dve.Fori(1, NT - 2) as b:
                dve_block(b, 1, 1)
            dve_block(NT - 2, 1, 2)
            dve_block(NT - 1, 2, None)
            move_o(NT - 1, 1)

            def o_low(t, p):
                dve.wait_ge(S("o_hi_done"), t + 1)
                ve.tensor_tensor(act_lo[:, ds(t, 1), :], qT[:, ds(t, 1), :], act_hi[:, ds(t, 1), :].bitcast(F32), ALU.subtract
                                 ).then_inc(S("o_done"), 1)
            pairs(dve, KT, o_low)

            def attn_gate(t, j):
                dve.wait_ge(S("mm_done"), t + (U0["attn"] + 1))
                dve.wait_ge(S(f"tile_landed{j}"), (t - j) * 8 + (8 * NT + 16))
                ve.tensor_tensor(gated[j][:], ps[:, 6:8, :].rearrange("p a l -> p (a l)"), gated[j][:], ALU.mult
                                 ).then_inc(S("attn_gated"), 1)

            def heads(tab, d, c, g):
                return tab[:, d, ds(c, 1), ds(g * R, R)].rearrange("p c r -> p (c r)")

            def wide(ap, n):
                return ap.unsqueeze(2).to_broadcast((P, R, n))
            dve.wait_ge(S("wend_done"), 1)
            w_low(U0["attn"], U0["attn"] % 2)

            def ssd_group(g, last=False):
                dve.wait_ge(S("y_done"), g * NT + 2)
                dve.wait_ge(S("h_fwd_done"), g * NT + 1)

                def back_x(i, p):
                    m = g * NT + i
                    c = i * -1 + (NT - 1)
                    dve.wait_ge(S("x_read"), g * (2 * NT) + (i + 3))
                    dve.wait_ge(S("back_state"), m + 1)
                    ve.tensor_tensor(xend[p][:], ps[:, 0, :].rearrange("p (r e) -> p r e", e=HEAD),
                                     wide(heads(wend, 1, c, g), HEAD), ALU.mult).then_inc(S("back_x"), 1)

                def back_h(i, p):
                    m = g * NT + i
                    c = i * -1 + (NT - 1)
                    dve.wait_ge(S("back_state"), m + 3)
                    dve.wait_ge(S("h_decayed"), m + 1)
                    dve.wait_ge(S("hb_done"), g * NT + 1)
                    ve.tensor_tensor(h_back[:, ds(c, 1), :].rearrange("p c e -> p (c e)"), ps[:, 3, :],
                                     h_tmp[:].rearrange("p r e -> p (r e)"), ALU.add).then_inc(S("h_back_done"), 1)
                skewed(dve, NT, [(back_x, 0), (back_h, 1)])
                ve.memset(h_fwd[0][:], 0.0).then_inc(S("h_cleared"), 1)
                for i in range(XT):
                    ve.tensor_scalar(ddiag[:, i, :], ident[:], dcol[:, ds(g * XT + i, 1)], None, ALU.mult
                                     ).then_inc(S("ddiag_done"), 1)
                w_low(g * 2 + (U0["attn"] + 1), (U0["attn"] + 1) % 2)

                def fwd_seg_f(c, p):
                    n = g * NT + c
                    dve.wait_ge(S("seg_landed"), n * 16 + 16)
                    dve.wait_ge(S("y_done"), n + 1)
                    ve.tensor_tensor(seg[p][:, 0, :, :], cum_all[:, 0, :, :], wide(heads(acum, 0, c, g), CHUNK), ALU.subtract
                                     ).then_inc(S("seg_f_done"), 1)

                def fwd_min(c, p):
                    n = g * NT + c
                    dve.wait_ge(S("seg_f_done"), n + 2)
                    dve.wait_ge(S("seg_b_done"), n + 2)
                    ve.tensor_tensor(seg[p][:, 0, :, :], seg[p][:, 0, :, :], seg[p][:, 1, :, :], ALU.min
                                     ).then_inc(S("arg_done"), 1)

                def fwd_gm(c, p):
                    n = g * NT + c
                    dve.wait_ge(S("fwd_turned"), n + 1)
                    ve.tensor_tensor(gm[p][:], ps[:, 2, 0:CHUNK].unsqueeze(1).to_broadcast((P, 2, CHUNK)), tri[:], ALU.mult
                                     ).then_inc(S("gm_done"), 1)

                def fwd_cdec(c, p):
                    n = g * NT + c
                    dve.wait_ge(S("seg_exp"), n + 2)
                    ve.tensor_tensor(cdec[p][:, 0, :, :], cdec[p][:, 0, :, :], cin[p][:].unsqueeze(1).to_broadcast((P, R, CHUNK)),
                                     ALU.mult).then_inc(S("c_read_dve"), 1)

                def fwd_masked(c, p):
                    n = g * NT + c
                    dve.wait_ge(S("decay_done"), n + 1)
                    dve.wait_ge(S("gm_done"), n + 2)
                    ve.tensor_tensor(seg[p][:, 1, :, :], seg[p][:, 0, :, :],
                                     gm[p][:, 1, :].unsqueeze(1).to_broadcast((P, R, CHUNK)), ALU.mult).then_inc(S("mask_step"), 1)
                    dve.wait_ge(S("mask_step"), n + 1)
                    ve.tensor_tensor(seg[p][:, 0, :, :], seg[p][:, 0, :, :],
                                     gm[p][:, 0, :].unsqueeze(1).to_broadcast((P, R, CHUNK)), ALU.mult).then_inc(S("mask_done"), 1)

                def fwd_h(c, p):
                    n = g * NT + c
                    dve.wait_ge(S("h_cleared"), g + 1)
                    dve.wait_ge(S("h_fwd_done"), n + 1)
                    ve.tensor_tensor(h_tmp[:], h_fwd[p][:], wide(heads(dec, 0, c, g), HEAD), ALU.mult).then_inc(S("h_step"), 1)
                    dve.wait_ge(S("h_step"), n + 1)
                    dve.wait_ge(S("fwd_state"), n + 3)
                    dve.wait_ge(S("y_done"), n + 2)
                    ve.tensor_tensor(h_fwd[1 - p][:].rearrange("p r e -> p (r e)"), ps[:, 3, :],
                                     h_tmp[:].rearrange("p r e -> p (r e)"), ALU.add).then_inc(S("h_fwd_done"), 1)

                def fwd_gate(c, p):
                    n = g * NT + c
                    dve.wait_ge(S("y_done"), n + 3)
                    dve.wait_ge(S(f"z_landed{p}"), n * 8 + (16 - 8 * p))
                    ve.tensor_tensor(zin[p][:], ps[:, 4 + p, :].rearrange("p (t l) -> p t l", t=XT), zin[p][:], ALU.mult
                                     ).then_inc(S("y_gated"), 1)

                attn_gate(g * 2, 0)
                skewed(dve, NT, [(fwd_masked, 1), (fwd_gate, 2), (fwd_seg_f, 0), (fwd_min, 0), (fwd_gm, 0), (fwd_h, 1),
                                 (fwd_cdec, 0)], lead=4,
                       between=None if last else lambda: w_low(g * 2 + (U0["attn"] + 2), U0["attn"] % 2))
                attn_gate(g * 2 + 1, 1)
            with dve.Fori(0, G - 1) as g:
                ssd_group(g)
            ssd_group(G - 1, last=True)
            w_low(U0["ssd"], U0["ssd"] % 2)
            w_low(U0["ssd"] + 1, (U0["ssd"] + 1) % 2)

            dve.wait_ge(S("stored0"), ST["attn end"])
            dve.wait_ge(S("stored1"), ST["attn end"])

            def y_low_step(t, q):
                dve.wait_ge(S("y_hi_done"), t + 1)
                ve.scalar_tensor_tensor(y_lo[:, ds(t, 1), :].rearrange("p t l -> p (t l)"), y_raw[q][:], ncol[:, ds(t, 1)],
                                        y_hi[:, ds(t, 1), :].rearrange("p t l -> p (t l)").bitcast(F32),
                                        ALU.mult, ALU.subtract).then_inc(S("y_lo_done"), 1)
            fours(dve, NI, y_low_step)
            dve.wait_ge(S("sq_summed"), NI)
            ve.tensor_scalar(yscale[:], ps[:, 4:6, :].rearrange("p a l -> p (a l)"), 1.0 / inner, EPS, ALU.mult, ALU.add
                             ).then_inc(S("sq_mean"), 1)
            dve.wait_ge(S("y_root"), 1)
            ve.reciprocal(yscale[:], yscale[:]).then_inc(S("yscale_done"), 1)
            dve.wait_ge(S("yscale_done"), 1)

            def merge_out(t, p):
                dve.wait_ge(S("mm_done"), t * 2 + (U0["ssd"] + 2))
                dve.wait_ge(S("merge_landed"), t * 32 + 32)
                mout = merged[:, ds(t, 1), :].rearrange("p t l -> p (t l)")
                ve.tensor_tensor(mout, out_ps("ssd", p).rearrange("p a l -> p (a l)"), yscale[:], ALU.mult
                                 ).then_inc(S("merge_step"), 1)
                dve.wait_ge(S("merge_step"), t * 2 + 1)
                ve.tensor_tensor(mout, mout, mga[:], ALU.mult).then_inc(S("merge_step"), 1)
                dve.wait_ge(S("merge_step"), t * 2 + 2)
                ve.tensor_tensor(mout, mout, mat[:], ALU.add).then_inc(S("merge_out"), 1)

            def merge_step(t, p):
                w_low(t * 2 + (U0["ssd"] + 2), U0["ssd"] % 2)
                merge_out(t, p)
                w_low(t * 2 + (U0["ssd"] + 3), (U0["ssd"] + 1) % 2)
            pairs(dve, KT, merge_step, peel=True)

            def m_low(t, p):
                dve.wait_ge(S("mix_hi_done"), t + 1)
                ve.tensor_tensor(m_lo[:, ds(t, 1), :], merged[:, ds(t, 1), :], m_hi[:, ds(t, 1), :].bitcast(F32), ALU.subtract
                                 ).then_inc(S("mix_lo_done"), 1)
            pairs(dve, KT, m_low)

            def n_a(n0):
                nf, nx, n1, n2, _ = norm_bufs(n0)

                def part(t, p):
                    dve.wait_ge(S("n_squared"), t + (n0 + NT + 1))
                    mean(stat[:, p, 1:2], stat[:, p, 0:1], "n_mean")
                    dve.wait_ge(S("n_root"), t + (n0 + NT + 1))
                    ve.reciprocal(stat[:, p, 3:4], stat[:, p, 2:3]).then_inc(S("n_rstd"), 1)
                    dve.wait_ge(S("n_rstd"), t + (n0 + NT + 1))
                    if n0 == 0:
                        wait(dve, "h2_turned", t - 1)
                    dve.wait_ge(S("norm_landed"), 64 if n0 else 48)
                    ve.scalar_tensor_tensor(n2[p], ps[:, 2:4, :], stat[:, p, 3:4], two(norm_a[:]), ALU.mult, ALU.mult
                                            ).then_inc(S("n_scaled"), 1)
                    dve.wait_ge(S("n_scaled"), t + (n0 + 1))
                    dve.wait_ge(S(f"n_x_landed{p}"), (t - p) * 8 + (8 * n0 + 16))
                    wait(dve, f"{'out' if n0 else 'x1'}_stored{p}", (t - p) * 8)
                    ve.tensor_tensor(n1[p], n2[p], nx[p], ALU.add).then_inc(S("n_added"), 1)
                return part

            def n_b(t, p):
                _, _, n1, n2, _ = norm_bufs(0)
                dve.wait_ge(S("n2_squared_b"), t + 1)
                mean(stat[:, p, 5:6], stat[:, p, 4:5], "n2_mean_b")
                dve.wait_ge(S("n2_root_b"), t + 1)
                ve.reciprocal(stat[:, p, 7:8], stat[:, p, 6:7]).then_inc(S("n2_rstd_b"), 1)
                dve.wait_ge(S("n2_rstd_b"), t + 1)
                ve.scalar_tensor_tensor(n2[p], n1[p], stat[:, p, 7:8], two(norm_b[:]), ALU.mult, ALU.mult
                                        ).then_inc(S("h2_done"), 1)

            def n_c(t, p):
                dve.wait_ge(S("h2_hi_done"), t + 1)
                cols = ds(t * CHUNK, CHUNK)
                ve.tensor_tensor(h2_lo[:, :, cols], ps[:, 4 + 2 * p:6 + 2 * p, :].rearrange("p a (b l) -> p (a b) l", l=CHUNK),
                                 h2_hi[:, :, cols].bitcast(F32), ALU.subtract).then_inc(S("h2_lo_done"), 1)

            def mix_low(t, p, half=0):
                if not (half and t == KT - 1):
                    w_low(t + (half * KT + U0["mix"] + 2), (p + U0["mix"]) % 2)
            pairs(dve, KT, mix_low)
            beside(norm_turns([(n_c, 3), (n_b, 1), (n_a(0), 0)]), NT + 3, lambda t: mix_low(t, t % 2, 1))

            dve.wait_ge(S("x1_stored0"), 16 * NT // 2)
            dve.wait_ge(S("x1_stored1"), 16 * NT // 2)

            def f_step(t):
                dve.wait_ge(S("g_done"), t + 2)
                dve.wait_ge(S("mm_done"), t * 2 + (U0["ffn_in"] + 2))
                ve.tensor_tensor(f_act[:, ds(t, 1), :].rearrange("p t l -> p (t l)"),
                                 pair_of(O0["ffn_in"] + 1).rearrange("p a l -> p (a l)"), gact[:], ALU.mult
                                 ).then_inc(S("gact_read"), 1)
            w_low(U0["ffn_in"] + 1, (U0["ffn_in"] + 1) % 2)
            with dve.Fori(0, FT - 1) as t:
                w_low(t * 2 + (U0["ffn_in"] + 2), U0["ffn_in"] % 2)
                f_step(t)
                w_low(t * 2 + (U0["ffn_in"] + 3), (U0["ffn_in"] + 1) % 2)
            w_low(U0["ffn_out"], U0["ffn_out"] % 2, FK[0])
            f_step(FT - 1)
            w_low(U0["ffn_out"] + 1, (U0["ffn_out"] + 1) % 2, FK[1])
            for half in range(2):
                def low_f(hi, k0, k1, half=half):
                    cols = slice(half * HALF, (half + 1) * HALF)
                    with dve.Fori(k0, k1) as k:
                        dve.wait_ge(S("f_hi_done"), k + (half * FT + 1))
                        ve.tensor_tensor(f_lo[:, ds(k, 1), cols], f_act[:, ds(k, 1), cols], hi[:, ds(k, 1), :].bitcast(F32),
                                         ALU.subtract).then_inc(S("f_lo_done"), 1)
                if half == 0:
                    low_f(f_hi, 0, FT)
                else:
                    low_f(f_hi, KT, FT)

                def ffn_low(t, p, half=half, last=False):
                    for j in ((2,) if last else (2, 3, 4)):
                        w_low(t * 3 + (U0["ffn_out"] + 3 * KT * half + j), (U0["ffn_out"] + p + j) % 2, FK[j % 3])
                if half == 0:
                    for t in range(2):
                        ffn_low(t, t)
                    low_f(f_hi2, 0, KT, half=1)
                    pairs(dve, KT, ffn_low, first=2)
                else:
                    beside(norm_turns([(n_a(NT), 0)]), NT, lambda t: ffn_low(t, t % 2, last=t == KT - 1))

        @block.tensor
        def _(pe):
            te = nc.tensor
            for name in ("p_turned", "pv_done"):
                pe.sem_inc(S(name), 1)
            for name in ("x_read", "back_state", "fwd_state", "y_done"):
                pe.sem_inc(S(name), 2)

            def product(dst, p, ks, moving, first=True, last=True, ready=None, kt=KT):
                for k in ks:
                    if ready:
                        ready(k)
                    begin, end = first and k == 0, last and k == kt - 1
                    ins = None
                    for h, d in enumerate(dst):
                        mh, ml = moving(h, k)
                        te.matmul(d, whi[p][:, k, :], mh, start=begin, stop=False)
                        te.matmul(d, whi[p][:, k, :], ml, start=False, stop=False)
                    for h, d in enumerate(dst):
                        ins = te.matmul(d, wlo[p][:, k, :], moving(h, k)[0], start=False, stop=end)
                return ins

            def from_act(h, k):
                cols = slice(h * HALF, (h + 1) * HALF)
                return act_hi[:, k, cols], act_lo[:, k, cols]

            def from_h2(h, k):
                cols = slice(h * HALF, (h + 1) * HALF)
                return h2_hi[:, k, cols], h2_lo[:, k, cols]

            def unit(name, t, p, ready=None, moving=from_act):
                u0, o0 = U0[name], O0[name]
                b = 2 * ((o0 + p) % 2)
                pe.wait_ge(S("w_lo_done"), t + (u0 + 1))
                product([ps[:, b, :], ps[:, b + 1, :]], (u0 + p) % 2, range(KT), moving, ready=ready).then_inc(S("mm_done"), 1)

            pe.wait_ge(S("const_step"), 8)

            def turn_x(t, p):
                pe.wait_ge(S("xn_done"), t + 1)
                wait(pe, "h_done", t - 1)
                for k in range(KT):
                    ins = te.transpose(ps[:, 2 * p + k // 4, (k % 4) * P:(k % 4 + 1) * P], x_n[p][:, k * P:(k + 1) * P], ident[:])
                ins.then_inc(S("x_turned"), 1)
            pairs(pe, NT, turn_x, peel=True)
            pe.wait_ge(S("h_done"), NT)
            unit("dt", 0, 0)

            def xbc_unit(t, p):
                wait(pe, "moved", t)
                unit("xbc", t, p)
            xbc_unit(0, 0)
            xbc_unit(1, 1)
            pe.wait_ge(S("dt_ready"), 1)
            HH = 2 * H
            for src, bank in ((dt_v, 4), (dt_e, 5)):
                for c in range(NT):
                    ins = te.transpose(ps[:, bank, c * HH:(c + 1) * HH], src[0:HH, c * CHUNK:(c + 1) * CHUNK], ident[0:HH, 0:HH])
            ins.then_inc(S("dt_turned"), 1)
            pe.wait_ge(S("dt_tok"), 2)
            for d in range(2):
                for bank, mat_ in ((6, tri[:, d, :]), (7, ones[:])):
                    ins = te.matmul(ps[:, bank, d * NT * H:(d + 1) * NT * H].rearrange("p (c h) -> p c h", h=H), mat_,
                                    atok[:, :, d, :], start=True, stop=True, skip_group_check=True)
            ins.then_inc(S("dt_summed"), 1)
            pe.wait_ge(S("tables_done"), 2)
            for c in range(NT):
                ins = te.matmul(ps[0:HH, 4 + c // 2, (c % 2) * 256:(c % 2 + 1) * 256], atok[:, c, :, :].rearrange("p d h -> p (d h)"),
                                tri[:].rearrange("p d l -> p (d l)"), start=True, stop=True, skip_group_check=True)
            ins.then_inc(S("rows_summed"), 1)
            pairs(pe, conv_dim // P, xbc_unit, first=2)

            for t in range(KV):
                pe.wait_ge(S("moved"), O0["kv"] + t - 1)
                unit("kv", t, t % 2)

            def q_unit(t, p):
                wait(pe, "moved", t + (O0["q"] - 1))
                unit("q", t, p)
            pe.wait_ge(S("moved"), O0["q"])
            for t in range(NT):
                wait(pe, "v_turned", t - 1)
                for j in range(2):
                    ins = te.transpose(ps[:, 4 + t % 2, j * P:(j + 1) * P], stage[j][:, t * CHUNK:(t + 1) * CHUNK], ident[:])
                ins.then_inc(S("v_turn"), 1)
            pairs(pe, q_dim // P, q_unit)

            def score(b, j, heads):
                half = slice((j % 2) * HEAD, (j % 2 + 1) * HEAD)
                g = j // 2
                pe.wait_ge(S("qs_done"), b * 2 + 2)
                for r in heads:
                    i = g * QR + r
                    dst = ps[:, 2 + r % 2, 0:3 * CHUNK]
                    if not (isinstance(b, int) and b == 0 and j == 0 and r < 2):
                        pe.wait_ge(S("biased"), b * QH + (j * QR + r - 1))
                    te.matmul(dst, qs_hi[half, i, :], k_hi[half, g, :], start=True, stop=False)
                    te.matmul(dst, qs_hi[half, i, :], k_lo[half, g, :], start=False, stop=False)
                    te.matmul(dst, qs_lo[half, i, :], k_hi[half, g, :], start=False, stop=True).then_inc(S("scored"), 1)

            def turn_p(b, j):
                pe.wait_ge(S("rdiag_done"), b * KV + (j + 1))
                pe.wait_ge(S("pT_done"), b * KV + (j + 1))
                for kb in range(3):
                    for r in range(QR):
                        ins = te.matmul(ps[:, 4 + kb, r * CHUNK:(r + 1) * CHUNK], prob[j % 2][:, r, kb * CHUNK:(kb + 1) * CHUNK],
                                        rdiag[:, r, :], start=True, stop=True, skip_group_check=True)
                ins.then_inc(S("p_turned"), 1)

            def weigh_v(b, j):
                pe.wait_ge(S("v_win_done"), b + 1)
                pe.wait_ge(S("pT_done"), b * KV + (j + 2))
                if j % 2 == 0:
                    pe.wait_ge(S("o_moved"), b * 2 + (j // 2 + 1))
                for kb in range(3):
                    ins = te.matmul(ps[(j % 2) * HEAD:(j % 2 + 1) * HEAD, 7, :], v_win[:, kb, j * HEAD:(j + 1) * HEAD],
                                    probT[:, kb, :], start=kb == 0, stop=kb == 2)
                ins.then_inc(S("pv_done"), 1)

            pe.wait_ge(S("pads_done"), 4)
            pe.wait_ge(S("moved"), O0["zg"])
            score(0, 0, range(QR))
            score(0, 1, range(QR))

            def zg_part(b, j, ks):
                if ks[0] == 0:
                    pe.wait_ge(S("w_lo_done"), b * KV + (U0["zg"] + j + 1))
                    pe.wait_ge(S("moved"), b * KV + (O0["zg"] + j))
                ins = product([ps[:, 0, :], ps[:, 1, :]], (U0["zg"] + j) % 2, ks, from_act)
                if ks[-1] == KT - 1:
                    ins.then_inc(S("mm_done"), 1)

            def pe_block(b, last=False):
                for j in range(KV):
                    turn_p(b, j)
                    nb, nj = (b, j + 2) if j < 2 else (b + 1, j - 2)
                    more = j < 2 or not last
                    if more:
                        score(nb, nj, range(0, 2))
                    zg_part(b, j, range(0, KT // 2))
                    if more:
                        score(nb, nj, range(2, QR))
                    zg_part(b, j, range(KT // 2, KT))
                    weigh_v(b, j)
            with pe.Fori(0, NT - 1) as b:
                pe_block(b)
            pe_block(NT - 1, True)

            def o_ready(k):
                pe.wait_ge(S("o_done"), k + 1)

            def attn_part(t, j, ks):
                if ks[0] == 0:
                    pe.wait_ge(S("w_lo_done"), t + (U0["attn"] + 1))
                    pe.wait_ge(S("attn_gated"), t + 1)
                ins = product([ps[:, 6, :], ps[:, 7, :]], (U0["attn"] + j) % 2, ks, from_act)
                if ks[-1] == KT - 1:
                    ins.then_inc(S("mm_done"), 1)

            o_ready(KT - 1)
            with pe.Fori(0, G) as g:
                def turn_back(i, p):
                    m = g * NT + i
                    pe.wait_ge(S(f"back_landed{p}"), g * (32 * NT // 2) + (i * 16 + (32 - 16 * p)))
                    pe.wait_ge(S("back_x"), m + 1)
                    pe.wait_ge(S("back_btok"), m + 1)
                    for k in range(XT):
                        te.transpose(ps[:, 0, k * P:(k + 1) * P], xin[p][:, k, :], ident[:])
                    te.transpose(ps[:, 1, 0:STATE], bin_[p][:], ident[:]).then_inc(S("x_read"), 1)

                def state_back(i, p):
                    m = g * NT + i
                    pe.wait_ge(S("back_x"), m + 2)
                    pe.wait_ge(S("back_btok"), m + 2)
                    pe.wait_ge(S("h_back_done"), m + 1)
                    te.matmul(ps[:, 3, :], btok[p][:], xend[p][:].rearrange("p r e -> p (r e)"), start=True, stop=True
                              ).then_inc(S("back_state"), 1)

                def attn_beside(j):
                    return lambda c, p: attn_part(g * 2 + j, j, range(c, c + 1))
                skewed_flat(NT, [(turn_back, 0), (attn_beside(0), 0), (state_back, 1)])

                def turn_fwd(c, p):
                    n = g * NT + c
                    pe.wait_ge(S(f"fwd_landed{p}"), g * (48 * NT // 2) + (c * 24 + (48 - 24 * p)))
                    pe.wait_ge(S("xtok_done"), n + 1)
                    pe.wait_ge(S("fwd_btok"), n + 1)
                    pe.wait_ge(S("gm_done"), n + 1)
                    pe.wait_ge(S("h_back_done"), g * NT + NT + 1)
                    for k in range(XT):
                        te.transpose(ps[:, 0, k * P:(k + 1) * P], xin[p][:, k, :], ident[:])
                    te.transpose(ps[:, 1, 0:STATE], bin_[p][:], ident[:])
                    te.matmul(ps[:, 2, 0:CHUNK], bin_[p][:], cin[p][:], start=True, stop=True).then_inc(S("fwd_turned"), 1)

                def skip_x(c, p):
                    n = g * NT + c
                    pe.wait_ge(S("y_gated"), n + 1)
                    pe.wait_ge(S("ddiag_done"), g * XT + XT)
                    for k in range(XT):
                        ins = te.matmul(ps[:, 4 + p, k * CHUNK:(k + 1) * CHUNK], ddiag[:, k, :], xin[p][:, k, :],
                                        start=k == 0, stop=False, skip_group_check=True)
                    ins.then_inc(S("x_read"), 1)

                def state(c, p):
                    n = g * NT + c
                    pe.wait_ge(S("xdt_done"), g * (3 * NT) + (c * 3 + 6) + 1)
                    pe.wait_ge(S("fwd_btok"), n + 2)
                    pe.wait_ge(S("h_fwd_done"), n + 1)
                    te.matmul(ps[:, 3, :], btok[p][:], xend[p][:].rearrange("p r e -> p (r e)"), start=True, stop=True
                              ).then_inc(S("fwd_state"), 1)

                def sums(c, p):
                    n = g * NT + c
                    pe.wait_ge(S("h_cleared"), g + 1)
                    pe.wait_ge(S("c_read_dve"), n + 3)
                    pe.wait_ge(S("c_read_pool"), n + 3)
                    pe.wait_ge(S("hb_done"), n + 2)
                    pe.wait_ge(S("mask_done"), n + 1)
                    for r in range(R):
                        dst = ps[(r % 2) * HEAD:(r % 2 + 1) * HEAD, 4 + p, (r // 2) * CHUNK:(r // 2 + 1) * CHUNK]
                        for a, (lhs, rhs) in enumerate(((h_fwd[p][:, r, :], cdec[p][:, 0, r, :]),
                                                        (hb_now[p][:, r, :], cdec[p][:, 1, r, :]),
                                                        (xdt[p][:, 1, r, :], seg[p][:, 1, r, :]),
                                                        (xdt[p][:, 0, r, :], seg[p][:, 0, r, :]))):
                            ins = te.matmul(dst, lhs, rhs, start=False, stop=a == 3, skip_group_check=True)
                    ins.then_inc(S("y_done"), 1)

                skewed_flat(NT, [(state, 1), (turn_fwd, 0), (attn_beside(1), 0), (sums, 1), (skip_x, 0)])

            def from_y(j):
                def moving(h, k):
                    cols = slice(h * HALF, (h + 1) * HALF)
                    return y_hi[:, j * KT + k, cols], y_lo[:, j * KT + k, cols]
                return moving

            def ssd_out(t, p, ready=None):
                u0 = U0["ssd"]
                b = 2 * ((O0["ssd"] + p) % 2)
                for j in range(2):
                    pe.wait_ge(S("w_lo_done"), t * 2 + (u0 + j + 1))
                    if j == 0:
                        wait(pe, "merge_out", t - 1)
                    product([ps[:, b, :], ps[:, b + 1, :]], (u0 + j) % 2, range(KT), from_y(j), first=j == 0, last=j == 1,
                            ready=(lambda k, j=j: ready(j * KT + k)) if ready else None).then_inc(S("mm_done"), 1)
            pe.wait_ge(S("y_gated"), G * NT + 2)

            def y_ready(k):
                pe.wait_ge(S("y_squared"), k + 1)
                for h in range(2):
                    ins = te.matmul(ps[:, 4 + h, :], ones[:], y_sq[k % 2][:, h * HALF:(h + 1) * HALF], start=k == 0,
                                    stop=k == NI - 1)
                ins.then_inc(S("sq_summed"), 1)
                pe.wait_ge(S("y_lo_done"), k + 1)
            ssd_out(0, 0, ready=y_ready)
            ssd_out(1, 1)
            pairs(pe, KT, ssd_out, first=2)

            def mix_out(t, p, half=0, ready=None):
                m = t + half * KT
                pe.wait_ge(S("w_lo_done"), m + (U0["mix"] + 1))
                wait(pe, "proj_out", m - 1)
                cols = slice(half * HALF, (half + 1) * HALF)
                product([ps[:, (O0["mix"] + p) % 2, :]], (U0["mix"] + p) % 2, range(KT),
                        lambda h, k: (m_hi[:, k, cols], m_lo[:, k, cols]), ready=ready).then_inc(S("mm_done"), 1)

            def turn_f(n0):
                nf = norm_bufs(n0)[0]

                def part(t, p):
                    pe.wait_ge(S(f"n_f_landed{p}"), (t - p) * 16 + (16 * n0 + 32))
                    wait(pe, "n_scaled", t + n0)
                    for k in range(KT):
                        a, b = k // (KT // 2), k % (KT // 2)
                        ins = te.transpose(ps[:, 2 + a, b * P:(b + 1) * P], nf[p][:, a, b * P:(b + 1) * P], ident[:])
                    ins.then_inc(S("n_turned"), 1)
                return part

            def turn_h2(t, p):
                pe.wait_ge(S("h2_done"), t + 1)
                wait(pe, "h2_lo_done", t)
                for k in range(KT):
                    a, b = k // (KT // 2), k % (KT // 2)
                    ins = te.transpose(ps[:, 4 + 2 * p + a, b * P:(b + 1) * P], norm_bufs(0)[3][p][:, a, b * P:(b + 1) * P],
                                       ident[:])
                ins.then_inc(S("h2_turned"), 1)
            pe.wait_ge(S("merge_out"), KT)
            mix_out(0, 0, ready=lambda k: pe.wait_ge(S("mix_lo_done"), k + 1))
            mix_out(1, 1)
            pairs(pe, KT, mix_out, first=2)
            beside(norm_turns([(turn_f(0), 0), (turn_h2, 2)]), NT + 2, lambda t: mix_out(t, t % 2, 1))

            pe.wait_ge(S("h2_lo_done"), NT + 1)
            pe.wait_ge(S("n_scaled"), NT)

            def ffn_pair(t):
                wait(pe, "g_done", t + 1)
                unit("ffn_in", t * 2, 0, moving=from_h2)
                wait(pe, "gact_read", t + 1)
                unit("ffn_in", t * 2 + 1, 1, moving=from_h2)
            with pe.Fori(0, FT) as t:
                ffn_pair(t)

            def ffn_out(t, p, half, ready=None):
                u0 = U0["ffn_out"] + half * 3 * KT
                b = (O0["ffn_out"] + p) % 2
                for j in range(3):
                    pe.wait_ge(S("w_lo_done"), t * 3 + (u0 + j + 1))
                    if j == 0:
                        wait(pe, "ffn_out_done", t + (half * KT - 1))

                    def moving(h, k, j=j):
                        hi = f_hi2 if half and j == 0 else f_hi
                        return hi[:, FK0[j] + k, :], f_lo[:, FK0[j] + k, half * HALF:(half + 1) * HALF]
                    product([ps[:, b, :]], (u0 + p + j) % 2, range(FK[j]), moving, first=j == 0, last=j == 2, kt=FK[j],
                            ready=(lambda k, j=j: ready(FK0[j] + k)) if ready else None).then_inc(S("mm_done"), 1)
            pe.wait_ge(S("gact_read"), FT + 1)

            def f_ready(half):
                return lambda k: pe.wait_ge(S("f_lo_done"), k + half * FT + 1)
            ffn_out(0, 0, 0, ready=f_ready(0))
            ffn_out(1, 1, 0)
            pairs(pe, KT, lambda t, p: ffn_out(t, p, 0), first=2)
            beside(norm_turns([(turn_f(NT), 0)]), NT, lambda t: ffn_out(t, t % 2, 1, ready=f_ready(1) if t == 0 else None))


_INS = ['x', 'pre_mix_norm', 'w_in', 'conv_w', 'conv_b', 'dt_bias_f', 'dt_bias_b', 'A_log_f', 'A_log_b', 'D_skip',
        'ssd_norm', 'w_ssd_proj', 'attn_sink', 'w_attn_proj', 'w_out', 'post_mix_norm', 'pre_ffn_norm', 'w_ffn_in',
        'w_ffn_out', 'post_ffn_norm']


def kernel(**inputs):
    import numpy as _np
    import concourse.bacc as _bacc
    from concourse import mybir as _mybir
    from concourse.bass_utils import run_bass_kernel_spmd as _run

    nc = _bacc.Bacc("TRN2", target_bir_lowering=False, num_devices=1)
    arrays, args = {}, []
    for name in _INS:
        a = _np.ascontiguousarray(inputs[name])
        arrays[f"in_{name}_dram"] = a
        args.append(nc.dram_tensor(f"in_{name}_dram", a.shape, _mybir.dt.from_np(a.dtype), kind="ExternalInput").ap())
    args.append(nc.dram_tensor("out_dram", inputs['x'].shape, _mybir.dt.float32, kind="ExternalOutput").ap())
    hybrid_encoder_layer(nc, *args)
    r = _run(nc, [arrays], core_ids=[0])
    return r.results[0]["out_dram"]
```
